# Optimizing a Trainium2 kernel written in Bass

```python
import math
import jax, jax.numpy as jnp
from jax import lax
import numpy as np

D_MODEL = 1024
BATCH = 1
SEQ = 1024
DEPTH = 1
DEC_BATCH = 8
DEC_SEQ = 1
PAST_LEN = 8192
PAGE_SIZE = 128

D_SC = D_MODEL
SC_CONV = 3
D_INNER = 2 * D_MODEL
SSM_HEADDIM = 64
SSM_HEADS = D_INNER // SSM_HEADDIM
SSM_GROUPS = 8
SSM_HPG = SSM_HEADS // SSM_GROUPS
SSM_STATE = 128
SSM_CONV = 4
SSM_CONV_DIM = D_INNER + 2 * SSM_GROUPS * SSM_STATE
SSM_CHUNK = 128
N_EXP_GROUPS = 4
EXP_PER_GROUP = 8
N_EXPERTS = N_EXP_GROUPS * EXP_PER_GROUP
TOP_K_INNER = 2
D_EXPERT = 512
MOE_BLOCK = 128
ALPHA = (2.0 * DEPTH) ** 0.25
BETA = (8.0 * DEPTH) ** -0.25
LN_EPS = 1e-5
RMS_EPS = 1e-5
IN_SIZES = (D_SC, D_SC, D_SC, D_INNER, SSM_CONV_DIM, SSM_HEADS, D_MODEL, D_MODEL)
IN_COLS = sum(IN_SIZES)

kernel_name = 'hybrid_shortconv_ssd_hmoe_step'

def _split_points(sizes):
    return [int(v) for v in np.cumsum(sizes)[:-1]]

def _layernorm(x, g, b):
    xf = x.astype(jnp.float32)
    mu = jnp.mean(xf, -1, keepdims=True)
    var = jnp.mean(jnp.square(xf - mu), -1, keepdims=True)
    return ((xf - mu) * lax.rsqrt(var + LN_EPS) * g + b).astype(x.dtype)

def _causal_dwconv(x, buf, w):
    K = w.shape[0]
    L = x.shape[1]
    xp = jnp.concatenate([buf.astype(x.dtype), x], axis=1)
    y = xp[:, 0:L] * w[0]
    for k in range(1, K):
        y = y + xp[:, k:k + L] * w[k]
    return y, xp[:, L:]

def _ssd(xh, dt, A, Bm, Cm, h0):
    f32 = jnp.float32
    b, L = xh.shape[0], xh.shape[1]
    Q = min(SSM_CHUNK, L)
    nc = -(-L // Q)
    pad = nc * Q - L

    def prep(a):
        a = a.astype(f32)
        a = jnp.pad(a, [(0, 0), (0, pad)] + [(0, 0)] * (a.ndim - 2))
        return jnp.moveaxis(a.reshape((b, nc, Q) + a.shape[2:]), 1, 0)

    xs, dts, Bs, Cs = prep(xh), prep(dt), prep(Bm), prep(Cm)
    causal = jnp.tril(jnp.ones((Q, Q), dtype=bool))

    def step(h, inp):
        x_c, dt_c, B_c, C_c = inp
        cum = jnp.cumsum(dt_c * A, axis=1)
        seg = cum[:, :, None] - cum[:, None, :]
        Lm = jnp.exp(jnp.where(causal[None, :, :, None, None], seg, -jnp.inf))
        CB = jnp.einsum('btgn,bsgn->btsg', C_c, B_c)
        M = CB[..., None] * Lm * dt_c[:, None]
        y = jnp.einsum('btsgr,bsgrp->btgrp', M, x_c)
        y = y + jnp.einsum('btgn,bgrpn->btgrp', C_c, h) * jnp.exp(cum)[..., None]
        w_end = dt_c * jnp.exp(cum[:, -1:] - cum)
        h = h * jnp.exp(cum[:, -1])[..., None, None] + jnp.einsum('bsgn,bsgr,bsgrp->bgrpn', B_c, w_end, x_c)
        return h, y

    h, ys = lax.scan(step, h0.astype(f32), (xs, dts, Bs, Cs))
    y = jnp.moveaxis(ys, 0, 1).reshape((b, nc * Q) + ys.shape[3:])[:, :L]
    return y, h

def _moe_dispatch(h, e_idx, w, w13, w2):
    T, D = h.shape
    K = e_idx.shape[1]
    A = T * K
    flat_e = e_idx.reshape(-1)
    flat_tok = jnp.repeat(jnp.arange(T, dtype=jnp.int32), K)
    flat_w = w.reshape(-1)
    order = jnp.argsort(flat_e)
    se, stok, sw = flat_e[order], flat_tok[order], flat_w[order]
    counts = jnp.bincount(flat_e, length=N_EXPERTS)
    padded = (counts + MOE_BLOCK - 1) // MOE_BLOCK * MOE_BLOCK
    pad_end = jnp.cumsum(padded)
    pad_start = pad_end - padded
    start = jnp.cumsum(counts) - counts
    dest = pad_start[se] + jnp.arange(A, dtype=jnp.int32) - start[se]
    n_blocks = -(-(A + N_EXPERTS * (MOE_BLOCK - 1)) // MOE_BLOCK)
    buf_tok = jnp.full((n_blocks * MOE_BLOCK,), T, dtype=jnp.int32).at[dest].set(stok)
    h_pad = jnp.concatenate([h, jnp.zeros((1, D), h.dtype)], axis=0)
    xb = h_pad[buf_tok].reshape(n_blocks, MOE_BLOCK, D)
    block_e = jnp.minimum(jnp.searchsorted(pad_end, jnp.arange(n_blocks) * MOE_BLOCK, side='right'), N_EXPERTS - 1)

    def expert_block(args):
        xblk, e = args
        gate, up = jnp.split(xblk @ w13[e], 2, axis=-1)
        return (jax.nn.silu(gate) * up) @ w2[e]

    yb = lax.map(expert_block, (xb, block_e)).reshape(-1, D)
    contrib = yb[dest] * sw[:, None].astype(h.dtype)
    return jax.ops.segment_sum(contrib, stok, num_segments=T)

def _hier_moe(h, w_rg, b_rg, w_re, b_re, w13, w2):
    T = h.shape[0]
    pg = jax.nn.softmax((h @ w_rg + b_rg).astype(jnp.float32), axis=-1)
    pg_top, g_idx = lax.top_k(pg, 1)
    le = (h @ w_re + b_re).astype(jnp.float32).reshape(T, N_EXP_GROUPS, EXP_PER_GROUP)
    le_sel = jnp.take_along_axis(le, g_idx[:, :, None], axis=1)[:, 0]
    pe = jax.nn.softmax(le_sel, axis=-1)
    pe_top, e_local = lax.top_k(pe, TOP_K_INNER)
    wts = pg_top * pe_top / jnp.sum(pe_top, -1, keepdims=True)
    e_idx = g_idx * EXP_PER_GROUP + e_local
    return _moe_dispatch(h, e_idx, wts, w13, w2)

def _layer(x, c, h0, buf_ssm, buf_sc, w_ada, b_ada, w_in, conv_sc_w, w_sc_out, conv_ssm_w, conv_ssm_b,
           dt_bias, a_log, d_skip, ssm_norm_g, w_ssm_out, w_o, ln_mix_g, ln_mix_b, w_route_g, b_route_g,
           w_route_e, b_route_e, w_moe_13, w_moe_2, ln_ffn_g, ln_ffn_b):
    b, L, D = x.shape
    G, R, P, N = SSM_GROUPS, SSM_HPG, SSM_HEADDIM, SSM_STATE
    mod = jax.nn.silu(c) @ w_ada + b_ada
    sh1, sc1, g1, sh2, sc2, g2 = jnp.split(mod[:, None, :], 6, axis=-1)
    u = x * (1 + sc1) + sh1
    proj = u @ w_in
    s_b, s_c, s_h, z, xbc, dt_raw, gate_a, gate_b = jnp.split(proj, _split_points(IN_SIZES), axis=-1)
    conv_a, new_sc = _causal_dwconv(s_c * s_h, buf_sc, conv_sc_w)
    y_a = (s_b * conv_a) @ w_sc_out
    xbc_c, new_ssm_conv = _causal_dwconv(xbc, buf_ssm, conv_ssm_w)
    xbc_c = jax.nn.silu(xbc_c + conv_ssm_b)
    xs, Bm, Cm = jnp.split(xbc_c, [D_INNER, D_INNER + G * N], axis=-1)
    xh = xs.reshape(b, L, G, R, P)
    dt = jax.nn.softplus((dt_raw + dt_bias).astype(jnp.float32)).reshape(b, L, G, R)
    A = -jnp.exp(a_log.astype(jnp.float32)).reshape(G, R)
    y, h_new = _ssd(xh, dt, A, Bm.reshape(b, L, G, N), Cm.reshape(b, L, G, N), h0.reshape(b, G, R, P, N))
    y = y + d_skip.reshape(G, R, 1).astype(jnp.float32) * xh.astype(jnp.float32)
    yg = (y * jax.nn.silu(z.astype(jnp.float32)).reshape(b, L, G, R, P)).reshape(b, L, G, R * P)
    yg = yg * lax.rsqrt(jnp.mean(jnp.square(yg), -1, keepdims=True) + RMS_EPS)
    y_b = (yg.reshape(b, L, D_INNER) * ssm_norm_g).astype(x.dtype) @ w_ssm_out
    merged = jax.nn.sigmoid(gate_a) * y_a + jax.nn.sigmoid(gate_b) * y_b
    x = _layernorm(ALPHA * x + (1 + g1) * (merged @ w_o), ln_mix_g, ln_mix_b)
    u2 = x * (1 + sc2) + sh2
    f = _hier_moe(u2.reshape(b * L, D), w_route_g, b_route_g, w_route_e, b_route_e, w_moe_13, w_moe_2).reshape(b, L, D)
    x = _layernorm(ALPHA * x + (1 + g2) * f, ln_ffn_g, ln_ffn_b)
    return x, h_new.reshape(b, SSM_HEADS, P, N).astype(x.dtype), new_ssm_conv, new_sc

def setup_inputs(seed: int = 0) -> dict:
    key = jax.random.key(seed)
    ks = jax.random.split(key, 40)
    f32 = jnp.float32

    def nrm(k, shape, scale):
        return jax.random.normal(k, shape, f32) * scale

    dt0 = jnp.exp(jax.random.uniform(ks[20], (DEPTH, SSM_HEADS), f32, math.log(1e-3), math.log(1e-1)))
    return {
        'x_prompt': nrm(ks[0], (BATCH, SEQ, D_MODEL), 1.0),
        'x_sample': nrm(ks[1], (DEC_BATCH, DEC_SEQ, D_MODEL), 1.0),
        'state_ssm': nrm(ks[2], (DEPTH, DEC_BATCH, SSM_HEADS, SSM_HEADDIM, SSM_STATE), 0.5),
        'state_ssm_conv': nrm(ks[3], (DEPTH, DEC_BATCH, SSM_CONV - 1, SSM_CONV_DIM), 1.0),
        'state_sc_conv': nrm(ks[4], (DEPTH, DEC_BATCH, SC_CONV - 1, D_SC), 1.0),
        'c_prompt': nrm(ks[5], (BATCH, D_MODEL), 1.0),
        'c_sample': nrm(ks[6], (DEC_BATCH, D_MODEL), 1.0),
        'ln_in_g': 1.0 + nrm(ks[7], (D_MODEL,), 0.02),
        'ln_in_b': nrm(ks[8], (D_MODEL,), 0.02),
        'w_ada': nrm(ks[9], (DEPTH, D_MODEL, 6 * D_MODEL), 0.1 * D_MODEL ** -0.5),
        'b_ada': nrm(ks[10], (DEPTH, 6 * D_MODEL), 0.01),
        'w_in': nrm(ks[11], (DEPTH, D_MODEL, IN_COLS), D_MODEL ** -0.5),
        'conv_sc_w': nrm(ks[12], (DEPTH, SC_CONV, D_SC), SC_CONV ** -0.5),
        'w_sc_out': nrm(ks[13], (DEPTH, D_SC, D_MODEL), BETA * D_SC ** -0.5),
        'conv_ssm_w': nrm(ks[14], (DEPTH, SSM_CONV, SSM_CONV_DIM), SSM_CONV ** -0.5),
        'conv_ssm_b': nrm(ks[15], (DEPTH, SSM_CONV_DIM), 0.01),
        'dt_bias': dt0 + jnp.log(-jnp.expm1(-dt0)),
        'a_log': jnp.log(jax.random.uniform(ks[16], (DEPTH, SSM_HEADS), f32, 1.0, 16.0)),
        'd_skip': 1.0 + nrm(ks[17], (DEPTH, SSM_HEADS), 0.1),
        'ssm_norm_g': 1.0 + nrm(ks[18], (DEPTH, D_INNER), 0.02),
        'w_ssm_out': nrm(ks[19], (DEPTH, D_INNER, D_MODEL), BETA * D_INNER ** -0.5),
        'w_o': nrm(ks[21], (DEPTH, D_MODEL, D_MODEL), BETA * D_MODEL ** -0.5),
        'ln_mix_g': 1.0 + nrm(ks[22], (DEPTH, D_MODEL), 0.02),
        'ln_mix_b': nrm(ks[23], (DEPTH, D_MODEL), 0.02),
        'w_route_g': nrm(ks[24], (DEPTH, D_MODEL, N_EXP_GROUPS), D_MODEL ** -0.5),
        'b_route_g': nrm(ks[25], (DEPTH, N_EXP_GROUPS), 0.01),
        'w_route_e': nrm(ks[26], (DEPTH, D_MODEL, N_EXPERTS), D_MODEL ** -0.5),
        'b_route_e': nrm(ks[27], (DEPTH, N_EXPERTS), 0.01),
        'w_moe_13': nrm(ks[28], (DEPTH, N_EXPERTS, D_MODEL, 2 * D_EXPERT), D_MODEL ** -0.5),
        'w_moe_2': nrm(ks[29], (DEPTH, N_EXPERTS, D_EXPERT, D_MODEL), BETA * D_EXPERT ** -0.5),
        'ln_ffn_g': 1.0 + nrm(ks[30], (DEPTH, D_MODEL), 0.02),
        'ln_ffn_b': nrm(ks[31], (DEPTH, D_MODEL), 0.02),
    }

def reference(x_prompt, x_sample, state_ssm, state_ssm_conv, state_sc_conv, c_prompt, c_sample,
              ln_in_g, ln_in_b, w_ada, b_ada, w_in, conv_sc_w, w_sc_out, conv_ssm_w, conv_ssm_b,
              dt_bias, a_log, d_skip, ssm_norm_g, w_ssm_out, w_o, ln_mix_g, ln_mix_b,
              w_route_g, b_route_g, w_route_e, b_route_e, w_moe_13, w_moe_2, ln_ffn_g, ln_ffn_b):
    def run(x, c, h_all, bssm_all, bsc_all):
        x = _layernorm(x, ln_in_g, ln_in_b)
        hs, b1s, b2s = [], [], []
        for l in range(DEPTH):
            x, h, b1, b2 = _layer(x, c, h_all[l], bssm_all[l], bsc_all[l], w_ada[l], b_ada[l], w_in[l],
                                  conv_sc_w[l], w_sc_out[l], conv_ssm_w[l], conv_ssm_b[l], dt_bias[l],
                                  a_log[l], d_skip[l], ssm_norm_g[l], w_ssm_out[l], w_o[l], ln_mix_g[l],
                                  ln_mix_b[l], w_route_g[l], b_route_g[l], w_route_e[l], b_route_e[l],
                                  w_moe_13[l], w_moe_2[l], ln_ffn_g[l], ln_ffn_b[l])
            hs.append(h)
            b1s.append(b1)
            b2s.append(b2)
        return x, jnp.stack(hs), jnp.stack(b1s), jnp.stack(b2s)

    bp = x_prompt.shape[0]
    dtp = x_prompt.dtype
    h0_p = jnp.zeros((DEPTH, bp, SSM_HEADS, SSM_HEADDIM, SSM_STATE), dtp)
    bssm_p = jnp.zeros((DEPTH, bp, SSM_CONV - 1, SSM_CONV_DIM), dtp)
    bsc_p = jnp.zeros((DEPTH, bp, SC_CONV - 1, D_SC), dtp)
    y_prompt, p_ssm, p_ssm_conv, p_sc_conv = run(x_prompt, c_prompt, h0_p, bssm_p, bsc_p)
    y_sample, s_ssm, s_ssm_conv, s_sc_conv = run(x_sample, c_sample, state_ssm, state_ssm_conv, state_sc_conv)
    return (y_prompt, y_sample, p_ssm, p_ssm_conv, p_sc_conv, s_ssm, s_ssm_conv, s_sc_conv)


_drawn_inputs = setup_inputs


def setup_inputs(seed=0):
    import zlib

    import numpy as np

    out = dict(_drawn_inputs(seed))
    spreads = {}
    factors = {'conv_ssm_b': 3.713,
     'd_skip': 5.809,
     'ssm_norm_g': 8.0,
     'b_route_g': 8.0,
     'b_route_e': 6.93,
     'ln_ffn_g': 2.719,
     'ln_ffn_b': 2.897}
    for name, (base, spread) in spreads.items():
        noise = np.random.default_rng([zlib.crc32(name.encode()), seed]).standard_normal(out[name].shape)
        drawn = base * np.exp(spread * noise) if base else spread * noise
        out[name] = __import__('jax').numpy.asarray(drawn.astype(out[name].dtype))
    for name, factor in factors.items():
        out[name] = (out[name] * factor).astype(out[name].dtype)
    return out
```

```python
from contextlib import ExitStack

import concourse.bass as bass
from concourse import mybir

F32 = mybir.dt.float32
I32 = mybir.dt.int32
ALU = mybir.AluOpType
ACT = mybir.ActivationFunctionType
AX = mybir.AxisListType
ds = bass.ds

P = 128
D = 1024
KD = D // P
SEQ = 1024
NS = 8
TOK = SEQ + NS
TILES = SEQ // P
SUB = TOK // 3
D_INNER = 2 * D
GROUPS = 8
HEADS = 32
HPG = HEADS // GROUPS
HD = 64
N = 128
CHUNKS = SEQ // P
CONV_DIM = D_INNER + 2 * GROUPS * N
NEG = -1.0e30
EPS = 1e-5
ALPHA = 2.0 ** 0.25
COL_SB, COL_SC, COL_SH = 0, D, 2 * D
COL_Z = 3 * D
COL_X = COL_Z + D_INNER
COL_B = COL_X + D_INNER
COL_C = COL_B + GROUPS * N
COL_DT = COL_C + GROUPS * N
COL_GA = COL_DT + HEADS
COL_GB = COL_GA + D
EXPERTS, EGROUPS, PER_GROUP, D_EXP = 32, 4, 8, 512
BLOCKS = 48
ROWS_S = 29
ROWS_C = 21
MODW = 6 * D
MROWS = NS + 1


class Steps:

    def __init__(self, eng, sem):
        self.eng, self.sem, self.n, self.turn, self.per = eng, sem, 0, None, 0

    def did(self, ins):
        ins.then_inc(self.sem, 1)
        self.n += 1

    def settle(self):
        if self.turn is None:
            self.eng.wait_ge(self.sem, self.n)
        else:
            self.eng.wait_ge(self.sem, self.turn * self.per + self.n)

    def enter(self, turn, per):
        self.turn, self.per, self.start = turn, per, self.n

    def leave(self, turns):
        assert self.n - self.start == self.per, f"steps per turn: {self.n - self.start}"
        self.n = self.start + turns * self.per
        self.turn = None


def widen(ap, axis, count):
    v = ap.unsqueeze(axis)
    shape = list(v.shape)
    shape[axis] = count
    return v.to_broadcast(shape)


def build(nc, t, o):
    (y_prompt, y_sample, p_ssm, p_ssm_conv, p_sc_conv, s_ssm, s_ssm_conv, s_sc_conv) = o
    ctx = ExitStack()
    with ctx:
        def sem(name):
            return ctx.enter_context(nc.semaphore(name))

        ARENA = 53200
        arena = ctx.enter_context(nc.sbuf_tensor("arena", [P, ARENA], F32))
        banks = [ctx.enter_context(nc.psum_tensor(f"bank{i}", [P, 512], F32)) for i in range(6)]
        pair = ctx.enter_context(nc.psum_tensor("bank67", [P, 1024], F32))
        bank6, bank7 = pair[:, 0:512], pair[:, 512:1024]
        x0_dram = nc.dram_tensor("x0_dram", (TOK, D), F32, kind="Internal").ap()
        mod_dram = nc.dram_tensor("mod_dram", (MROWS, MODW), F32, kind="Internal").ap()
        u2_dram = nc.dram_tensor("u2_dram", (TOK, D), F32, kind="Internal").ap()
        rows_dram = nc.dram_tensor("rows_dram", (BLOCKS * P, D), F32, kind="Internal").ap()

        class Room:

            def __init__(self, start, end):
                self.at, self.end = start, end

            def take(self, n):
                assert self.at + n <= self.end, f"over by {self.at + n - self.end}"
                self.at += n
                return arena[:, self.at - n:self.at]

        UT0 = 0
        Y0 = UT0 + KD * TOK
        W0 = Y0 + 2 * KD * TOK
        S0 = W0 + 6 * KD * P
        K0 = ARENA - 3312
        uT = arena[:, UT0:Y0].rearrange("p (k t) -> p k t", k=KD)
        ybT_f = arena[:, Y0:W0]
        ybT = ybT_f.rearrange("p (k t) -> p k t", k=2 * KD)
        wslot = [arena[:, W0 + u * D:W0 + (u + 1) * D].rearrange("p (k c) -> p k c", k=KD) for u in range(6)]

        keep = Room(K0, ARENA)
        ident = keep.take(P)
        tri = keep.take(P)
        stri = keep.take(P)
        ones = keep.take(P)
        ones_avg = keep.take(P)
        epsc = keep.take(1)
        convw_f = keep.take(32 * 5)
        convst_f = keep.take(32 * 24)
        colc_f = keep.take(KD * ROWS_C)
        colc = colc_f.rearrange("p (k r) -> p k r", k=KD)
        normg = keep.take(16)
        dskip = keep.take(16)
        dt_g = keep.take(GROUPS * CHUNKS * HPG)
        cum_t = keep.take(GROUPS * CHUNKS * HPG)
        wend = keep.take(GROUPS * CHUNKS * HPG)
        decay = keep.take(GROUPS * CHUNKS * HPG)
        dta_g = keep.take(GROUPS * CHUNKS * HPG)
        dt_s = keep.take(16 * NS)
        dec_s = keep.take(16 * NS)
        stats2 = cum_t[:, 0:12]
        mv2 = cum_t[:, 16:24].rearrange("p (x a) -> p x a", x=2)

        r0 = Room(Y0, W0)
        wada = [r0.take(KD * 512).rearrange("p (k c) -> p k c", k=KD) for _ in range(3)]
        xr = [r0.take(D) for _ in range(4)]
        bada = arena[0:MROWS, W0:W0 + MODW]
        r0 = Room(S0, K0)
        mod = r0.take(MODW)[0:MROWS]
        rows_s = r0.take(CONV_DIM)[0:ROWS_S]
        rows_c = r0.take(D)[0:ROWS_C]
        crow = r0.take(D)[0:MROWS]
        ln_g = r0.take(D)
        ln_b = r0.take(D)
        mod_t = r0.take(16 * MROWS).rearrange("p (k m) -> p k m", k=16)
        c_t = r0.take(KD * MROWS).rearrange("p (k m) -> p k m", k=KD)
        w_dt = r0.take(KD * HEADS).rearrange("p (k h) -> p k h", k=KD)
        dtb = r0.take(HEADS)
        alog = r0.take(HEADS)
        dskb = r0.take(HEADS)
        stats = r0.take(4 * 12).rearrange("p (x a) -> p x a", x=4)
        mv = r0.take(4 * 4).rearrange("p (x a) -> p x a", x=4)
        DTW = (TILES + 1) * HEADS
        dtr = ln_g[:, 0:DTW]
        dte = ln_g[:, DTW:2 * DTW]
        dtw = ln_g[:, 2 * DTW:3 * DTW]
        dtl = ln_b[:, 0:DTW]
        dtq = ln_b[:, DTW:2 * DTW]
        dtm = ln_b[:, 2 * DTW:3 * DTW]
        cend = arena[:, S0:S0 + 256]
        spread = arena[0:NS, S0 + 256:S0 + 256 + 512]
        das = arena[0:NS, S0 + 768:S0 + 800]

        r1 = Room(S0, K0)
        raw_f = r1.take(6 * TOK)
        raw = [raw_f[:, u * TOK:(u + 1) * TOK] for u in range(6)]
        z2 = raw_f[:, 4 * TOK:6 * TOK].rearrange("p (j t) -> p j t", j=2)
        proc_f = r1.take(4 * TOK)
        proc = [proc_f[:, u * TOK:(u + 1) * TOK] for u in range(4)]
        xs2 = proc_f[:, 0:2 * TOK].rearrange("p (j t) -> p j t", j=2)
        hs = r1.take(NS * 2 * N).rearrange("p (b j n) -> p b j n", b=NS, j=2)
        tmp = r1.take(NS * N).rearrange("p (b n) -> p b n", b=NS)
        diag_f = r1.take(NS * N)
        diag = diag_f.rearrange("p (b n) -> p b n", b=NS)
        pstate = diag_f[:, 0:2 * N]
        cumb = r1.take(4 * P)
        csc = r1.take(4 * P)
        segm = r1.take(4 * P)
        rhs_cum = r1.take(4 * P)
        xdt = r1.take(HPG * HD)
        xw = r1.take(HPG * HD)
        b_tok = r1.take(N)
        cb_m = r1.take(P)
        h_t = r1.take(HPG * HD)
        ybuf = [r1.take(2 * P).rearrange("p (j t) -> p j t", j=2) for _ in range(2)]
        sq = r1.take(2 * P).rearrange("p (j t) -> p j t", j=2)
        rs = r1.take(P)
        ys = r1.take(2 * NS).rearrange("p (j b) -> p j b", j=2)
        dtx = r1.take(2 * NS).rearrange("p (j b) -> p j b", j=2)
        tail = r1.take(4 * P)[0:11]

        merged_f = arena[:, S0:S0 + KD * TOK]
        merged = merged_f.rearrange("p (k t) -> p k t", k=KD)
        r2 = Room(S0 + KD * TOK, K0)
        gsb = [r2.take(TOK) for _ in range(2)]
        MIX0 = r2.at
        scb = [r2.take(TOK) for _ in range(2)]
        pt = [r2.take(TOK) for _ in range(2)]
        sbb = [r2.take(TOK) for _ in range(2)]
        acc = r2.take(TOK)
        tail_sc = r2.take(D)[0:10]
        ya_f = ybT_f[:, 0:KD * TOK]
        yaT = ya_f.rearrange("p (k t) -> p k t", k=KD)

        X1W = (TILES + 1) * D
        x1 = arena[:, 0:X1W].rearrange("p (i d) -> p i d", i=TILES + 1)
        w_o = ybT_f[:, KD * TOK:KD * TOK + KD * D].rearrange("p (k c) -> p k c", k=KD)
        r3 = Room(MIX0, K0)
        g1_p, mix_g, mix_b, sc2_p, sh2_p = (r3.take(D) for _ in range(5))
        g1_s, sc2_s, sh2_s = (r3.take(D)[0:NS] for _ in range(3))
        w_r = r3.take(KD * 36).rearrange("p (k e) -> p k e", k=KD)
        b_r = r3.take(36)
        wflat = [arena[:, W0 + u * D:W0 + (u + 1) * D] for u in range(6)]
        x0b = [wflat[2], wflat[5]]
        u2 = [wflat[0], wflat[1]]
        u2t = [wflat[3], wflat[4]]

        r4 = Room(X1W, W0)
        NI = TILES + 1
        logit = r4.take(NI * 36).rearrange("p (i e) -> p i e", i=NI)
        iota_r = r4.take(P)
        tok_id = r4.take(NI)
        valid = r4.take(NI)
        grp = r4.take(NI * 4).rearrange("p (i e) -> p i e", i=NI)
        grp_d = r4.take(NI * 4).rearrange("p (i e) -> p i e", i=NI)
        grp_t = r4.take(NI * 4).rearrange("p (i e) -> p i e", i=NI)
        lm, ld, lt, e1, e2, mm, ss, rr = (r4.take(NI * EXPERTS).rearrange("p (i e) -> p i e", i=NI) for _ in range(8))
        s_all = r4.take(EXPERTS)
        gmx, gix, gsum, m1, m2, ix, esum, wa, wb = (r4.take(NI) for _ in range(9))
        cnt, nb, bend, bst, one32 = (r4.take(EXPERTS) for _ in range(5))
        nb_i = r4.take(EXPERTS).bitcast(I32)
        dest_f, lo_f, hi_f = (r4.take(2 * NI) for _ in range(3))
        lo_i, hi_i = (r4.take(2 * NI).bitcast(I32) for _ in range(2))
        NBX = BLOCKS + 2
        oh_lo = r4.take(2 * NI * P).rearrange("p (a c) -> p a c", c=P)
        oh_hi = r4.take(2 * NI * NBX).rearrange("p (a b) -> p a b", b=NBX)
        cmp = r4.take(NBX * EXPERTS)[0:1].rearrange("p (b e) -> p b e", e=EXPERTS)
        ef = r4.take(NBX)[0:1]

        r5 = Room(X1W, K0)
        w13 = [r5.take(KD * 2 * D_EXP).rearrange("p (k c) -> p k c", k=KD) for _ in range(2)]
        w2 = [r5.take(4 * D).rearrange("p (k c) -> p k c", k=4) for _ in range(2)]
        xg = [r5.take(D) for _ in range(2)]
        xt = [r5.take(D) for _ in range(2)]
        hm = [r5.take(D_EXP) for _ in range(2)]
        ht = [r5.take(D_EXP) for _ in range(2)]
        yo = [r5.take(D) for _ in range(2)]
        g2_p, ffn_g, ffn_b = (r5.take(D) for _ in range(3))
        g2_s = r5.take(D)[0:NS]
        dest_i = r5.take(2 * NI).bitcast(I32)
        wts = r5.take(2 * NI)
        tok_of = r5.take(NBX).bitcast(I32)
        plan = r5.take(NBX + 1)[0:1].bitcast(I32)
        idx2 = r5.take(2).bitcast(I32)
        spare = r5.take(1)

        r6 = Room(X1W, X1W + 2 * KD * 2 * D_EXP)
        fa = [r6.take(D) for _ in range(3)]
        fb = [r6.take(D) for _ in range(3)]

        c_landed, small_landed = sem("c_landed"), sem("small_landed")
        wada_landed = [sem(f"wada_landed{i}") for i in range(3)]
        x_landed = [sem(f"x_landed{i}") for i in range(4)]
        consts_ready = sem("consts_ready")
        pool_step, dve_step, act_step = sem("pool_step"), sem("dve_step"), sem("act_step")
        ct_turned, ct_ready = sem("ct_turned"), sem("ct_ready")
        mod_done, mod_added, mod_stored = sem("mod_done"), sem("mod_added"), sem("mod_stored")
        cols_turned, cols_copied = sem("cols_turned"), sem("cols_copied")
        var_ready, std_ready = sem("var_ready"), sem("std_ready")
        x0_ready = sem("x0_ready")
        x0_stored = [sem(f"x0_stored{i}") for i in range(4)]
        x_turned, ut_ready, ut_s_ready = sem("x_turned"), sem("ut_ready"), sem("ut_s_ready")
        dt_raw, dt_in, dt_exp, dt_sum, dt_ln, dta_ready = (sem("dt_raw"), sem("dt_in"), sem("dt_exp"), sem("dt_sum"),
                                                         sem("dt_ln"), sem("dta_ready"))
        filled, cum_done, wend_ready = sem("filled"), sem("cum_done"), sem("wend_ready")
        spread_ready, spread_done, dt_ready = sem("spread_ready"), sem("spread_done"), sem("dt_ready")
        w_landed = [sem(f"w_landed{u}") for u in range(6)]
        proj_done, raw_ready, tails_done, tail_copied, tail_stored = (
            sem("proj_done"), sem("raw_ready"), sem("tails_done"), sem("tail_copied"), sem("tail_stored"))
        conv_done, silu_done, zsilu_done = sem("conv_done"), sem("silu_done"), sem("zsilu_done")
        rh_ready, cum_ready, scores_ready = sem("rh_ready"), sem("cum_ready"), sem("scores_ready")
        cum_copied, ecum_ready, seg_ready, e_ready = (sem("cum_copied"), sem("ecum_ready"), sem("seg_ready"),
                                                      sem("e_ready"))
        ops_ready, y_ready, y_gated, sq_ready = sem("ops_ready"), sem("y_ready"), sem("y_gated"), sem("sq_ready")
        rms_ready, rs_ready, normed = sem("rms_ready"), sem("rs_ready"), sem("normed")
        diag_b_ready, diag_c_ready, sb_ready, sc_ready = (sem("diag_b_ready"), sem("diag_c_ready"), sem("sb_ready"),
                                                          sem("sc_ready"))
        sb_used, sc_used, hs_ready, hs_stored, h0_landed = (sem("sb_used"), sem("sc_used"), sem("hs_ready"),
                                                            sem("hs_stored"), sem("h0_landed"))
        ht_ready, pstate_copied, pstate_stored = sem("ht_ready"), sem("pstate_copied"), sem("pstate_stored")
        old_rows, act_ln, fin_step = sem("old_rows"), sem("act_ln"), sem("fin_step")

        gb_done, gsig_ready, yb_done, merged_b = sem("gb_done"), sem("gsig_ready"), sem("yb_done"), sem("merged_b")
        ga_done, gsig2_ready, ya_done, merged_a = sem("ga_done"), sem("gsig2_ready"), sem("ya_done"), sem("merged_a")
        short_done, sc_copied, p_made, sb_copied = sem("short_done"), sem("sc_copied"), sem("p_made"), sem("sb_copied")
        ya_ready, tail2_done, tail2_copied, tail2_stored = (sem("ya_ready"), sem("tail2_done"), sem("tail2_copied"),
                                                            sem("tail2_stored"))
        mixw_landed, wo_landed = sem("mixw_landed"), sem("wo_landed")
        x0_landed = [sem(f"x0_landed{i}") for i in range(2)]
        wo_done, mvar_ready, mstd_ready, x0_used = sem("wo_done"), sem("mvar_ready"), sem("mstd_ready"), sem("x0_used")
        u2_ready, u2_turned, u2t_ready, logits_done = (sem("u2_ready"), sem("u2_turned"), sem("u2t_ready"),
                                                       sem("logits_done"))
        u2_stored = [sem(f"u2_stored{i}") for i in range(2)]
        iotas_ready, route_d, route_e, member_ready = (sem("iotas_ready"), sem("route_d"), sem("route_e"),
                                                       sem("member_ready"))
        rank_done, onehot_ready, slots_done, routed = sem("rank_done"), sem("onehot_ready"), sem("slots_done"), sem("routed")
        finw_landed = sem("finw_landed")
        w13_landed = [sem(f"w13_landed{i}") for i in range(2)]
        w2_landed = [sem(f"w2_landed{i}") for i in range(2)]
        xg_landed = [sem(f"xg_landed{i}") for i in range(2)]
        idx_ready = sem("idx_ready")
        xg_turned, xt_ready, gate_done, up_done = sem("xg_turned"), sem("xt_ready"), sem("gate_done"), sem("up_done")
        sig_ready, h_ready, ht_turned, ht_copied = sem("sig_ready"), sem("h_ready"), sem("ht_turned"), sem("ht_copied")
        o_done, o_free = sem("o_done"), sem("o_free")
        rows_stored = [sem(f"rows_stored{i}") for i in range(2)]
        fa_landed = [sem(f"fa_landed{i}") for i in range(3)]
        fb_landed = [sem(f"fb_landed{i}") for i in range(3)]
        fvar_ready, fstd_ready, f_scaled, y_out = sem("fvar_ready"), sem("fstd_ready"), sem("f_scaled"), sem("y_out")
        y_stored = [sem(f"y_stored{i}") for i in range(3)]
        carried = sem("carried")

        w_in_v = t["w_in"][0].rearrange("(k p) c -> p k c", p=P)
        w_ada_v = t["w_ada"][0].rearrange("(k p) c -> p k c", p=P)
        LAST_S2 = 13
        LEAST = 2 * ((2 * TOK // P + 1 + 1) // 2)

        def group_cols(g):
            return [COL_X + g * 256, COL_X + g * 256 + P, COL_B + g * N, COL_C + g * N,
                    COL_Z + g * 256, COL_Z + g * 256 + P]

        def state_rows(ap, pair_of_heads):
            return ap[0].rearrange("b (j h) p n -> (h p) b j n", h=2)[:, :, ds(pair_of_heads, 1), :]

        def tile_rows(ap, i):
            return ap[i * P:(i + 1) * P, :] if i < TILES else ap[SEQ:TOK, :]

        block = ctx.enter_context(nc.Block())

        @block.sync
        def _(sp):
            def load_x(i):
                if i >= 4:
                    sp.wait_ge(x0_stored[i % 4], 16 * (i // 4))
                    sp.wait_ge(x_turned, i - 3)
                src = t["x_prompt"][0, i * P:(i + 1) * P, :] if i < TILES else t["x_sample"].rearrange("b l d -> (b l) d")
                sp.dma_start(xr[i % 4][0:src.shape[0], :], src).then_inc(x_landed[i % 4], 16)

            def load_wada(q):
                if q >= 3:
                    sp.wait_ge(mod_done, q - 2)
                sp.dma_start(wada[q % 3], w_ada_v[:, :, q * 512:(q + 1) * 512]).then_inc(wada_landed[q % 3], 16)

            sp.dma_start(crow[0:NS, :], t["c_sample"]).then_inc(c_landed, 16)
            sp.dma_start(crow[NS:MROWS, :], t["c_prompt"]).then_inc(c_landed, 16)
            for i in range(2):
                load_x(i)
            load_wada(0)
            small = [(ln_g, t["ln_in_g"].partition_broadcast(P)), (ln_b, t["ln_in_b"].partition_broadcast(P)),
                     (bada, t["b_ada"][0].partition_broadcast(MROWS)),
                     (rows_c[0:3, :], t["conv_sc_w"][0]),
                     (rows_c[3:19, :], t["state_sc_conv"][0].rearrange("b r d -> (b r) d")),
                     (rows_c[19:21, :], t["ssm_norm_g"][0].rearrange("(r d) -> r d", r=2)),
                     (rows_s[0:4, :], t["conv_ssm_w"][0]), (rows_s[4:5, :], t["conv_ssm_b"]),
                     (rows_s[5:29, :], t["state_ssm_conv"][0].rearrange("b r d -> (b r) d")),
                     (dtb, t["dt_bias"][0].partition_broadcast(P)), (alog, t["a_log"][0].partition_broadcast(P)),
                     (dskb, t["d_skip"][0].partition_broadcast(P)), (w_dt, w_in_v[:, :, COL_DT:COL_DT + HEADS])]
            for dst, src in small:
                sp.dma_start(dst, src).then_inc(small_landed, 16)
            load_wada(1)
            load_x(2)
            load_wada(2)
            load_x(3)
            for q in range(3, 12):
                load_wada(q)
                if 1 <= q - 3 <= 5:
                    load_x(q)
            sp.dma_start(s_ssm_conv[0, :, 0:2, :], t["state_ssm_conv"][0, :, 1:3, :]).then_inc(old_rows, 16)
            sp.dma_start(s_sc_conv[0, :, 0:1, :], t["state_sc_conv"][0, :, 1:2, :]).then_inc(old_rows, 16)

            def load_unit(u, col):
                sp.dma_start(wslot[u], w_in_v[:, :, ds(col, P)]).then_inc(w_landed[u], 16)

            w_ssm_v = t["w_ssm_out"][0].rearrange("(k p) c -> p k c", p=P)
            w_sc_v = t["w_sc_out"][0].rearrange("(k p) c -> p k c", p=P)

            def load(u, src):
                sp.dma_start(wslot[u], src).then_inc(w_landed[u], 16)

            def load_b(c, h, x):
                load(3 * h + x, [w_in_v[:, :, COL_GB + h * P:], w_ssm_v[:, 0:KD, h * P:],
                                 w_ssm_v[:, KD:2 * KD, h * P:]][x][:, :, ds(c, P)])

            def load_short(c, h, x):
                load(3 * h + x, w_in_v[:, :, (COL_SC, COL_SH, COL_SB)[x] + h * P:][:, :, ds(c, P)])

            def load_a(c, h, x):
                load(3 * h + x, [w_in_v[:, :, COL_GA + h * P:], w_sc_v[:, :, h * P:]][x][:, :, ds(c, P)])

            def load_states(g):
                for j in range(2):
                    sp.dma_start(hs[:, :, j, :], state_rows(t["state_ssm"], g * 2 + j)).then_inc(h0_landed, 16)

            def turn(g, load, ssd):
                gp = g - 1 if ssd else None
                if ssd:
                    sp.wait_ge(tail_copied, gp + 1)
                    cols = [(0, gp * 256, 256), (256, gp * N + D_INNER, N), (384, gp * N + (D_INNER + GROUPS * N), N)]
                    for at, col, w in cols:
                        sp.dma_start(p_ssm_conv[0, 0, :, ds(col, w)], tail[0:3, at:at + w]).then_inc(tail_stored, 16)
                        sp.dma_start(s_ssm_conv[0, :, 2, ds(col, w)], tail[3:11, at:at + w]).then_inc(tail_stored, 16)
                for u in range(6):
                    if load:
                        sp.wait_ge(proj_done, g * 18 + (3 * u + 3))
                        if isinstance(g, int) and g == GROUPS - 1:
                            load_b(0, u // 3, u % 3)
                        else:
                            load_unit(u, group_cols(g + 1)[u])
                    if ssd and u == 1:
                        sp.wait_ge(hs_ready, gp + 1)
                        sp.wait_ge(sc_used, gp + 1)
                        for j in range(2):
                            sp.dma_start(state_rows(s_ssm, gp * 2 + j), hs[:, :, j, :]).then_inc(hs_stored, 16)
                    if ssd and u == 4:
                        sp.wait_ge(pstate_copied, gp + 1)
                        sp.dma_start(p_ssm[0, 0, ds(gp * HPG, HPG)].rearrange("(j h) p n -> (h p) j n", h=2),
                                     pstate.rearrange("p (j n) -> p j n", j=2)).then_inc(pstate_stored, 16)
                        if not (isinstance(g, int) and g == GROUPS):
                            sp.wait_ge(hs_stored, gp * 32 + 32)
                            load_states(gp + 1)

            sp.wait_ge(mod_added, 12)
            for u in range(6):
                load_unit(u, group_cols(0)[u])
            sp.wait_ge(dt_ready, 1)
            load_states(0)
            turn(0, True, False)
            with sp.Fori(0, GROUPS - 2) as i:
                turn(i + 1, True, True)
            turn(GROUPS - 1, True, True)
            turn(GROUPS, False, True)
            def merge_b_turn(i):
                c = sp.snap(i * 256 + 256)
                for h in range(2):
                    sp.wait_ge(gb_done, i * 6 + (3 * h + 3))
                    load_b(c, h, 0)
                    for x in (1, 2):
                        sp.wait_ge(yb_done, i * 6 + (3 * h + 3))
                        load_b(c, h, x)

            def short_turn(i):
                c = sp.snap(i * 256 + 256)
                for h in range(2):
                    for x in range(3):
                        sp.wait_ge(short_done, i * 18 + (9 * h + 3 * x + 3))
                        load_short(c, h, x)

            def merge_a_turn(i):
                c = sp.snap(i * 256 + 256)
                for h in range(2):
                    sp.wait_ge(ga_done, i * 6 + (3 * h + 3))
                    load_a(c, h, 0)
                    sp.wait_ge(ya_done, i * 6 + (3 * h + 3))
                    load_a(c, h, 1)

            with sp.Fori(0, 3) as i:
                merge_b_turn(i)
            for h in range(2):
                for x in range(3):
                    sp.wait_ge(gb_done if x == 0 else yb_done, 18 + 3 * h + 3)
                    load_short(0, h, x)
            sp.wait_ge(yb_done, 24)
            sp.dma_start(w_o, t["w_o"][0].rearrange("(k p) c -> p k c", p=P)).then_inc(wo_landed, 16)
            with sp.Fori(0, 3) as i:
                short_turn(i)
            for h in range(2):
                for x in range(2):
                    sp.wait_ge(short_done, 54 + 9 * h + 3 * x + 3)
                    load_a(0, h, x)

            def load_x0(i):
                rows = P if i < TILES else NS
                sp.dma_start(x0b[i % 2][0:rows, :], tile_rows(x0_dram, i)).then_inc(x0_landed[i % 2], 16)

            sp.wait_ge(short_done, 72)
            sp.wait_ge(ya_ready, 8)
            sp.wait_ge(tail2_copied, 8)
            sp.dma_start(p_sc_conv[0, 0], tail_sc[0:2, :]).then_inc(tail2_stored, 16)
            sp.dma_start(s_sc_conv[0, :, 1, :], tail_sc[2:10, :]).then_inc(tail2_stored, 16)
            sp.wait_ge(tail2_stored, 32)
            for dst, src in ((g1_p, mod_dram[NS, 2 * D:3 * D].partition_broadcast(P)),
                             (sh2_p, mod_dram[NS, 3 * D:4 * D].partition_broadcast(P)),
                             (sc2_p, mod_dram[NS, 4 * D:5 * D].partition_broadcast(P)),
                             (g1_s, mod_dram[0:NS, 2 * D:3 * D]), (sh2_s, mod_dram[0:NS, 3 * D:4 * D]),
                             (sc2_s, mod_dram[0:NS, 4 * D:5 * D]),
                             (mix_g, t["ln_mix_g"][0].partition_broadcast(P)),
                             (mix_b, t["ln_mix_b"][0].partition_broadcast(P)),
                             (w_r[:, :, 0:EGROUPS], t["w_route_g"][0].rearrange("(k p) e -> p k e", p=P)),
                             (w_r[:, :, EGROUPS:36], t["w_route_e"][0].rearrange("(k p) e -> p k e", p=P)),
                             (b_r[:, 0:EGROUPS], t["b_route_g"][0].partition_broadcast(P)),
                             (b_r[:, EGROUPS:36], t["b_route_e"][0].partition_broadcast(P))):
                sp.dma_start(dst, src).then_inc(mixw_landed, 16)
            for i in range(2):
                load_x0(i)
            with sp.Fori(0, 3) as i:
                merge_a_turn(i)
            for i in range(2, TILES + 1):
                sp.wait_ge(x0_used, i - 1)
                load_x0(i)

            sp.wait_ge(routed, 1)
            sp.wait_ge(u2_stored[0], 80)
            sp.wait_ge(u2_stored[1], 64)
            pairs = sp.value_load(plan[:, NBX:NBX + 1], min_val=1, max_val=BLOCKS // 2)
            for dst, src in ((g2_p, mod_dram[NS, 5 * D:6 * D].partition_broadcast(P)), (g2_s, mod_dram[0:NS, 5 * D:6 * D]),
                             (ffn_g, t["ln_ffn_g"][0].partition_broadcast(P)),
                             (ffn_b, t["ln_ffn_b"][0].partition_broadcast(P))):
                sp.dma_start(dst, src).then_inc(finw_landed, 16)
            with sp.Fori(0, pairs) as i:
                for b in range(2):
                    expert = sp.value_load(plan[:, ds(i * 2 + b, 1)], min_val=0, max_val=EXPERTS - 1)
                    sp.wait_ge(up_done, i * 2 + (b + 1))
                    sp.dma_start(w13[b], t["w_moe_13"][0].rearrange("e (k p) c -> p (e k) c", p=P)
                                 [:, ds(expert * KD, KD), :]).then_inc(w13_landed[b], 16)
                    sp.wait_ge(o_done, i * 2 + (b + 1))
                    sp.dma_start(w2[b], t["w_moe_2"][0].rearrange("e (k p) c -> p (e k) c", p=P)
                                 [:, ds(expert * 4, 4), :]).then_inc(w2_landed[b], 16)

            for i in range(TILES + 1):
                sp.wait_ge(y_out, i + 1)
                rows = P if i < TILES else NS
                dst = y_prompt[0, i * P:(i + 1) * P, :] if i < TILES else y_sample.rearrange("b l d -> (b l) d")
                sp.dma_start(dst, fa[i % 3][0:rows, :]).then_inc(y_stored[i % 3], 16)
            for i in range(3):
                sp.wait_ge(y_stored[i], 48)
            sp.wait_ge(old_rows, 32)
            sp.wait_ge(tail_stored, 768)
            sp.wait_ge(pstate_stored, 128)
            sp.wait_ge(hs_stored, 256)

        @block.gpsimd
        def _(pool):
            st = Steps(pool, pool_step)
            st.did(pool.memset(ones, 1.0))
            st.did(pool.memset(ones_avg, 1.0 / 256))
            st.did(pool.memset(epsc, EPS))
            st.settle()
            st.did(pool.affine_select(out=ident, in_=ones, pattern=[[1, P]], compare_op=ALU.is_equal, fill=0.0,
                                      base=0, channel_multiplier=-1))
            st.did(pool.affine_select(out=tri, in_=ones, pattern=[[1, P]], compare_op=ALU.is_ge, fill=0.0,
                                      base=0, channel_multiplier=-1))
            pool.affine_select(out=stri, in_=ones, pattern=[[1, P]], compare_op=ALU.is_gt, fill=0.0,
                               base=0, channel_multiplier=-1).then_inc(consts_ready, 1)
            pool.wait_ge(consts_ready, 1)
            for i in range(TILES + 1):
                pool.wait_ge(x0_ready, i + 1)
                rows = P if i < TILES else NS
                pool.dma_start(tile_rows(x0_dram, i), xr[i % 4][0:rows, :]).then_inc(x0_stored[i % 4], 16)
            pool.wait_ge(mod_added, 12)
            pool.dma_start(mod_dram, mod).then_inc(mod_stored, 16)
            pool.wait_ge(dt_ready, 1)
            pool.wait_ge(ut_ready, TILES)
            pool.wait_ge(mod_stored, 16)

            def rh(g, c):
                pool.tensor_tensor(rhs_cum.rearrange("p (r t) -> p r t", r=HPG), widen(tri, 1, HPG),
                                   widen(dta_g[:, ds(g * 32 + c * 4, 4)], 2, P), ALU.mult).then_inc(rh_ready, 1)

            def group(g, last):
                pool.wait_ge(silu_done, g * 4 + 4)
                pool.tensor_tensor(diag, widen(ident, 1, NS), widen(proc[2][:, SEQ:TOK], 2, N),
                                   ALU.mult).then_inc(diag_b_ready, 1)
                pool.wait_ge(sb_ready, g + 1)
                pool.tensor_tensor(diag, widen(ident, 1, NS), widen(proc[3][:, SEQ:TOK], 2, N),
                                   ALU.mult).then_inc(diag_c_ready, 1)
                for c in range(1, CHUNKS):
                    pool.wait_ge(cum_ready, g * 8 + c)
                    rh(g, c)
                if not last:
                    pool.wait_ge(pstate_stored, g * 16 + 16)
                    pool.wait_ge(cum_ready, g * 8 + 8)
                    rh(g + 1, 0)

            for first in range(LEAST, BLOCKS, KD):
                n = min(KD, BLOCKS - first)
                pool.dma_start(rows_dram[first * P:(first + n) * P, :].rearrange("(b p) d -> p b d", p=P),
                               arena[:, UT0:UT0 + n * D].rearrange("p (b d) -> p b d", b=n)).then_inc(filled, 16)
            rh(0, 0)
            with pool.Fori(0, GROUPS - 1) as g:
                group(g, False)
            group(GROUPS - 1, True)
            pool.wait_ge(filled, 16 * len(range(LEAST, BLOCKS, KD)))
            pool.wait_ge(merged_a, 24)
            st.did(pool.iota(iota_r, [[1, P]], base=0, channel_multiplier=0, allow_small_or_imprecise_dtypes=True))
            st.did(pool.iota(tok_id, [[P, NI]], base=0, channel_multiplier=1, allow_small_or_imprecise_dtypes=True))
            st.did(pool.memset(one32, 1.0))
            st.settle()
            pool.tensor_single_scalar(valid, tok_id, float(TOK), ALU.is_lt).then_inc(iotas_ready, 1)
            for i in range(TILES + 1):
                rows = P if i < TILES else NS
                pool.wait_ge(u2_ready, i + 1)
                pool.dma_start(tile_rows(u2_dram, i), u2[i % 2][0:rows, :]).then_inc(u2_stored[i % 2], 16)
            pool.wait_ge(u2_stored[0], 80)
            pool.wait_ge(u2_stored[1], 64)

            def gather(b, column):
                pool.indirect_dma_start(xg[b], None, u2_dram, bass.IndirectOffsetOnAxis(ap=column, axis=0)).then_inc(xg_landed[b], 16)

            def carry_wait(carries_before):
                if carries_before is not None:
                    pool.wait_ge(carried, carries_before)
                pool.tensor_tensor(spare, ones[:, 0:1], ones[:, 0:1], ALU.mult).then_inc(carried, 1)

            pool.wait_ge(routed, 1)
            pairs = pool.value_load(plan[:, NBX:NBX + 1], min_val=1, max_val=BLOCKS // 2)
            carry_wait(None)
            for b in range(2):
                gather(b, tok_of[:, b:b + 1])
            with pool.Fori(0, pairs) as i:
                for b in range(2):
                    pool.wait_ge(xg_turned, i * 2 + (b + 1))
                    pool.wait_ge(idx_ready, i * 2 + (b + 1))
                    carry_wait(i * 2 + (b + 1))
                    gather(b, idx2[:, b:b + 1])
            pool.wait_ge(xg_landed[0], pairs * 16 + 16)
            pool.wait_ge(xg_landed[1], pairs * 16 + 16)
            pool.wait_ge(rows_stored[0], pairs * 16)
            pool.wait_ge(rows_stored[1], pairs * 16)
            carry_wait(pairs * 2 + 1)
            for i in range(TILES + 1):
                rows = P if i < TILES else NS
                if i >= 3:
                    pool.wait_ge(y_stored[i % 3], 16 * (i // 3))
                for a, (buf, landed) in enumerate(((fa, fa_landed), (fb, fb_landed))):
                    pool.indirect_dma_start(
                        buf[i % 3][0:rows, :], None, rows_dram,
                        bass.IndirectOffsetOnAxis(ap=dest_i[0:rows, a * NI + i:a * NI + i + 1], axis=0)).then_inc(landed[i % 3], 16)

        @block.scalar
        def _(act):
            st = Steps(act, act_step)
            act.wait_ge(ct_turned, 1)
            act.activation(c_t.rearrange("p k m -> p (k m)"), bank6[:, 0:KD * MROWS], ACT.Silu).then_inc(ct_ready, 1)
            act.wait_ge(consts_ready, 1)

            def std(i):
                rows = P if i < TILES else NS
                act.wait_ge(var_ready, i + 1)
                act.activation(mv[0:rows, i % 4, 2:3], mv[0:rows, i % 4, 1:2], ACT.Sqrt,
                               bias=epsc[0:rows, :]).then_inc(std_ready, 1)

            def ut(i):
                act.wait_ge(cols_copied, 1)
                act.wait_ge(x_turned, i + 1)
                for k in range(KD):
                    src = banks[2 + 2 * (i % 2) + k // 4][:, (k % 4) * P:(k % 4 + 1) * P]
                    last = act.activation(uT[:, k, i * P:(i + 1) * P], src, ACT.Identity,
                                          bias=mod_t[:, k, NS:MROWS], scale=mod_t[:, KD + k, NS:MROWS])
                last.then_inc(ut_ready, 1)

            for i in range(4):
                std(i)
            for i in range(TILES):
                if i + 4 <= TILES:
                    std(i + 4)
                ut(i)
            act.wait_ge(dt_in, 1)
            st.did(act.activation(dte, dtr, ACT.Abs))
            st.settle()
            act.activation(dte, dte, ACT.Exp, scale=-1.0).then_inc(dt_exp, 1)
            act.wait_ge(small_landed, 13 * 16)
            act.activation(alog, alog, ACT.Exp).then_inc(dt_ln, 1)
            act.wait_ge(dt_sum, 1)
            act.activation(dtl, dtw, ACT.Ln).then_inc(dt_ln, 1)
            act.wait_ge(dta_ready, 2)
            act.activation(das, das, ACT.Exp).then_inc(dt_exp, 1)
            act.wait_ge(dt_sum, 2)
            act.activation(wend, wend, ACT.Exp).then_inc(wend_ready, 1)
            act.activation(decay, cend, ACT.Exp).then_inc(wend_ready, 1)

            def turn(g, proj, ssd):
                gp = g - 1 if ssd else None
                n0 = g * 18

                def cum_side(c):
                    q = gp * 8
                    act.wait_ge(cum_ready, q + (c + 1))
                    act.activation(cumb, banks[4][:, :], ACT.Copy).then_inc(cum_copied, 1)
                    act.wait_ge(cum_copied, q + (c + 1))
                    act.activation(csc, cumb, ACT.Exp).then_inc(ecum_ready, 1)

                def e_side(c):
                    act.wait_ge(seg_ready, gp * 8 + (c + 1))
                    act.activation(segm, segm, ACT.Exp).then_inc(e_ready, 1)

                def rms_side(c):
                    w = P if c < 8 else NS
                    act.wait_ge(rms_ready, gp * 9 + (c + 1))
                    if c:
                        act.wait_ge(normed, gp * 9 + c)
                    act.activation(rs[:, 0:w], bank7[:, 0:w], ACT.Ln, bias=epsc).then_inc(act_ln, 1)
                    act.wait_ge(act_ln, gp * 9 + (c + 1))
                    act.activation(rs[:, 0:w], rs[:, 0:w], ACT.Exp, scale=-0.5).then_inc(rs_ready, 1)

                def square(c):
                    w = P if c < 8 else NS
                    act.wait_ge(y_gated, gp * 9 + (c + 1))
                    if c:
                        act.wait_ge(rms_ready, gp * 9 + c)
                    act.activation(sq[:, :, 0:w], ybuf[c % 2][:, :, 0:w], ACT.Square).then_inc(sq_ready, 1)

                def silu(u):
                    act.wait_ge(conv_done, gp * 4 + (u + 1))
                    act.activation(proc[u], proc[u], ACT.Silu).then_inc(silu_done, 1)

                if ssd:
                    for j in range(2):
                        act.wait_ge(raw_ready, gp * 18 + (15 + 3 * j))
                        act.activation(raw[4 + j], raw[4 + j], ACT.Silu).then_inc(zsilu_done, 1)
                for s in range(18):
                    u = s // 3
                    if proj:
                        act.wait_ge(proj_done, n0 + (s + 1))
                        if ssd and u < 4:
                            act.wait_ge(conv_done, gp * 4 + (u + 1))
                            if s == 0:
                                act.wait_ge(tails_done, gp + 1)
                        if ssd and u >= 4:
                            act.wait_ge(y_gated, gp * 9 + 3 * (s % 3 + 1))
                        act.activation(raw[u][:, (s % 3) * SUB:(s % 3 + 1) * SUB], banks[s % 3][:, 0:SUB],
                                       ACT.Copy).then_inc(raw_ready, 1)
                    if not ssd:
                        continue
                    if s == 0:
                        act.wait_ge(tails_done, gp + 1)
                        act.activation(tail, bank6[0:11, :], ACT.Copy).then_inc(tail_copied, 1)
                    if s <= 2:
                        silu(s)
                    if s == 2:
                        silu(3)
                    if s == 3:
                        cum_side(0)
                        e_side(0)
                    if 6 <= s <= LAST_S2:
                        c = s - 6
                        if c < 7:
                            cum_side(c + 1)
                        if c:
                            rms_side(c - 1)
                        square(c)
                        if c < 7:
                            e_side(c + 1)
                    if s == 14:
                        rms_side(7)
                        square(8)
                    if s == 15:
                        rms_side(8)
                if ssd:
                    act.wait_ge(normed, gp * 9 + 9)
                    act.wait_ge(tail_stored, gp * 96 + 96)

            act.wait_ge(dt_ready, 1)
            act.wait_ge(mod_stored, 16)
            turn(0, True, False)
            with act.Fori(0, GROUPS - 1) as i:
                turn(i + 1, True, True)
            turn(GROUPS, False, True)
            def gates(i, first, done, ready, used):
                for h in range(2):
                    for part in range(3):
                        n = 3 * h + part
                        act.wait_ge(done, i * 6 + (n + 1))
                        if not first:
                            act.wait_ge(used, i * 6 + (n - 5))
                        act.activation(gsb[h][:, part * SUB:(part + 1) * SUB], banks[part][:, 0:SUB],
                                       ACT.Sigmoid).then_inc(ready, 1)

            gates(0, True, gb_done, gsig_ready, merged_b)
            with act.Fori(0, 3) as i:
                gates(i + 1, False, gb_done, gsig_ready, merged_b)

            def short(i, first):
                for h in range(2):
                    v = 3 * h
                    for part in range(3):
                        act.wait_ge(short_done, i * 18 + (3 * v + part + 1))
                        if not first:
                            act.wait_ge(p_made, i * 6 + (3 * h + part - 5))
                        act.activation(scb[h][:, part * SUB:(part + 1) * SUB],
                                       banks[3 * (v % 2) + part][:, 0:SUB], ACT.Copy).then_inc(sc_copied, 1)
                    for part in range(3):
                        act.wait_ge(short_done, i * 18 + (3 * (v + 2) + part + 1))
                        if not first:
                            act.wait_ge(ya_ready, i * 2 + (h - 1))
                        act.activation(sbb[h][:, part * SUB:(part + 1) * SUB],
                                       banks[3 * (v % 2) + part][:, 0:SUB], ACT.Copy).then_inc(sb_copied, 1)
                    act.wait_ge(tail2_done, i * 2 + (h + 1))
                    act.activation(tail_sc[:, ds((i * 2 + h) * P, P)], bank6[0:10, h * P:(h + 1) * P],
                                   ACT.Copy).then_inc(tail2_copied, 1)

            short(0, True)
            with act.Fori(0, 3) as i:
                short(i + 1, False)
            gates(0, True, ga_done, gsig2_ready, merged_a)
            with act.Fori(0, 3) as i:
                gates(i + 1, False, ga_done, gsig2_ready, merged_a)

            for i in range(TILES + 1):
                rows = P if i < TILES else NS
                act.wait_ge(mvar_ready, i + 1)
                act.activation(mv2[0:rows, i % 2, 2:3], mv2[0:rows, i % 2, 1:2], ACT.Sqrt,
                               bias=epsc[0:rows, :]).then_inc(mstd_ready, 1)
                act.wait_ge(u2_turned, i + 1)
                for half in range(2):
                    src = banks[4 + half].rearrange("p (k t) -> p k t", k=4)[:, :, 0:rows]
                    dst = u2t[i % 2][:, 512 * half:512 * half + 512].rearrange("p (k t) -> p k t", k=4)[:, :, 0:rows]
                    last = act.activation(dst, src, ACT.Copy)
                    if half == 0:
                        st.did(last)
                last.then_inc(u2t_ready, 1)
            act.wait_ge(route_d, 1)
            act.activation(grp_t, grp_d, ACT.Exp).then_inc(route_e, 1)
            act.wait_ge(route_d, 2)
            act.activation(lt, ld, ACT.Exp).then_inc(route_e, 1)
            act.wait_ge(route_d, 3)
            act.activation(wb, wb, ACT.Exp).then_inc(route_e, 1)

            def turned(b, n):
                act.wait_ge(xg_turned, n)
                st.did(act.activation(xt[b][:, 0:512], banks[4][:, :], ACT.Copy))
                act.activation(xt[b][:, 512:1024], banks[5][:, :], ACT.Copy).then_inc(xt_ready, 1)

            act.wait_ge(routed, 1)
            pairs = act.value_load(plan[:, NBX:NBX + 1], min_val=1, max_val=BLOCKS // 2)
            turned(0, 1)
            with act.Fori(0, pairs) as i:
                for b in range(2):
                    act.wait_ge(gate_done, i * 2 + (b + 1))
                    act.activation(hm[b], banks[0][:, :], ACT.Silu).then_inc(sig_ready, 1)
                    turned(1 - b, i * 2 + (b + 2))
                    act.wait_ge(o_free, i * 2 + (b + 2))
                    act.dma_start(rows_dram[ds((i * 2 + b) * P, P), :], yo[b]).then_inc(rows_stored[b], 16)
            for i in range(TILES + 1):
                rows = P if i < TILES else NS
                act.wait_ge(fa_landed[i % 3], 16 * (i // 3 + 1))
                act.activation(fa[i % 3][0:rows, :], fa[i % 3][0:rows, :], ACT.Copy,
                               scale=wts[0:rows, i:i + 1]).then_inc(f_scaled, 1)
                act.wait_ge(fvar_ready, i + 1)
                act.activation(mv2[0:rows, i % 2, 2:3], mv2[0:rows, i % 2, 1:2], ACT.Sqrt,
                               bias=epsc[0:rows, :]).then_inc(fstd_ready, 1)

        @block.vector
        def _(dve):
            st = Steps(dve, dve_step)

            def norm(i):
                rows = P if i < TILES else NS
                x = xr[i % 4][0:rows, :]
                dve.wait_ge(x_landed[i % 4], 16 * (i // 4 + 1))
                for h in range(2):
                    st.did(dve.bn_stats(stats[0:rows, i % 4, 6 * h:6 * h + 6], x[:, 512 * h:512 * h + 512]))
                st.settle()
                dve.bn_aggr(mv[0:rows, i % 4, 0:2], stats[0:rows, i % 4, :]).then_inc(var_ready, 1)
                dve.wait_ge(std_ready, i + 1)
                st.did(dve.reciprocal(mv[0:rows, i % 4, 3:4], mv[0:rows, i % 4, 2:3]))
                st.settle()
                st.did(dve.tensor_scalar(x, x, mv[0:rows, i % 4, 0:1], mv[0:rows, i % 4, 3:4],
                                         ALU.subtract, ALU.mult))
                st.settle()
                if i == 0:
                    dve.wait_ge(small_landed, 13 * 16)
                st.did(dve.tensor_tensor(x, x, ln_g[0:rows, :], ALU.mult))
                st.settle()
                dve.tensor_tensor(x, x, ln_b[0:rows, :], ALU.add).then_inc(x0_ready, 1)

            def add_mod(q):
                dve.wait_ge(mod_done, q + 1)
                dve.tensor_tensor(mod[:, q * 512:(q + 1) * 512], banks[q % 2][0:MROWS, :],
                                  bada[:, q * 512:(q + 1) * 512], ALU.add).then_inc(mod_added, 1)

            for q in range(4):
                norm(q)
                add_mod(q)
            dve.wait_ge(cols_turned, 1)
            st.did(dve.tensor_copy(mod_t[:, 0:KD, :], bank6[:, 0:72].rearrange("p (k m) -> p k m", k=KD)))
            dve.tensor_scalar(mod_t[:, KD:16, :], bank6[:, 72:144].rearrange("p (k m) -> p k m", k=KD), 1.0, None,
                              ALU.add).then_inc(cols_copied, 1)
            dve.wait_ge(cols_turned, 2)
            src = bank6[:, 0:KD * ROWS_C].rearrange("p (k r) -> p k r", k=KD)
            for a, b in ((0, 3), (19, 21)):
                st.did(dve.tensor_copy(colc[:, :, a:b], src[:, :, a:b]))
            for r in range(2):
                last = dve.tensor_copy(colc[:, :, 3 + r * NS:3 + (r + 1) * NS],
                                       src[:, :, 3:19].rearrange("p k (b r) -> p r k b", r=2)[:, r])
                if r == 0:
                    st.did(last)
            last.then_inc(cols_copied, 1)
            dve.wait_ge(cols_copied, 2)
            for r in range(2):
                st.did(dve.tensor_copy(normg[:, KD * r:KD * r + KD], colc[:, :, 19 + r]))
            for h in range(2):
                st.did(dve.tensor_copy(dskip[HD * h:HD * h + HD, :],
                                       dskb[HD * h:HD * h + HD, :].rearrange("p (j h) -> p h j", h=2)[:, h, :]))
            for half in range(2):
                dve.wait_ge(cols_turned, 3 + half)
                src = bank6[:, 0:16 * ROWS_S].rearrange("p (k r) -> p k r", k=16)
                st.did(dve.tensor_copy(convw_f.rearrange("p (k r) -> p k r", r=5)[:, 16 * half:16 * half + 16, :],
                                       src[:, :, 0:5]))
                for r in range(3):
                    last = dve.tensor_copy(
                        convst_f.rearrange("p (k r b) -> p k r b", r=3, b=NS)[:, 16 * half:16 * half + 16, r, :],
                        src[:, :, 5:29].rearrange("p k (b r) -> p r k b", r=3)[:, r])
                    if r < 2:
                        st.did(last)
                last.then_inc(cols_copied, 1)
            for i in range(TILES):
                if i + 4 <= TILES:
                    norm(i + 4)
                add_mod(4 + i)
            dve.wait_ge(x_turned, 9)
            for k in range(KD):
                src = banks[2 + k // 4][:, (k % 4) * P:(k % 4) * P + NS]
                st.did(dve.tensor_tensor(uT[:, k, SEQ:TOK], src, mod_t[:, KD + k, 0:NS], ALU.mult))
            st.settle()
            for k in range(KD):
                last = dve.tensor_tensor(uT[:, k, SEQ:TOK], uT[:, k, SEQ:TOK], mod_t[:, k, 0:NS], ALU.add)
            last.then_inc(ut_s_ready, 1)

            st.did(dve.memset(dtr, 0.0))
            st.settle()
            dve.wait_ge(dt_raw, 1)
            NP_ = TILES * HEADS
            st.did(dve.tensor_tensor(dtr[:, 0:NP_].rearrange("p (c h) -> p c h", c=TILES),
                                     bank7[:, 0:NP_].rearrange("p (c h) -> p c h", c=TILES),
                                     widen(dtb, 1, TILES), ALU.add))
            dve.tensor_tensor(dtr[0:NS, NP_:DTW], bank7[0:NS, NP_:DTW], dtb[0:NS, :], ALU.add).then_inc(dt_in, 1)
            dve.wait_ge(dt_exp, 1)
            st.did(dve.tensor_scalar(dtw, dte, 1.0, None, ALU.add))
            st.settle()
            dve.tensor_scalar(dtq, dtw, -1.0, None, ALU.add).then_inc(dt_sum, 1)
            dve.wait_ge(dt_sum, 1)
            st.did(dve.tensor_scalar(dtm, dtq, 0.0, None, ALU.is_equal))
            st.settle()
            st.did(dve.tensor_tensor(dtq, dtq, dtm, ALU.add))
            st.settle()
            st.did(dve.reciprocal(dtq, dtq))
            dve.wait_ge(dt_ln, 2)
            st.did(dve.tensor_tensor(dtl, dtl, dtm, ALU.add))
            st.settle()
            st.did(dve.tensor_tensor(dtl, dtl, dte, ALU.mult))
            st.did(dve.tensor_scalar(dtr, dtr, 0.0, None, ALU.max))
            st.settle()
            st.did(dve.tensor_tensor(dtl, dtl, dtq, ALU.mult))
            st.did(dve.tensor_scalar(alog, alog, -1.0, None, ALU.mult))
            st.settle()
            st.did(dve.tensor_tensor(dtr, dtr, dtl, ALU.add))
            st.settle()
            gcr = dict(g=GROUPS, c=CHUNKS, r=HPG)
            st.did(dve.tensor_copy(dt_g.rearrange("p (g c r) -> p c g r", **gcr),
                                   dtr[:, 0:NP_].rearrange("p (c g r) -> p c g r", **gcr)))
            st.settle()
            dve.tensor_tensor(dta_g.rearrange("p (g c r) -> p g c r", **gcr),
                              dt_g.rearrange("p (g c r) -> p g c r", **gcr),
                              widen(alog.rearrange("p (g r) -> p g r", g=GROUPS), 2, CHUNKS),
                              ALU.mult).then_inc(dta_ready, 1)
            dve.wait_ge(mod_stored, 16)
            dve.tensor_tensor(das, dtr[0:NS, NP_:DTW], alog[0:NS, :], ALU.mult).then_inc(dta_ready, 1)
            dve.wait_ge(cum_done, 1)
            st.did(dve.tensor_copy(cum_t, bank7[:, 0:256]))
            st.did(dve.tensor_copy(cend, bank7[:, 256:512]))
            st.settle()
            dve.tensor_tensor(wend, cend, cum_t, ALU.subtract).then_inc(dt_sum, 1)
            dve.wait_ge(dt_exp, 2)
            spr = spread.rearrange("p (x b h) -> p x b h", x=2, b=NS)
            st.did(dve.tensor_tensor(spr[:, 0], widen(dtr[0:NS, NP_:DTW], 1, NS),
                                     widen(ident[0:NS, 0:NS], 2, HEADS), ALU.mult))
            dve.tensor_tensor(spr[:, 1], widen(das, 1, NS),
                              widen(ident[0:NS, 0:NS], 2, HEADS), ALU.mult).then_inc(spread_ready, 1)
            dve.wait_ge(wend_ready, 1)
            st.did(dve.tensor_tensor(wend, wend, dt_g, ALU.mult))
            dve.wait_ge(spread_done, 1)
            dve.wait_ge(wend_ready, 2)
            for x, dst in ((0, dt_s), (1, dec_s)):
                for h in range(2):
                    src = bank7[HD * h:HD * h + HD, 256 * x:256 * x + 256].rearrange("p (b j h) -> p h j b", b=NS, h=2)
                    last = dve.tensor_copy(dst[HD * h:HD * h + HD, :].rearrange("p (j b) -> p j b", b=NS), src[:, h])
                    if (x, h) != (1, 1):
                        st.did(last)
            last.then_inc(dt_ready, 1)
            dve.wait_ge(dt_ready, 1)

            def scan(g):
                idx = [g * 2, g * 2 + 1, g + 16, g + 24]
                for u in range(4):
                    src, dst = raw[u], proc[u]

                    def w(k):
                        return convw_f[:, ds(idx[u] * 5 + k, 1)]

                    def old(r):
                        return convst_f[:, ds(idx[u] * 24 + r * 8, NS)]

                    dve.wait_ge(raw_ready, g * 18 + (3 * u + 3))
                    st.did(dve.tensor_scalar(dst, src, w(3), w(4), ALU.mult, ALU.add))
                    for back in (1, 2, 3):
                        st.settle()
                        st.did(dve.scalar_tensor_tensor(dst[:, SEQ:TOK], old(3 - back), w(3 - back), dst[:, SEQ:TOK],
                                                        ALU.mult, ALU.add))
                        last = dve.scalar_tensor_tensor(dst[:, back:SEQ], src[:, 0:SEQ - back], w(3 - back),
                                                        dst[:, back:SEQ], ALU.mult, ALU.add)
                        if back < 3:
                            st.did(last)
                    last.then_inc(conv_done, 1)

                def operands(c):
                    at = slice(c * P, (c + 1) * P)
                    q = g * 8 + (c + 1)
                    rp = dict(r=HPG)
                    dve.wait_ge(scores_ready, q)
                    st.did(dve.tensor_tensor(cb_m, banks[3][:, 384:512], tri, ALU.mult))
                    x_tok = banks[3][:, 0:256].rearrange("p (r d) -> p r d", **rp)
                    st.did(dve.tensor_tensor(xdt.rearrange("p (r d) -> p r d", **rp), x_tok,
                                             widen(dt_g[:, ds(g * 32 + c * 4, 4)], 2, HD), ALU.mult))
                    st.did(dve.tensor_tensor(xw.rearrange("p (r d) -> p r d", **rp), x_tok,
                                             widen(wend[:, ds(g * 32 + c * 4, 4)], 2, HD), ALU.mult))
                    st.did(dve.tensor_copy(b_tok, banks[3][:, 256:384]))
                    dve.wait_ge(cum_copied, q)
                    for r in range(HPG):
                        last = dve.tensor_scalar(segm[:, r * P:(r + 1) * P], cumb[:, r * P:(r + 1) * P],
                                                 cum_t[:, ds(g * 32 + (c * 4 + r), 1)], 0.0, ALU.subtract, ALU.min)
                        if r < 3:
                            st.did(last)
                    last.then_inc(seg_ready, 1)
                    dve.wait_ge(ecum_ready, q)
                    cs3 = csc.rearrange("p (r t) -> p r t", **rp)
                    st.did(dve.tensor_tensor(cs3, cs3, widen(proc[3][:, at], 1, HPG), ALU.mult))
                    dve.wait_ge(e_ready, q)
                    st.settle()
                    m3 = segm.rearrange("p (r t) -> p r t", **rp)
                    dve.tensor_tensor(m3, m3, widen(cb_m, 1, HPG), ALU.mult).then_inc(ops_ready, 1)

                def gate(c, y_in, w):
                    at = slice(c * P, c * P + w)
                    yb = ybuf[c % 2][:, :, 0:w]
                    for j in range(2):
                        st.did(dve.scalar_tensor_tensor(yb[:, j, :], xs2[:, j, at], dskip[:, ds(g * 2 + j, 1)],
                                                        y_in[:, j, 0:w], ALU.mult, ALU.add))
                    st.settle()
                    dve.tensor_tensor(yb, yb, z2[:, :, at], ALU.mult).then_inc(y_gated, 1)

                def apply(c):
                    w = P if c < 8 else NS
                    dve.wait_ge(rs_ready, g * 9 + (c + 1))
                    for j in range(2):
                        last = dve.scalar_tensor_tensor(ybT_f[:, ds((g * 2 + j) * TOK + c * P, w)],
                                                        ybuf[c % 2][:, j, 0:w], normg[:, ds(g * 2 + j, 1)],
                                                        rs[:, 0:w], ALU.mult, ALU.mult)
                        if j == 0:
                            st.did(last)
                    last.then_inc(normed, 1)

                operands(0)
                dve.wait_ge(silu_done, g * 4 + 4)
                st.did(dve.tensor_tensor(dtx, xs2[:, :, SEQ:TOK],
                                         dt_s[:, ds(g * 16, 16)].rearrange("p (j b) -> p j b", j=2), ALU.mult))
                dve.wait_ge(h0_landed, g * 32 + 32)
                st.did(dve.tensor_tensor(hs, hs, widen(dec_s[:, ds(g * 16, 16)].rearrange("p (j b) -> p b j", j=2),
                                                       3, N), ALU.mult))
                dve.wait_ge(sb_ready, g + 1)
                st.settle()
                spread_bc = pair[:, :].rearrange("p (b n) -> p b n", b=NS)
                st.did(dve.tensor_tensor(tmp, spread_bc, widen(dtx[:, 0, :], 2, N), ALU.mult))
                st.settle()
                st.did(dve.tensor_tensor(hs[:, :, 0, :], hs[:, :, 0, :], tmp, ALU.add))
                st.settle()
                dve.tensor_tensor(tmp, spread_bc, widen(dtx[:, 1, :], 2, N), ALU.mult).then_inc(sb_used, 1)
                dve.wait_ge(sb_used, g + 1)
                dve.tensor_tensor(hs[:, :, 1, :], hs[:, :, 1, :], tmp, ALU.add).then_inc(hs_ready, 1)
                dve.wait_ge(hs_ready, g + 1)
                dve.wait_ge(sc_ready, g + 1)
                st.did(dve.tensor_tensor(tmp, hs[:, :, 0, :], spread_bc, ALU.mult))
                st.settle()
                st.did(dve.tensor_reduce(ys[:, 0, :], tmp, AX.X, ALU.add))
                st.settle()
                dve.tensor_tensor(tmp, hs[:, :, 1, :], spread_bc, ALU.mult).then_inc(sc_used, 1)
                dve.wait_ge(sc_used, g + 1)
                st.did(dve.tensor_reduce(ys[:, 1, :], tmp, AX.X, ALU.add))
                dve.wait_ge(zsilu_done, g * 2 + 2)
                for c in range(CHUNKS):
                    dve.wait_ge(y_ready, g * 8 + (c + 1))
                    new = banks[5][:, 256:512]
                    if c == 0:
                        st.did(dve.tensor_copy(h_t, new))
                    else:
                        h3 = h_t.rearrange("p (r d) -> p r d", r=HPG)
                        st.did(dve.tensor_tensor(h3, h3, widen(decay[:, ds(g * 32 + c * 4, 4)], 2, HD), ALU.mult))
                        st.settle()
                        st.did(dve.tensor_tensor(h_t, h_t, new, ALU.add))
                    gate(c, banks[5][:, 0:256].rearrange("p (j t) -> p j t", j=2), P)
                    if c < 7:
                        operands(c + 1)
                    if c:
                        apply(c - 1)
                st.settle()
                dve.wait_ge(normed, g * 9 + 7)
                gate(8, ys, NS)
                apply(7)
                dve.wait_ge(ht_ready, g + 1)
                dve.tensor_copy(pstate, bank6[:, 0:256]).then_inc(pstate_copied, 1)
                apply(8)

            PER = 137
            with dve.Fori(0, GROUPS) as g:
                st.enter(g, PER)
                scan(g)
            st.leave(GROUPS)
            dve.wait_ge(hs_stored, 256)
            dve.wait_ge(tail_stored, 768)
            dve.wait_ge(pstate_stored, 128)

            def merge_b(i):
                for h in range(2):
                    for part in range(3):
                        n = 3 * h + part
                        dve.wait_ge(gsig_ready, i * 6 + (n + 1))
                        dve.wait_ge(yb_done, i * 6 + (n + 1))
                        dve.tensor_tensor(merged_f[:, ds((i * 2 + h) * TOK + part * SUB, SUB)],
                                          gsb[h][:, part * SUB:(part + 1) * SUB], banks[3 + part][:, 0:SUB],
                                          ALU.mult).then_inc(merged_b, 1)

            with dve.Fori(0, 4) as i:
                merge_b(i)

            def short(i):
                for h in range(2):
                    p, k = pt[h], i * 2 + h
                    for part in range(3):
                        at = slice(part * SUB, (part + 1) * SUB)
                        dve.wait_ge(sc_copied, i * 6 + (3 * h + part + 1))
                        dve.wait_ge(short_done, i * 18 + (9 * h + 3 + part + 1))
                        dve.tensor_tensor(p[:, at], scb[h][:, at], banks[3 * ((3 * h + 1) % 2) + part][:, 0:SUB],
                                          ALU.mult).then_inc(p_made, 1)
                    dve.wait_ge(p_made, i * 6 + (3 * h + 3))

                    def w(x):
                        return colc_f[:, ds(k * ROWS_C + x, 1)]

                    st.did(dve.tensor_scalar(acc, p, w(2), None, ALU.mult))
                    for back in (1, 2):
                        st.settle()
                        st.did(dve.scalar_tensor_tensor(acc[:, SEQ:TOK],
                                                        colc_f[:, ds(k * ROWS_C + (3 + (2 - back) * NS), NS)],
                                                        w(2 - back), acc[:, SEQ:TOK], ALU.mult, ALU.add))
                        st.did(dve.scalar_tensor_tensor(acc[:, back:SEQ], p[:, 0:SEQ - back], w(2 - back),
                                                        acc[:, back:SEQ], ALU.mult, ALU.add))
                    dve.wait_ge(sb_copied, i * 6 + (3 * h + 3))
                    st.settle()
                    dve.tensor_tensor(ya_f[:, ds(k * TOK, TOK)], acc, sbb[h], ALU.mult).then_inc(ya_ready, 1)

            SHORT_STEPS = 10
            with dve.Fori(0, 4) as i:
                st.enter(i, SHORT_STEPS)
                short(i)
            st.leave(4)

            def merge_a(i):
                for h in range(2):
                    for part in range(3):
                        n = 3 * h + part
                        g = gsb[h][:, part * SUB:(part + 1) * SUB]
                        m = merged_f[:, ds((i * 2 + h) * TOK + part * SUB, SUB)]
                        dve.wait_ge(gsig2_ready, i * 6 + (n + 1))
                        dve.wait_ge(ya_done, i * 6 + (n + 1))
                        st.did(dve.tensor_tensor(g, g, banks[3 + part][:, 0:SUB], ALU.mult))
                        st.settle()
                        dve.tensor_tensor(m, m, g, ALU.add).then_inc(merged_a, 1)

            with dve.Fori(0, 4) as i:
                st.enter(i, 6)
                merge_a(i)
            st.leave(4)

            dve.wait_ge(mixw_landed, 12 * 16)
            dve.wait_ge(filled, 16 * len(range(LEAST, BLOCKS, KD)))
            dve.wait_ge(merged_a, 24)
            for row in (g1_p, g1_s, sc2_p, sc2_s):
                st.did(dve.tensor_scalar(row, row, 1.0, None, ALU.add))
            for i in range(TILES + 1):
                rows = P if i < TILES else NS
                g1, sc2, sh2 = (g1_p, sc2_p, sh2_p) if i < TILES else (g1_s, sc2_s, sh2_s)
                x = x1[0:rows, i, :]
                x0 = x0b[i % 2][0:rows, :]
                st.settle()
                dve.wait_ge(wo_done, i + 1)
                for half in range(2):
                    at = slice(512 * half, 512 * half + 512)
                    st.did(dve.tensor_tensor(x[:, at], banks[2 * (i % 2) + half][0:rows, :], g1[:, at], ALU.mult))
                st.settle()
                dve.wait_ge(x0_landed[i % 2], 16 * (i // 2 + 1))
                dve.scalar_tensor_tensor(x, x0, ALPHA, x, ALU.mult, ALU.add).then_inc(x0_used, 1)
                dve.wait_ge(x0_used, i + 1)
                for half in range(2):
                    st.did(dve.bn_stats(stats2[0:rows, 6 * half:6 * half + 6], x[:, 512 * half:512 * half + 512]))
                st.settle()
                dve.bn_aggr(mv2[0:rows, i % 2, 0:2], stats2[0:rows, :]).then_inc(mvar_ready, 1)
                dve.wait_ge(mstd_ready, i + 1)
                st.did(dve.reciprocal(mv2[0:rows, i % 2, 3:4], mv2[0:rows, i % 2, 2:3]))
                st.settle()
                st.did(dve.tensor_scalar(x, x, mv2[0:rows, i % 2, 0:1], mv2[0:rows, i % 2, 3:4],
                                         ALU.subtract, ALU.mult))
                st.settle()
                st.did(dve.tensor_tensor(x, x, mix_g[0:rows, :], ALU.mult))
                st.settle()
                st.did(dve.tensor_tensor(x, x, mix_b[0:rows, :], ALU.add))
                st.settle()
                u = u2[i % 2][0:rows, :]
                if i >= 2:
                    dve.wait_ge(u2_turned, i - 1)
                    dve.wait_ge(u2_stored[i % 2], 16 * (i // 2))
                st.did(dve.tensor_tensor(u, x, sc2, ALU.mult))
                st.settle()
                dve.tensor_tensor(u, u, sh2, ALU.add).then_inc(u2_ready, 1)

            dve.wait_ge(iotas_ready, 1)
            st.did(dve.memset(logit, 0.0))
            st.settle()
            dve.wait_ge(logits_done, 1)
            ps = bank7[:, 0:NI * 36].rearrange("p (i e) -> p i e", i=NI)
            st.did(dve.tensor_tensor(logit[:, 0:TILES, :], ps[:, 0:TILES, :], widen(b_r, 1, TILES), ALU.add))
            st.did(dve.tensor_tensor(logit[0:NS, TILES, :], ps[0:NS, TILES, :], b_r[0:NS, :], ALU.add))
            st.settle()

            def step(ins):
                st.did(ins)
                st.settle()

            def first_of(eq, n, idx, onehot):
                step(dve.scalar_tensor_tensor(eq, eq, -64.0, widen(iota_r[:, 0:n], 1, NI), ALU.mult, ALU.add))
                step(dve.tensor_reduce(idx, eq, AX.X, ALU.min))
                step(dve.tensor_scalar(idx, idx, 64.0, None, ALU.add))
                step(dve.tensor_tensor(onehot, widen(iota_r[:, 0:n], 1, NI), widen(idx, 2, n), ALU.is_equal))

            l4, l32 = logit[:, :, 0:EGROUPS], logit[:, :, EGROUPS:36]
            step(dve.tensor_reduce(gmx, l4, AX.X, ALU.max))
            dve.tensor_tensor(grp_d, l4, widen(gmx, 2, EGROUPS), ALU.subtract).then_inc(route_d, 1)
            dve.wait_ge(route_d, 1)
            dve.wait_ge(route_e, 1)
            step(dve.tensor_reduce(gsum, grp_t, AX.X, ALU.add))
            step(dve.tensor_scalar(grp_d, grp_d, 0.0, None, ALU.is_equal))
            first_of(grp_d, EGROUPS, gix, grp)
            step(dve.tensor_scalar(grp_t, grp, -NEG, NEG, ALU.mult, ALU.add))

            def by_group(x):
                return x.rearrange("p i (g e) -> p i g e", g=EGROUPS)

            step(dve.tensor_tensor(by_group(lm), by_group(l32), widen(grp, 3, PER_GROUP), ALU.mult))
            step(dve.tensor_tensor(by_group(lm), by_group(lm), widen(grp_t, 3, PER_GROUP), ALU.add))
            step(dve.tensor_reduce(m1, lm, AX.X, ALU.max))
            dve.tensor_tensor(ld, lm, widen(m1, 2, EXPERTS), ALU.subtract).then_inc(route_d, 1)
            dve.wait_ge(route_d, 2)
            dve.wait_ge(route_e, 2)
            step(dve.tensor_reduce(esum, lt, AX.X, ALU.add))
            step(dve.tensor_scalar(ld, ld, 0.0, None, ALU.is_equal))
            first_of(ld, EXPERTS, ix, e1)
            step(dve.scalar_tensor_tensor(lm, e1, 2 * NEG, lm, ALU.mult, ALU.add))
            step(dve.tensor_reduce(m2, lm, AX.X, ALU.max))
            dve.tensor_tensor(wb, m2, m1, ALU.subtract).then_inc(route_d, 1)
            step(dve.tensor_tensor(ld, lm, widen(m2, 2, EXPERTS), ALU.is_equal))
            first_of(ld, EXPERTS, ix, e2)
            dve.wait_ge(route_e, 3)
            step(dve.reciprocal(wa, esum))
            step(dve.tensor_tensor(wb, wb, wa, ALU.mult))
            step(dve.tensor_tensor(esum, wa, wb, ALU.add))
            step(dve.tensor_tensor(esum, esum, gsum, ALU.mult))
            step(dve.reciprocal(esum, esum))
            step(dve.tensor_tensor(wts[:, 0:NI], wa, esum, ALU.mult))
            step(dve.tensor_tensor(wts[:, NI:2 * NI], wb, esum, ALU.mult))
            step(dve.tensor_tensor(mm, e1, e2, ALU.add))
            step(dve.tensor_tensor(mm, mm, widen(valid, 2, EXPERTS), ALU.mult))
            step(dve.memset(ss[:, 0, :], 0.0))
            for i in range(1, NI):
                step(dve.tensor_tensor(ss[:, i, :], ss[:, i - 1, :], mm[:, i - 1, :], ALU.add))
            dve.tensor_tensor(s_all, ss[:, TILES, :], mm[:, TILES, :], ALU.add).then_inc(member_ready, 1)
            dve.wait_ge(rank_done, 1)
            step(dve.tensor_scalar(nb, banks[5][:, 0:EXPERTS], float(P - 1), None, ALU.add))
            step(dve.tensor_copy(nb_i, nb))
            step(dve.tensor_single_scalar(nb_i, nb_i, 7, ALU.arith_shift_right))
            step(dve.tensor_copy(nb, nb_i))
            step(dve.tensor_tensor_scan(bend, one32, nb, 0.0, ALU.mult, ALU.add))
            step(dve.tensor_tensor(bst, bend, nb, ALU.subtract))
            step(dve.tensor_scalar(bst, bst, float(P), None, ALU.mult))
            step(dve.tensor_tensor(rr, bank6[:, 0:NI * EXPERTS].rearrange("p (i e) -> p i e", i=NI),
                                   widen(bst, 1, NI), ALU.add))
            for a, e in enumerate((e1, e2)):
                step(dve.tensor_tensor(e, e, rr, ALU.mult))
                step(dve.tensor_reduce(dest_f[:, a * NI:(a + 1) * NI], e, AX.X, ALU.add))
            step(dve.tensor_copy(dest_i, dest_f))
            step(dve.tensor_single_scalar(lo_i, dest_i, P - 1, ALU.bitwise_and))
            step(dve.tensor_single_scalar(hi_i, dest_i, 7, ALU.arith_shift_right))
            step(dve.tensor_copy(lo_f, lo_i))
            step(dve.tensor_copy(hi_f, hi_i))
            step(dve.tensor_tensor(oh_lo, widen(iota_r, 1, 2 * NI), widen(lo_f, 2, P), ALU.is_equal))
            step(dve.tensor_tensor(oh_hi, widen(iota_r[:, 0:NBX], 1, 2 * NI), widen(hi_f, 2, NBX), ALU.is_equal))
            step(dve.tensor_tensor(tok_id, tok_id, valid, ALU.mult))
            step(dve.tensor_tensor(oh_hi[:, 0:NI, :], oh_hi[:, 0:NI, :], widen(tok_id, 2, NBX), ALU.mult))
            dve.tensor_tensor(oh_hi[:, NI:2 * NI, :], oh_hi[:, NI:2 * NI, :], widen(tok_id, 2, NBX),
                              ALU.mult).then_inc(onehot_ready, 1)
            step(dve.tensor_tensor(cmp, widen(bend[0:1, :], 1, NBX), widen(iota_r[0:1, 0:NBX], 2, EXPERTS),
                                   ALU.is_le))
            step(dve.tensor_reduce(ef, cmp, AX.X, ALU.add))
            step(dve.tensor_scalar(ef, ef, float(EXPERTS - 1), None, ALU.min))
            step(dve.tensor_copy(plan[:, 0:NBX], ef))
            step(dve.tensor_scalar(ef[:, 0:1], bend[0:1, EXPERTS - 1:EXPERTS], 1.0, None, ALU.add))
            step(dve.tensor_copy(plan[:, NBX:NBX + 1], ef[:, 0:1]))
            step(dve.tensor_single_scalar(plan[:, NBX:NBX + 1], plan[:, NBX:NBX + 1], 1, ALU.arith_shift_right))
            dve.wait_ge(slots_done, 1)
            dve.tensor_copy(tok_of, banks[4][:, 0:NBX]).then_inc(routed, 1)
            dve.wait_ge(routed, 1)

            pairs = dve.value_load(plan[:, NBX:NBX + 1], min_val=1, max_val=BLOCKS // 2)
            dve.memset(yo[0][:, 0:1], 0.0).then_inc(o_free, 1)
            with dve.Fori(0, pairs) as i:
                st.enter(i, 2)
                for b in range(2):
                    n = i * 2 + (b + 1)
                    dve.tensor_copy(idx2[:, b:b + 1], tok_of[:, ds(i * 2 + (b + 2), 1)]).then_inc(idx_ready, 1)
                    dve.wait_ge(up_done, i * 2 + (b + 3))
                    dve.wait_ge(sig_ready, n)
                    dve.tensor_tensor(hm[b], hm[b], banks[1][:, :], ALU.mult).then_inc(h_ready, 1)
                    dve.wait_ge(ht_turned, n)
                    dve.tensor_copy(ht[b], bank6).then_inc(ht_copied, 1)
                    dve.wait_ge(o_done, i * 2 + (b + 3))
                    st.did(dve.tensor_copy(yo[b][:, 0:512], banks[2][:, :]))
                    dve.tensor_copy(yo[b][:, 512:1024], banks[3][:, :]).then_inc(o_free, 1)
                dve.wait_ge(rows_stored[0], i * 16 + 16)
                dve.wait_ge(rows_stored[1], i * 16 + 16)
            dve.wait_ge(finw_landed, 64)
            dve.wait_ge(routed, 1)
            fin = Steps(dve, fin_step)
            for row in (g2_p, g2_s):
                fin.did(dve.tensor_scalar(row, row, 1.0, None, ALU.add))
            for i in range(TILES + 1):
                rows = P if i < TILES else NS
                g2 = g2_p if i < TILES else g2_s
                x = fa[i % 3][0:rows, :]
                dve.wait_ge(fb_landed[i % 3], 16 * (i // 3 + 1))
                dve.wait_ge(f_scaled, i + 1)
                fin.did(dve.scalar_tensor_tensor(x, fb[i % 3][0:rows, :], wts[0:rows, NI + i:NI + i + 1], x,
                                                 ALU.mult, ALU.add))
                fin.settle()
                fin.did(dve.tensor_tensor(x, x, g2, ALU.mult))
                fin.settle()
                fin.did(dve.scalar_tensor_tensor(x, x1[0:rows, i, :], ALPHA, x, ALU.mult, ALU.add))
                fin.settle()
                for half in range(2):
                    fin.did(dve.bn_stats(stats2[0:rows, 6 * half:6 * half + 6], x[:, 512 * half:512 * half + 512]))
                fin.settle()
                dve.bn_aggr(mv2[0:rows, i % 2, 0:2], stats2[0:rows, :]).then_inc(fvar_ready, 1)
                dve.wait_ge(fstd_ready, i + 1)
                fin.did(dve.reciprocal(mv2[0:rows, i % 2, 3:4], mv2[0:rows, i % 2, 2:3]))
                fin.settle()
                fin.did(dve.tensor_scalar(x, x, mv2[0:rows, i % 2, 0:1], mv2[0:rows, i % 2, 3:4],
                                          ALU.subtract, ALU.mult))
                fin.settle()
                fin.did(dve.tensor_tensor(x, x, ffn_g[0:rows, :], ALU.mult))
                fin.settle()
                dve.tensor_tensor(x, x, ffn_b[0:rows, :], ALU.add).then_inc(y_out, 1)

        @block.tensor
        def _(pe):
            pe.wait_ge(consts_ready, 1)
            pe.wait_ge(c_landed, 32)
            for k in range(KD):
                last = pe.transpose(bank6[:, k * MROWS:(k + 1) * MROWS], crow[:, k * P:(k + 1) * P],
                                    ident[0:MROWS, 0:MROWS])
            last.then_inc(ct_turned, 1)
            pe.wait_ge(ct_ready, 1)

            def mod_group(q):
                pe.wait_ge(wada_landed[q % 3], 16 * (q // 3 + 1))
                if q >= 2:
                    pe.wait_ge(mod_added, q - 1)
                for k in range(KD):
                    last = pe.matmul(banks[q % 2][0:MROWS, :], c_t[:, k, :], wada[q % 3][:, k, :],
                                     start=(k == 0), stop=(k == KD - 1))
                last.then_inc(mod_done, 1)

            def turn_x(i):
                rows = P if i < TILES else NS
                pe.wait_ge(x0_ready, i + 1)
                if i >= 2:
                    pe.wait_ge(ut_ready, i - 1)
                for k in range(KD):
                    last = pe.transpose(banks[2 + 2 * (i % 2) + k // 4][:, (k % 4) * P:(k % 4) * P + rows],
                                        xr[i % 4][0:rows, k * P:(k + 1) * P], ident[0:rows, 0:rows])
                last.then_inc(x_turned, 1)

            for q in range(4):
                mod_group(q)
            pe.wait_ge(mod_added, 4)
            for k in range(16):
                last = pe.transpose(bank6[:, k * MROWS:(k + 1) * MROWS], mod[:, k * P:(k + 1) * P],
                                    ident[0:MROWS, 0:MROWS])
            last.then_inc(cols_turned, 1)
            pe.wait_ge(small_landed, 13 * 16)
            pe.wait_ge(cols_copied, 1)
            for k in range(KD):
                last = pe.transpose(bank6[:, k * ROWS_C:(k + 1) * ROWS_C], rows_c[:, k * P:(k + 1) * P],
                                    ident[0:ROWS_C, 0:ROWS_C])
            last.then_inc(cols_turned, 1)
            for half in range(2):
                pe.wait_ge(cols_copied, 2 + half)
                for k in range(16):
                    kk = 16 * half + k
                    last = pe.transpose(bank6[:, k * ROWS_S:(k + 1) * ROWS_S], rows_s[:, kk * P:(kk + 1) * P],
                                        ident[0:ROWS_S, 0:ROWS_S])
                last.then_inc(cols_turned, 1)
            for i in range(TILES):
                turn_x(i)
                mod_group(4 + i)
            turn_x(TILES)

            pe.wait_ge(ut_ready, TILES)
            pe.wait_ge(ut_s_ready, 1)
            for i in range(TILES + 1):
                rows = P if i < TILES else NS
                for k in range(KD):
                    last = pe.matmul(bank7[0:rows, i * HEADS:(i + 1) * HEADS], uT[:, k, i * P:i * P + rows],
                                     w_dt[:, k, :], start=(k == 0), stop=(k == KD - 1))
            last.then_inc(dt_raw, 1)
            pe.wait_ge(dta_ready, 1)
            pe.matmul(bank7[:, 0:256], tri, dta_g, start=True, stop=True)
            pe.matmul(bank7[:, 256:512], ones, dta_g, start=True, stop=True).then_inc(cum_done, 1)
            pe.wait_ge(spread_ready, 1)
            pe.matmul(bank7, ones[0:NS, :], spread, start=True, stop=True).then_inc(spread_done, 1)

            def turn(g, proj, ssd):
                gp = g - 1 if ssd else None

                def sub(s):
                    u, part = s // 3, s % 3
                    if part == 0:
                        pe.wait_ge(w_landed[u], g * 16 + 16)
                    if ssd or s >= 3:
                        pe.wait_ge(raw_ready, g * 18 + (s - 2))
                    for k in range(KD):
                        last = pe.matmul(banks[part][:, 0:SUB], wslot[u][:, k, :],
                                         uT[:, k, part * SUB:(part + 1) * SUB], start=(k == 0), stop=(k == KD - 1))
                    last.then_inc(proj_done, 1)

                def tails():
                    pe.wait_ge(raw_ready, gp * 18 + 18)
                    for u in range(4):
                        last = pe.transpose(bank6[0:11, u * P:(u + 1) * P], raw[u][:, SEQ - 3:TOK], ident)
                    last.then_inc(tails_done, 1)

                def scores(c):
                    at = slice(c * P, (c + 1) * P)
                    if c == 0:
                        pe.wait_ge(silu_done, gp * 4 + 4)
                    pe.wait_ge(rh_ready, gp * 8 + (c + 1))
                    pe.matmul(banks[4][:, :], ones, rhs_cum, start=True, stop=True).then_inc(cum_ready, 1)
                    pe.transpose(banks[3][:, 0:128], proc[0][:, at], ident)
                    pe.transpose(banks[3][:, 128:256], proc[1][:, at], ident)
                    pe.transpose(banks[3][:, 256:384], proc[2][:, at], ident)
                    pe.matmul(banks[3][:, 384:512], proc[2][:, at], proc[3][:, at], start=True,
                              stop=True).then_inc(scores_ready, 1)

                def outputs(c):
                    pe.wait_ge(ops_ready, gp * 8 + (c + 1))
                    pe.matmul(banks[5][:, 256:512], b_tok, xw, start=True, stop=True)
                    for r in range(HPG):
                        out = banks[5][HD * (r % 2):HD * (r % 2) + HD, (r // 2) * P:(r // 2 + 1) * P]
                        last = pe.matmul(out, xdt[:, r * HD:(r + 1) * HD], segm[:, r * P:(r + 1) * P], start=True,
                                         stop=(c == 0))
                        if c:
                            last = pe.matmul(out, h_t[:, r * HD:(r + 1) * HD], csc[:, r * P:(r + 1) * P],
                                             start=False, stop=True)
                    last.then_inc(y_ready, 1)

                def rms(c):
                    w = P if c < 8 else NS
                    if c == 0:
                        pe.wait_ge(sc_used, gp + 1)
                    pe.wait_ge(sq_ready, gp * 9 + (c + 1))
                    for j in range(2):
                        last = pe.matmul(bank7[:, 0:w], ones_avg, sq[:, j, 0:w], start=(j == 0), stop=(j == 1))
                    last.then_inc(rms_ready, 1)

                def spread_rows(diag_ready, done):
                    pe.wait_ge(diag_ready, gp + 1)
                    for h in range(2):
                        last = pe.matmul(pair[:, 512 * h:512 * h + 512], ones, diag_f[:, 512 * h:512 * h + 512],
                                         start=True, stop=True)
                    last.then_inc(done, 1)

                for s in range(18):
                    if proj:
                        sub(s)
                    if not ssd:
                        continue
                    if s == 0:
                        tails()
                    if s == 3:
                        scores(0)
                    if s == 4:
                        pe.wait_ge(tail_copied, gp + 1)
                        spread_rows(diag_b_ready, sb_ready)
                    if s == 5:
                        pe.wait_ge(sb_used, gp + 1)
                        spread_rows(diag_c_ready, sc_ready)
                    if 6 <= s <= LAST_S2:
                        c = s - 6
                        outputs(c)
                        if c < 7:
                            scores(c + 1)
                        if c:
                            rms(c - 1)
                    if s == 14:
                        rms(7)
                        for j in range(2):
                            last = pe.transpose(bank6[:, j * P:(j + 1) * P], h_t[:, j * P:(j + 1) * P], ident)
                        last.then_inc(ht_ready, 1)
                    if s == 15:
                        rms(8)
                if ssd:
                    pe.wait_ge(pstate_copied, gp + 1)
                    pe.wait_ge(rs_ready, gp * 9 + 9)

            turn(0, True, False)
            with pe.Fori(0, GROUPS - 1) as i:
                turn(i + 1, True, True)
            turn(GROUPS, False, True)
            pe.wait_ge(normed, 72)
            pe.wait_ge(raw_ready, 144)

            def merge(i, first, before, loads, ks, src, gate_sem, gate_free, out_sem, out_free):
                for h in range(2):
                    pe.wait_ge(w_landed[3 * h], i * 16 + (loads[0] + 16))
                    for part in range(3):
                        n = 3 * h + part
                        if not (first and h == 0):
                            pe.wait_ge(gate_free, i * 6 + (n - 2))
                        for k in range(KD):
                            last = pe.matmul(banks[part][:, 0:SUB], wslot[3 * h][:, k, :],
                                             uT[:, k, part * SUB:(part + 1) * SUB], start=(k == 0),
                                             stop=(k == KD - 1))
                        last.then_inc(gate_sem, 1)
                    for x in range(1, ks // KD + 1):
                        pe.wait_ge(w_landed[3 * h + x], i * 16 + (loads[x] + 16))
                    for part in range(3):
                        n = 3 * h + part
                        if not (first and h == 0):
                            pe.wait_ge(out_free, i * 6 + (n - 2))
                        for k in range(ks):
                            last = pe.matmul(banks[3 + part][:, 0:SUB], wslot[3 * h + 1 + k // KD][:, k % KD, :],
                                             src[:, k, part * SUB:(part + 1) * SUB], start=(k == 0),
                                             stop=(k == ks - 1))
                        last.then_inc(out_sem, 1)

            args_b = (None, (128, 128, 128), 2 * KD, ybT, gb_done, gsig_ready, yb_done, merged_b)
            merge(0, True, *args_b)
            with pe.Fori(0, 3) as i:
                merge(i + 1, False, *args_b)
            pe.wait_ge(merged_b, 24)

            def short(i, first):
                for h in range(2):
                    for x in range(3):
                        v = 3 * h + x
                        pe.wait_ge(w_landed[v], i * 16 + (192 + 16))
                        for part in range(3):
                            n = 3 * h + part + 1
                            if x == 2:
                                pe.wait_ge(sc_copied, i * 6 + n)
                            elif not (first and h == 0):
                                pe.wait_ge(p_made if x == 0 else sb_copied, i * 6 + (n - 3))
                            for k in range(KD):
                                last = pe.matmul(banks[3 * (v % 2) + part][:, 0:SUB], wslot[v][:, k, :],
                                                 uT[:, k, part * SUB:(part + 1) * SUB], start=(k == 0),
                                                 stop=(k == KD - 1))
                            last.then_inc(short_done, 1)
                    pe.wait_ge(p_made, i * 6 + (3 * h + 3))
                    if not (first and h == 0):
                        pe.wait_ge(tail2_copied, i * 2 + h)
                    pe.transpose(bank6[0:10, h * P:(h + 1) * P], pt[h][:, SEQ - 2:TOK], ident).then_inc(tail2_done, 1)

            short(0, True)
            with pe.Fori(0, 3) as i:
                short(i + 1, False)
            pe.wait_ge(ya_ready, 8)
            args_a = (None, (256, 256), KD, yaT, ga_done, gsig2_ready, ya_done, merged_a)
            pe.wait_ge(sb_copied, 24)
            merge(0, True, *args_a)
            with pe.Fori(0, 3) as i:
                merge(i + 1, False, *args_a)

            pe.wait_ge(merged_a, 24)
            pe.wait_ge(wo_landed, 16)

            def turn_u2(i):
                rows = P if i < TILES else NS
                pe.wait_ge(u2_ready, i + 1)
                if i:
                    pe.wait_ge(u2t_ready, i)
                for k in range(KD):
                    last = pe.transpose(banks[4 + k // 4][:, (k % 4) * P:(k % 4) * P + rows],
                                        u2[i % 2][0:rows, k * P:(k + 1) * P], ident[0:rows, 0:rows])
                last.then_inc(u2_turned, 1)

            def logits(i):
                rows = P if i < TILES else NS
                pe.wait_ge(u2t_ready, i + 1)
                if i == 0:
                    pe.wait_ge(mixw_landed, 12 * 16)
                for k in range(KD):
                    last = pe.matmul(bank7[0:rows, i * 36:(i + 1) * 36], u2t[i % 2][:, k * P:k * P + rows],
                                     w_r[:, k, :], start=(k == 0), stop=(k == KD - 1))
                if i == TILES:
                    last.then_inc(logits_done, 1)

            for i in range(TILES + 1):
                rows = P if i < TILES else NS
                if i >= 2:
                    pe.wait_ge(x0_used, i - 1)
                for half in range(2):
                    for k in range(KD):
                        last = pe.matmul(banks[2 * (i % 2) + half][0:rows, :], merged[:, k, i * P:i * P + rows],
                                         w_o[:, k, 512 * half:512 * half + 512], start=(k == 0), stop=(k == KD - 1))
                last.then_inc(wo_done, 1)
                if i >= 2:
                    logits(i - 2)
                if i >= 1:
                    turn_u2(i - 1)
            logits(TILES - 1)
            turn_u2(TILES)
            logits(TILES)

            pe.wait_ge(member_ready, 1)
            flat = dict(i=NI)
            pe.matmul(bank6[:, 0:NI * EXPERTS], stri, mm.rearrange("p i e -> p (i e)", **flat), start=True, stop=False)
            pe.matmul(bank6[:, 0:NI * EXPERTS], ones, ss.rearrange("p i e -> p (i e)", **flat), start=False, stop=True)
            pe.matmul(banks[5][:, 0:EXPERTS], ones, s_all, start=True, stop=True).then_inc(rank_done, 1)
            pe.wait_ge(onehot_ready, 1)
            primes = {0: up_done, 1: up_done, 2: o_done, 3: o_done, 2 * NI - 1: slots_done}
            for a in range(2 * NI):
                last = pe.matmul(banks[4][:, 0:NBX], oh_lo[:, a, :], oh_hi[:, a, :], start=(a == 0),
                                 stop=(a == 2 * NI - 1))
                if a in primes:
                    last.then_inc(primes[a], 1)

            def turn_rows(b, landed):
                pe.wait_ge(xg_landed[b], landed)
                for k in range(KD):
                    last = pe.transpose(banks[4 + k // 4][:, (k % 4) * P:(k % 4 + 1) * P], xg[b][:, k * P:(k + 1) * P],
                                        ident)
                last.then_inc(xg_turned, 1)

            pe.wait_ge(routed, 1)
            pairs = pe.value_load(plan[:, NBX:NBX + 1], min_val=1, max_val=BLOCKS // 2)
            turn_rows(0, 16)
            with pe.Fori(0, pairs) as i:
                for b in range(2):
                    n = i * 2 + (b + 1)
                    pe.wait_ge(xt_ready, n)
                    pe.wait_ge(w13_landed[b], i * 16 + 16)
                    for half, done in ((0, gate_done), (1, up_done)):
                        for k in range(KD):
                            last = pe.matmul(banks[half][:, :], xt[b][:, k * P:(k + 1) * P],
                                             w13[b][:, k, D_EXP * half:D_EXP * half + D_EXP], start=(k == 0),
                                             stop=(k == KD - 1))
                        last.then_inc(done, 1)
                    turn_rows(1 - b, i * 16 + (16 if b == 0 else 32))
                    pe.wait_ge(h_ready, n)
                    for k in range(4):
                        last = pe.transpose(bank6[:, k * P:(k + 1) * P], hm[b][:, k * P:(k + 1) * P], ident)
                    last.then_inc(ht_turned, 1)
                    pe.wait_ge(ht_copied, n)
                    pe.wait_ge(w2_landed[b], i * 16 + 16)
                    pe.wait_ge(o_free, n)
                    for half in range(2):
                        for k in range(4):
                            last = pe.matmul(banks[2 + half][:, :], ht[b][:, k * P:(k + 1) * P],
                                             w2[b][:, k, 512 * half:512 * half + 512], start=(k == 0), stop=(k == 3))
                    last.then_inc(o_done, 1)


_INS = ["x_prompt", "x_sample", "state_ssm", "state_ssm_conv", "state_sc_conv", "c_prompt", "c_sample", "ln_in_g",
        "ln_in_b", "w_ada", "b_ada", "w_in", "conv_sc_w", "w_sc_out", "conv_ssm_w", "conv_ssm_b", "dt_bias", "a_log",
        "d_skip", "ssm_norm_g", "w_ssm_out", "w_o", "ln_mix_g", "ln_mix_b", "w_route_g", "b_route_g", "w_route_e",
        "b_route_e", "w_moe_13", "w_moe_2", "ln_ffn_g", "ln_ffn_b"]
_OUTS = [(1, SEQ, D), (NS, 1, D), (1, 1, HEADS, HD, N), (1, 1, 3, CONV_DIM), (1, 1, 2, D), (1, NS, HEADS, HD, N),
         (1, NS, 3, CONV_DIM), (1, NS, 2, D)]


def kernel(**inputs):
    import numpy as _np
    import concourse.bacc as _bacc
    from concourse.bass_utils import run_bass_kernel_spmd as _run

    nc = _bacc.Bacc("TRN2", target_bir_lowering=False, num_devices=1)
    arrays, args, outs = {}, {}, []
    for name in _INS:
        a = _np.ascontiguousarray(inputs[name])
        arrays[f"in_{name}_dram"] = a
        args[name] = nc.dram_tensor(f"in_{name}_dram", a.shape, mybir.dt.from_np(a.dtype), kind="ExternalInput").ap()
    for i, shape in enumerate(_OUTS):
        outs.append(nc.dram_tensor(f"out_{i}_dram", shape, F32, kind="ExternalOutput").ap())
    build(nc, args, outs)
    r = _run(nc, [arrays], core_ids=[0])
    return tuple(r.results[0][f"out_{i}_dram"] for i in range(len(_OUTS)))
```

```python
from contextlib import ExitStack

import concourse.bass as bass
from concourse import mybir

F32 = mybir.dt.float32
F32R = mybir.dt.float32r
I32 = mybir.dt.int32
ALU = mybir.AluOpType
ACT = mybir.ActivationFunctionType
AX = mybir.AxisListType
ds = bass.ds

P = 128
D = 1024
KD = D // P
SEQ = 1024
NS = 8
TOK = SEQ + NS
TILES = SEQ // P
SUB = TOK // 3
D_INNER = 2 * D
GROUPS = 8
HEADS = 32
HPG = HEADS // GROUPS
HD = 64
N = 128
CHUNKS = SEQ // P
CONV_DIM = D_INNER + 2 * GROUPS * N
NEG = -1.0e30
EPS = 1e-5
ALPHA = 2.0 ** 0.25
COL_SB, COL_SC, COL_SH = 0, D, 2 * D
COL_Z = 3 * D
COL_X = COL_Z + D_INNER
COL_B = COL_X + D_INNER
COL_C = COL_B + GROUPS * N
COL_DT = COL_C + GROUPS * N
COL_GA = COL_DT + HEADS
COL_GB = COL_GA + D
EXPERTS, EGROUPS, PER_GROUP, D_EXP = 32, 4, 8, 512
BLOCKS = 48
ROWS_S = 29
ROWS_C = 21
MODW = 6 * D
MROWS = NS + 1


class Steps:

    def __init__(self, eng, sem):
        self.eng, self.sem, self.n, self.turn, self.per = eng, sem, 0, None, 0

    def did(self, ins):
        ins.then_inc(self.sem, 1)
        self.n += 1

    def settle(self):
        if self.turn is None:
            self.eng.wait_ge(self.sem, self.n)
        else:
            self.eng.wait_ge(self.sem, self.turn * self.per + self.n)

    def enter(self, turn, per):
        self.turn, self.per, self.start = turn, per, self.n

    def leave(self, turns):
        assert self.n - self.start == self.per, f"steps per turn: {self.n - self.start}"
        self.n = self.start + turns * self.per
        self.turn = None


def widen(ap, axis, count):
    v = ap.unsqueeze(axis)
    shape = list(v.shape)
    shape[axis] = count
    return v.to_broadcast(shape)


def build(nc, t, o):
    (y_prompt, y_sample, p_ssm, p_ssm_conv, p_sc_conv, s_ssm, s_ssm_conv, s_sc_conv) = o
    ctx = ExitStack()
    with ctx:
        def sem(name):
            return ctx.enter_context(nc.semaphore(name))

        ARENA = 53200 - KD * TOK - 8
        one = ctx.enter_context(nc.sbuf_tensor("one", [P, 8], F32))
        u_whole = ctx.enter_context(nc.sbuf_tensor("u_whole", [P, KD * TOK], F32))
        with nc.sbuf_tensor("arena", [P, ARENA], F32) as whole:
            arena = whole
        W0 = 2 * KD * TOK
        HI0 = W0 + 7 * D + TOK
        ctx.enter_context(nc.sbuf_tensor("below_w_whole", [P, W0], F32))
        w_whole = ctx.enter_context(nc.sbuf_tensor("w_whole", [P, 3 * D], F32))
        w_parts = ctx.enter_context(nc.sbuf_tensor("w_parts", [P, 4 * D], F32R))
        ctx.enter_context(nc.sbuf_tensor("below_u_parts", [P, TOK], F32))
        u_parts = ctx.enter_context(nc.sbuf_tensor("u_parts", [P, 2 * KD * TOK], F32R))
        K0 = ARENA - 3312
        banks = [ctx.enter_context(nc.psum_tensor(f"bank{i}", [P, 512], F32)) for i in range(6)]
        pair = ctx.enter_context(nc.psum_tensor("bank67", [P, 1024], F32))
        bank6, bank7 = pair[:, 0:512], pair[:, 512:1024]
        x0_dram = nc.dram_tensor("x0_dram", (TOK, D), F32, kind="Internal").ap()
        mod_dram = nc.dram_tensor("mod_dram", (MROWS, MODW), F32, kind="Internal").ap()
        cum_dram = nc.dram_tensor("cum_dram", (GROUPS * CHUNKS * HPG * P,), F32, kind="Internal").ap()
        u2_dram = nc.dram_tensor("u2_dram", (TOK, D), F32, kind="Internal").ap()
        rows_dram = nc.dram_tensor("rows_dram", (BLOCKS * P, D), F32, kind="Internal").ap()

        class Room:

            def __init__(self, start, end):
                self.at, self.end = start, end

            def take(self, n):
                assert self.at + n <= self.end, f"over by {self.at + n - self.end}"
                self.at += n
                return arena[:, self.at - n:self.at]

        Y0 = 0
        assert W0 == Y0 + 2 * KD * TOK
        S0 = W0 + 6 * KD * P
        uT = u_whole[:, :].rearrange("p (k t) -> p k t", k=KD)
        ybT_f = arena[:, Y0:W0]
        ybT = ybT_f.rearrange("p (k t) -> p k t", k=2 * KD)
        wslot = [arena[:, W0 + u * D:W0 + (u + 1) * D].rearrange("p (k c) -> p k c", k=KD) for u in range(7)]

        keep = Room(K0, ARENA)
        ident = keep.take(P)
        tri = keep.take(P)
        stri = keep.take(P)
        ones = keep.take(P)
        ones_avg = keep.take(P)
        epsc = keep.take(1)
        convw_f = keep.take(32 * 5)
        convst_f = keep.take(32 * 24)
        colc_f = keep.take(KD * ROWS_C)
        colc = colc_f.rearrange("p (k r) -> p k r", k=KD)
        normg = keep.take(16)
        dskip = keep.take(16)
        dt_g = keep.take(GROUPS * CHUNKS * HPG)
        cum_t = keep.take(GROUPS * CHUNKS * HPG)
        wend = keep.take(GROUPS * CHUNKS * HPG)
        decay = keep.take(GROUPS * CHUNKS * HPG)
        dta_g = keep.take(GROUPS * CHUNKS * HPG)
        dt_s = keep.take(16 * NS)
        dec_s = keep.take(16 * NS)
        stats2 = cum_t[:, 0:12]
        mv2 = cum_t[:, 16:24].rearrange("p (x a) -> p x a", x=2)

        r0 = Room(Y0, W0)
        wada = [r0.take(KD * 512).rearrange("p (k c) -> p k c", k=KD) for _ in range(3)]
        xr = [r0.take(D) for _ in range(4)]
        bada = arena[0:MROWS, W0:W0 + MODW]
        r0 = Room(S0, K0)
        mod = r0.take(MODW)[0:MROWS]
        rows_s = r0.take(CONV_DIM)[0:ROWS_S]
        rows_c = r0.take(D)[0:ROWS_C]
        crow = r0.take(D)[0:MROWS]
        ln_g = r0.take(D)
        ln_b = r0.take(D)
        mod_t = r0.take(16 * MROWS).rearrange("p (k m) -> p k m", k=16)
        c_t = r0.take(KD * MROWS).rearrange("p (k m) -> p k m", k=KD)
        w_dt = r0.take(KD * HEADS).rearrange("p (k h) -> p k h", k=KD)
        dtb = r0.take(HEADS)
        alog = r0.take(HEADS)
        dskb = r0.take(HEADS)
        stats = r0.take(4 * 12).rearrange("p (x a) -> p x a", x=4)
        mv = r0.take(4 * 4).rearrange("p (x a) -> p x a", x=4)
        DTW = (TILES + 1) * HEADS
        dtr = ln_g[:, 0:DTW]
        dte = ln_g[:, DTW:2 * DTW]
        dtw = ln_g[:, 2 * DTW:3 * DTW]
        dtl = ln_b[:, 0:DTW]
        dtq = ln_b[:, DTW:2 * DTW]
        dtm = ln_b[:, 2 * DTW:3 * DTW]
        D0 = S0 + 6 * TOK
        cend = arena[:, D0:D0 + 256]
        spread = arena[0:NS, D0 + 256:D0 + 256 + 512]
        das = arena[0:NS, D0 + 768:D0 + 800]

        r1 = Room(S0, K0)
        raw_f = r1.take(6 * TOK)
        raw = [raw_f[:, u * TOK:(u + 1) * TOK] for u in range(6)]
        z2 = raw_f[:, 4 * TOK:6 * TOK].rearrange("p (j t) -> p j t", j=2)
        proc_f = r1.take(4 * TOK)
        proc = [proc_f[:, u * TOK:(u + 1) * TOK] for u in range(4)]
        xs2 = proc_f[:, 0:2 * TOK].rearrange("p (j t) -> p j t", j=2)
        hs = r1.take(NS * 2 * N).rearrange("p (b j n) -> p b j n", b=NS, j=2)
        tmp = r1.take(NS * N).rearrange("p (b n) -> p b n", b=NS)
        diag_f = r1.take(NS * N)
        diag = diag_f.rearrange("p (b n) -> p b n", b=NS)
        pstate = diag_f[:, 0:2 * N]
        cumb = [r1.take(4 * P)]
        csc = r1.take(4 * P)
        segm = r1.take(4 * P)
        cumb.append(r1.take(4 * P))
        cum_rows = segm[:, 0:2 * P]
        xdt = r1.take(HPG * HD)
        xw = r1.take(HPG * HD)
        b_tok = r1.take(N)
        cb_m = r1.take(P)
        h_t = r1.take(HPG * HD)
        ybuf = [r1.take(2 * P).rearrange("p (j t) -> p j t", j=2) for _ in range(2)]
        sq = r1.take(2 * P).rearrange("p (j t) -> p j t", j=2)
        rs = r1.take(P)
        ys = r1.take(2 * NS).rearrange("p (j b) -> p j b", j=2)
        dtx = r1.take(2 * NS).rearrange("p (j b) -> p j b", j=2)
        tail = r1.take(4 * P)[0:11]

        u_hi = u_parts[:, 0:KD * TOK].rearrange("p (k t) -> p k t", k=KD)
        u_lo = u_parts[:, KD * TOK:2 * KD * TOK].rearrange("p (k t) -> p k t", k=KD)
        w_all = [w_whole[:, x * D:(x + 1) * D].rearrange("p (k c) -> p k c", k=KD) for x in range(3)]
        w_hi = [w_parts[:, 2 * D * v:2 * D * v + D].rearrange("p (k c) -> p k c", k=KD) for v in range(2)]
        w_lo = [w_parts[:, 2 * D * v + D:2 * D * v + 2 * D].rearrange("p (k c) -> p k c", k=KD) for v in range(2)]
        merged_f = u_whole[:, :]
        merged = merged_f.rearrange("p (k t) -> p k t", k=KD)
        gsb = arena[:, W0 + 7 * D:HI0]
        r2 = Room(Y0 + KD * TOK, W0)
        scb = [r2.take(TOK) for _ in range(2)]
        pt = [r2.take(TOK) for _ in range(2)]
        sbb = [r2.take(TOK) for _ in range(2)]
        acc = r2.take(TOK)
        tail_sc = r2.take(D)[0:10]
        ya_f = ybT_f[:, 0:KD * TOK]
        yaT = ya_f.rearrange("p (k t) -> p k t", k=KD)

        X1 = W0 + 7 * D
        X1_END = X1 + (TILES + 1) * D
        x1 = arena[:, X1:X1_END].rearrange("p (i d) -> p i d", i=TILES + 1)
        w_o = ybT_f[:, KD * TOK:KD * TOK + KD * D].rearrange("p (k c) -> p k c", k=KD)
        r3 = Room(X1_END, K0)
        g1_p, mix_g, mix_b, sc2_p, sh2_p = (r3.take(D) for _ in range(5))
        g1_s, sc2_s, sh2_s = (r3.take(D)[0:NS] for _ in range(3))
        w_r = r3.take(KD * 36).rearrange("p (k e) -> p k e", k=KD)
        b_r = r3.take(36)
        wflat = [arena[:, W0 + u * D:W0 + (u + 1) * D] for u in range(7)]
        x0b = [wflat[5], wflat[6]]
        u2 = [wflat[0], wflat[1]]
        u2t = [wflat[2], wflat[3]]

        r4 = Room(Y0, W0)
        NI = TILES + 1
        logit = r4.take(NI * 36).rearrange("p (i e) -> p i e", i=NI)
        iota_r = r4.take(P)
        tok_id = r4.take(NI)
        valid = r4.take(NI)
        grp = r4.take(NI * 4).rearrange("p (i e) -> p i e", i=NI)
        grp_d = r4.take(NI * 4).rearrange("p (i e) -> p i e", i=NI)
        grp_t = r4.take(NI * 4).rearrange("p (i e) -> p i e", i=NI)
        lm, ld, lt, e1, e2, mm, ss, rr = (r4.take(NI * EXPERTS).rearrange("p (i e) -> p i e", i=NI) for _ in range(8))
        s_all = r4.take(EXPERTS)
        gmx, gix, gsum, m1, m2, ix, esum, wa, wb = (r4.take(NI) for _ in range(9))
        cnt, nb, bend, bst, one32 = (r4.take(EXPERTS) for _ in range(5))
        nb_i = r4.take(EXPERTS).bitcast(I32)
        dest_f, lo_f, hi_f = (r4.take(2 * NI) for _ in range(3))
        lo_i, hi_i = (r4.take(2 * NI).bitcast(I32) for _ in range(2))
        NBX = BLOCKS + 2
        oh_lo = r4.take(2 * NI * P).rearrange("p (a c) -> p a c", c=P)
        oh_hi = r4.take(2 * NI * NBX).rearrange("p (a b) -> p a b", b=NBX)
        cmp = r4.take(NBX * EXPERTS)[0:1].rearrange("p (b e) -> p b e", e=EXPERTS)
        ef = r4.take(NBX)[0:1]

        r5 = Room(Y0, X1)
        w13 = [w.rearrange("p (k c) -> p k c", k=KD)
               for w in (u_whole[:, 0:KD * 2 * D_EXP], r5.take(KD * 2 * D_EXP))]
        w2 = [r5.take(4 * D).rearrange("p (k c) -> p k c", k=4) for _ in range(2)]
        xg = [r5.take(D) for _ in range(2)]
        xt = [r5.take(D) for _ in range(2)]
        hm = [r5.take(D_EXP) for _ in range(2)]
        ht = [r5.take(D_EXP) for _ in range(2)]
        r5 = Room(X1_END, K0)
        yo = [r5.take(D) for _ in range(2)]
        g2_p, ffn_g, ffn_b = (r5.take(D) for _ in range(3))
        g2_s = r5.take(D)[0:NS]
        dest_i = r5.take(2 * NI).bitcast(I32)
        wts = r5.take(2 * NI)
        tok_of = r5.take(NBX).bitcast(I32)
        plan = r5.take(NBX + 1)[0:1].bitcast(I32)
        idx2 = r5.take(2).bitcast(I32)
        spare = r5.take(1)

        fa = [u_whole[:, x * D:(x + 1) * D] for x in range(3)]
        fb = [u_whole[:, x * D:(x + 1) * D] for x in range(3, 6)]

        c_landed, small_landed = sem("c_landed"), sem("small_landed")
        wada_landed = [sem(f"wada_landed{i}") for i in range(3)]
        x_landed = [sem(f"x_landed{i}") for i in range(4)]
        consts_ready = sem("consts_ready")
        pool_step, dve_step, act_step = sem("pool_step"), sem("dve_step"), sem("act_step")
        ct_turned, ct_ready = sem("ct_turned"), sem("ct_ready")
        mod_done, mod_added, mod_stored = sem("mod_done"), sem("mod_added"), sem("mod_stored")
        cols_turned, cols_copied = sem("cols_turned"), sem("cols_copied")
        var_ready, std_ready = sem("var_ready"), sem("std_ready")
        x0_ready = sem("x0_ready")
        x0_stored = [sem(f"x0_stored{i}") for i in range(4)]
        x_turned, ut_ready, ut_s_ready = sem("x_turned"), sem("ut_ready"), sem("ut_s_ready")
        dt_raw, dt_in, dt_exp, dt_sum, dt_ln, dta_ready = (sem("dt_raw"), sem("dt_in"), sem("dt_exp"), sem("dt_sum"),
                                                         sem("dt_ln"), sem("dta_ready"))
        filled, cum_done, wend_ready = sem("filled"), sem("cum_done"), sem("wend_ready")
        spread_ready, spread_done, dt_ready = sem("spread_ready"), sem("spread_done"), sem("dt_ready")
        w_landed = [sem(f"w_landed{u}") for u in range(7)]
        proj_done, raw_ready, tails_done, tail_copied, tail_stored = (
            sem("proj_done"), sem("raw_ready"), sem("tails_done"), sem("tail_copied"), sem("tail_stored"))
        conv_done, silu_done, zsilu_done = sem("conv_done"), sem("silu_done"), sem("zsilu_done")
        cum_stored, scores_ready = sem("cum_stored"), sem("scores_ready")
        cum_landed = [sem(f"cum_landed{i}") for i in range(2)]
        ecum_ready, seg_ready, e_ready = (sem("ecum_ready"), sem("seg_ready"),
                                                      sem("e_ready"))
        ops_ready, y_ready, y_gated, sq_ready = sem("ops_ready"), sem("y_ready"), sem("y_gated"), sem("sq_ready")
        rms_ready, rs_ready, normed = sem("rms_ready"), sem("rs_ready"), sem("normed")
        diag_b_ready, diag_c_ready, sb_ready, sc_ready = (sem("diag_b_ready"), sem("diag_c_ready"), sem("sb_ready"),
                                                          sem("sc_ready"))
        sb_used, sc_used, hs_ready, hs_stored, h0_landed = (sem("sb_used"), sem("sc_used"), sem("hs_ready"),
                                                            sem("hs_stored"), sem("h0_landed"))
        ht_ready, pstate_copied, pstate_stored = sem("ht_ready"), sem("pstate_copied"), sem("pstate_stored")
        act_ln, fin_step = sem("act_ln"), sem("fin_step")

        gb_done, gsig_ready, yb_done, merged_b = sem("gb_done"), sem("gsig_ready"), sem("yb_done"), sem("merged_b")
        ga_done, gsig2_ready, ya_done, merged_a = sem("ga_done"), sem("gsig2_ready"), sem("ya_done"), sem("merged_a")
        short_done, sc_copied, p_made, sb_copied = sem("short_done"), sem("sc_copied"), sem("p_made"), sem("sb_copied")
        ya_ready, tail2_done, tail2_copied, tail2_stored = (sem("ya_ready"), sem("tail2_done"), sem("tail2_copied"),
                                                            sem("tail2_stored"))
        mixw_landed, wo_landed = sem("mixw_landed"), sem("wo_landed")
        x0_landed = [sem(f"x0_landed{i}") for i in range(2)]
        wo_done, mvar_ready, mstd_ready, x0_used = sem("wo_done"), sem("mvar_ready"), sem("mstd_ready"), sem("x0_used")
        u2_ready, u2_turned, u2t_ready, logits_done = (sem("u2_ready"), sem("u2_turned"), sem("u2t_ready"),
                                                       sem("logits_done"))
        u2_stored = [sem(f"u2_stored{i}") for i in range(2)]
        iotas_ready, route_d, route_e, member_ready = (sem("iotas_ready"), sem("route_d"), sem("route_e"),
                                                       sem("member_ready"))
        rank_done, onehot_ready, slots_done, routed = sem("rank_done"), sem("onehot_ready"), sem("slots_done"), sem("routed")
        finw_landed = sem("finw_landed")
        w13_landed = [sem(f"w13_landed{i}") for i in range(2)]
        w2_landed = [sem(f"w2_landed{i}") for i in range(2)]
        xg_landed = [sem(f"xg_landed{i}") for i in range(2)]
        idx_ready = sem("idx_ready")
        xg_turned, xt_ready, gate_done, up_done = sem("xg_turned"), sem("xt_ready"), sem("gate_done"), sem("up_done")
        sig_ready, h_ready, ht_turned, ht_copied = sem("sig_ready"), sem("h_ready"), sem("ht_turned"), sem("ht_copied")
        o_done, o_free = sem("o_done"), sem("o_free")
        rows_stored = [sem(f"rows_stored{i}") for i in range(2)]
        fin_landed = [sem(f"fin_landed{i}") for i in range(3)]
        u_hi_ready, u_lo_ready, split_ready = sem("u_hi_ready"), sem("u_lo_ready"), sem("split_ready")
        fvar_ready, fstd_ready, f_scaled, y_out = sem("fvar_ready"), sem("fstd_ready"), sem("f_scaled"), sem("y_out")
        y_stored = [sem(f"y_stored{i}") for i in range(3)]
        carried = sem("carried")

        w_in_v = t["w_in"][0].rearrange("(k p) c -> p k c", p=P)
        w_ada_v = t["w_ada"][0].rearrange("(k p) c -> p k c", p=P)
        LAST_S2 = 13
        LEAST = 2 * ((2 * TOK // P + 1 + 1) // 2)

        def group_cols(g):
            return [COL_X + g * 256, COL_X + g * 256 + P, COL_B + g * N, COL_C + g * N,
                    COL_Z + g * 256, COL_Z + g * 256 + P]

        def state_rows(ap, pair_of_heads):
            return ap[0].rearrange("b (j h) p n -> (h p) b j n", h=2)[:, :, ds(pair_of_heads, 1), :]

        def chunk_sums(q):
            return cum_dram[ds(q * (HPG * P), HPG * P)].partition_broadcast(P)

        def tile_rows(ap, i):
            return ap[i * P:(i + 1) * P, :] if i < TILES else ap[SEQ:TOK, :]

        block = ctx.enter_context(nc.Block())

        @block.sync
        def _(sp):
            def load_x(i):
                if i >= 4:
                    sp.wait_ge(x0_stored[i % 4], 16 * (i // 4))
                    sp.wait_ge(x_turned, i - 3)
                src = t["x_prompt"][0, i * P:(i + 1) * P, :] if i < TILES else t["x_sample"].rearrange("b l d -> (b l) d")
                sp.dma_start(xr[i % 4][0:src.shape[0], :], src).then_inc(x_landed[i % 4], 16)

            def load_wada(q):
                if q >= 3:
                    sp.wait_ge(mod_done, q - 2)
                sp.dma_start(wada[q % 3], w_ada_v[:, :, q * 512:(q + 1) * 512]).then_inc(wada_landed[q % 3], 16)

            sp.dma_start(crow[0:NS, :], t["c_sample"]).then_inc(c_landed, 16)
            sp.dma_start(crow[NS:MROWS, :], t["c_prompt"]).then_inc(c_landed, 16)
            for i in range(2):
                load_x(i)
            load_wada(0)
            small = [(ln_g, t["ln_in_g"].partition_broadcast(P)), (ln_b, t["ln_in_b"].partition_broadcast(P)),
                     (bada, t["b_ada"][0].partition_broadcast(MROWS)),
                     (rows_c[0:3, :], t["conv_sc_w"][0]),
                     (rows_c[3:19, :], t["state_sc_conv"][0].rearrange("b r d -> (b r) d")),
                     (rows_c[19:21, :], t["ssm_norm_g"][0].rearrange("(r d) -> r d", r=2)),
                     (rows_s[0:4, :], t["conv_ssm_w"][0]), (rows_s[4:5, :], t["conv_ssm_b"]),
                     (rows_s[5:29, :], t["state_ssm_conv"][0].rearrange("b r d -> (b r) d")),
                     (dtb, t["dt_bias"][0].partition_broadcast(P)), (alog, t["a_log"][0].partition_broadcast(P)),
                     (dskb, t["d_skip"][0].partition_broadcast(P)), (w_dt, w_in_v[:, :, COL_DT:COL_DT + HEADS])]
            for dst, src in small:
                sp.dma_start(dst, src).then_inc(small_landed, 16)
            load_wada(1)
            load_x(2)
            load_wada(2)
            load_x(3)
            for q in range(3, 12):
                load_wada(q)
                if 1 <= q - 3 <= 5:
                    load_x(q)
            sp.dma_start(s_ssm_conv[0, :, 0:2, :], t["state_ssm_conv"][0, :, 1:3, :]).then_inc(tail2_stored, 16)
            sp.dma_start(s_sc_conv[0, :, 0:1, :], t["state_sc_conv"][0, :, 1:2, :]).then_inc(tail2_stored, 16)

            def load_unit(u, col):
                sp.dma_start(wslot[u], w_in_v[:, :, ds(col, P)]).then_inc(w_landed[u], 16)

            w_ssm_v = t["w_ssm_out"][0].rearrange("(k p) c -> p k c", p=P)
            w_sc_v = t["w_sc_out"][0].rearrange("(k p) c -> p k c", p=P)

            def load(u, src):
                sp.dma_start(wslot[u], src).then_inc(w_landed[u], 16)

            def load_whole(u, src):
                sp.dma_start(w_all[u], src).then_inc(w_landed[u], 16)

            def load_b(c, h, x):
                (load_whole if x == 0 else load)((0, 1 + 4 * h, 2 + 4 * h)[x], [w_in_v[:, :, COL_GB + h * P:], w_ssm_v[:, 0:KD, h * P:],
                                 w_ssm_v[:, KD:2 * KD, h * P:]][x][:, :, ds(c, P)])

            def load_short(c, h, x):
                load_whole(x, w_in_v[:, :, (COL_SC, COL_SH, COL_SB)[x] + h * P:][:, :, ds(c, P)])

            def load_a(c, h, x):
                (load_whole if x == 0 else load)(x * (1 + h), [w_in_v[:, :, COL_GA + h * P:], w_sc_v[:, :, h * P:]][x][:, :, ds(c, P)])

            def load_states(g):
                for j in range(2):
                    sp.dma_start(hs[:, :, j, :], state_rows(t["state_ssm"], g * 2 + j)).then_inc(h0_landed, 16)

            def turn(g, load, ssd):
                gp = g - 1 if ssd else None
                if ssd:
                    sp.wait_ge(tail_copied, gp + 1)
                    cols = [(0, gp * 256, 256), (256, gp * N + D_INNER, N), (384, gp * N + (D_INNER + GROUPS * N), N)]
                    for at, col, w in cols:
                        sp.dma_start(p_ssm_conv[0, 0, :, ds(col, w)], tail[0:3, at:at + w]).then_inc(tail_stored, 16)
                        sp.dma_start(s_ssm_conv[0, :, 2, ds(col, w)], tail[3:11, at:at + w]).then_inc(tail_stored, 16)
                for u in range(6):
                    if load:
                        sp.wait_ge(proj_done, g * 18 + (3 * u + 3))
                        if isinstance(g, int) and g == GROUPS - 1:
                            if u in (0, 1, 2, 5):
                                load_b(0, u // 5, u % 4)
                        else:
                            load_unit(u, group_cols(g + 1)[u])
                    if ssd and u == 1:
                        sp.wait_ge(hs_ready, gp + 1)
                        sp.wait_ge(sc_used, gp + 1)
                        for j in range(2):
                            sp.dma_start(state_rows(s_ssm, gp * 2 + j), hs[:, :, j, :]).then_inc(hs_stored, 16)
                    if ssd and u == 4:
                        sp.wait_ge(pstate_copied, gp + 1)
                        sp.dma_start(p_ssm[0, 0, ds(gp * HPG, HPG)].rearrange("(j h) p n -> (h p) j n", h=2),
                                     pstate.rearrange("p (j n) -> p j n", j=2)).then_inc(pstate_stored, 16)
                        if not (isinstance(g, int) and g == GROUPS):
                            sp.wait_ge(hs_stored, gp * 32 + 32)
                            load_states(gp + 1)

            sp.wait_ge(mod_added, 12)
            for u in range(6):
                load_unit(u, group_cols(0)[u])
            sp.wait_ge(cols_copied, 5)
            sp.dma_start(cum_dram.rearrange("(x p t) -> p x t", x=2, p=P),
                         cum_rows.rearrange("p (x t) -> p x t", x=2)).then_inc(cum_stored, 16)
            sp.wait_ge(dt_ready, 1)
            sp.wait_ge(cum_stored, 16)
            for c in range(2):
                sp.dma_start(cumb[c], chunk_sums(c)).then_inc(cum_landed[c], 16)
            load_states(0)
            turn(0, True, False)
            with sp.Fori(0, GROUPS - 2) as i:
                turn(i + 1, True, True)
            turn(GROUPS - 1, True, True)
            turn(GROUPS, False, True)
            def merge_turn(i, load, out_loads, split_before, out_done):
                c = sp.snap(i * 256 + 256)
                for h in range(2):
                    sp.wait_ge(split_ready, i * 2 + (split_before + h + 2))
                    load(c, h, 0)
                    sp.wait_ge(out_done, i * 6 + (3 * h + 3))
                    for x in out_loads:
                        load(c, h, x)

            sp.wait_ge(normed, 72)
            load_b(0, 1, 2)
            sp.wait_ge(split_ready, 1)
            load_b(0, 1, 0)
            with sp.Fori(0, 3) as i:
                merge_turn(i, load_b, (1, 2), 0, yb_done)
            sp.wait_ge(split_ready, 8)
            load_short(0, 0, 0)
            sp.wait_ge(yb_done, 21)
            load_short(0, 0, 1)
            load_short(0, 0, 2)
            with sp.Fori(0, 3) as i:
                c = sp.snap(i * 256)
                for v in range(6):
                    sp.wait_ge(split_ready, i * 6 + (v + 9))
                    load_short(c, (v + 3) // 3, v % 3)
            for x in range(3):
                sp.wait_ge(split_ready, 27 + x)
                load_short(3 * 256, 1, x)
            sp.wait_ge(split_ready, 30)
            load_a(0, 0, 0)
            for h in range(2):
                sp.wait_ge(split_ready, 31 + h)
                load_a(0, h, 1)

            def load_x0(i):
                rows = P if i < TILES else NS
                sp.dma_start(x0b[i % 2][0:rows, :], tile_rows(x0_dram, i)).then_inc(x0_landed[i % 2], 16)

            sp.wait_ge(split_ready, 33)
            load_a(0, 1, 0)
            sp.wait_ge(short_done, 72)
            sp.wait_ge(ya_ready, 8)
            sp.wait_ge(tail2_copied, 8)
            sp.dma_start(p_sc_conv[0, 0], tail_sc[0:2, :]).then_inc(tail2_stored, 16)
            sp.dma_start(s_sc_conv[0, :, 1, :], tail_sc[2:10, :]).then_inc(tail2_stored, 16)
            sp.wait_ge(tail2_stored, 64)
            sp.dma_start(w_o, t["w_o"][0].rearrange("(k p) c -> p k c", p=P)).then_inc(wo_landed, 16)
            for i in range(2):
                load_x0(i)
            with sp.Fori(0, 3) as i:
                merge_turn(i, load_a, (1,), 32, ya_done)
            sp.wait_ge(ga_done, 24)
            for dst, src in ((g1_p, mod_dram[NS, 2 * D:3 * D].partition_broadcast(P)),
                             (sh2_p, mod_dram[NS, 3 * D:4 * D].partition_broadcast(P)),
                             (sc2_p, mod_dram[NS, 4 * D:5 * D].partition_broadcast(P)),
                             (g1_s, mod_dram[0:NS, 2 * D:3 * D]), (sh2_s, mod_dram[0:NS, 3 * D:4 * D]),
                             (sc2_s, mod_dram[0:NS, 4 * D:5 * D]),
                             (mix_g, t["ln_mix_g"][0].partition_broadcast(P)),
                             (mix_b, t["ln_mix_b"][0].partition_broadcast(P)),
                             (w_r[:, :, 0:EGROUPS], t["w_route_g"][0].rearrange("(k p) e -> p k e", p=P)),
                             (w_r[:, :, EGROUPS:36], t["w_route_e"][0].rearrange("(k p) e -> p k e", p=P)),
                             (b_r[:, 0:EGROUPS], t["b_route_g"][0].partition_broadcast(P)),
                             (b_r[:, EGROUPS:36], t["b_route_e"][0].partition_broadcast(P))):
                sp.dma_start(dst, src).then_inc(mixw_landed, 16)
            for i in range(2, TILES + 1):
                sp.wait_ge(x0_used, i - 1)
                load_x0(i)

            sp.wait_ge(routed, 1)
            sp.wait_ge(u2_stored[0], 80)
            sp.wait_ge(u2_stored[1], 64)
            pairs = sp.value_load(plan[:, NBX:NBX + 1], min_val=1, max_val=BLOCKS // 2)
            for dst, src in ((g2_p, mod_dram[NS, 5 * D:6 * D].partition_broadcast(P)), (g2_s, mod_dram[0:NS, 5 * D:6 * D]),
                             (ffn_g, t["ln_ffn_g"][0].partition_broadcast(P)),
                             (ffn_b, t["ln_ffn_b"][0].partition_broadcast(P))):
                sp.dma_start(dst, src).then_inc(finw_landed, 16)
            with sp.Fori(0, pairs) as i:
                for b in range(2):
                    expert = sp.value_load(plan[:, ds(i * 2 + b, 1)], min_val=0, max_val=EXPERTS - 1)
                    sp.wait_ge(up_done, i * 2 + (b + 1))
                    sp.dma_start(w13[b], t["w_moe_13"][0].rearrange("e (k p) c -> p (e k) c", p=P)
                                 [:, ds(expert * KD, KD), :]).then_inc(w13_landed[b], 16)
                    sp.wait_ge(o_done, i * 2 + (b + 1))
                    sp.dma_start(w2[b], t["w_moe_2"][0].rearrange("e (k p) c -> p (e k) c", p=P)
                                 [:, ds(expert * 4, 4), :]).then_inc(w2_landed[b], 16)

            for i in range(TILES + 1):
                sp.wait_ge(y_out, i + 1)
                rows = P if i < TILES else NS
                dst = y_prompt[0, i * P:(i + 1) * P, :] if i < TILES else y_sample.rearrange("b l d -> (b l) d")
                sp.dma_start(dst, fa[i % 3][0:rows, :]).then_inc(y_stored[i % 3], 16)
            for i in range(3):
                sp.wait_ge(y_stored[i], 48)
            sp.wait_ge(tail_stored, 768)
            sp.wait_ge(pstate_stored, 128)
            sp.wait_ge(hs_stored, 256)

        @block.gpsimd
        def _(pool):
            st = Steps(pool, pool_step)
            st.did(pool.memset(ones, 1.0))
            st.did(pool.memset(one[:, :], 1.0))
            st.did(pool.memset(ones_avg, 1.0 / 256))
            st.did(pool.memset(epsc, EPS))
            st.settle()
            st.did(pool.affine_select(out=ident, in_=ones, pattern=[[1, P]], compare_op=ALU.is_equal, fill=0.0,
                                      base=0, channel_multiplier=-1))
            st.did(pool.affine_select(out=tri, in_=ones, pattern=[[1, P]], compare_op=ALU.is_ge, fill=0.0,
                                      base=0, channel_multiplier=-1))
            pool.affine_select(out=stri, in_=ones, pattern=[[1, P]], compare_op=ALU.is_gt, fill=0.0,
                               base=0, channel_multiplier=-1).then_inc(consts_ready, 1)
            pool.wait_ge(consts_ready, 1)
            for i in range(TILES + 1):
                pool.wait_ge(x0_ready, i + 1)
                rows = P if i < TILES else NS
                pool.dma_start(tile_rows(x0_dram, i), xr[i % 4][0:rows, :]).then_inc(x0_stored[i % 4], 16)
            pool.wait_ge(mod_added, 12)
            pool.dma_start(mod_dram, mod).then_inc(mod_stored, 16)
            pool.wait_ge(dt_ready, 1)
            pool.wait_ge(ut_ready, TILES)
            pool.wait_ge(mod_stored, 16)

            def group(g, last):
                pool.wait_ge(silu_done, g * 4 + 4)
                pool.tensor_tensor(diag, widen(ident, 1, NS), widen(proc[2][:, SEQ:TOK], 2, N),
                                   ALU.mult).then_inc(diag_b_ready, 1)
                pool.wait_ge(sb_ready, g + 1)
                pool.tensor_tensor(diag, widen(ident, 1, NS), widen(proc[3][:, SEQ:TOK], 2, N),
                                   ALU.mult).then_inc(diag_c_ready, 1)
                if not last:
                    pool.wait_ge(pstate_stored, g * 16 + 16)

            for first in range(LEAST, BLOCKS, KD):
                n = min(KD, BLOCKS - first)
                pool.dma_start(rows_dram[first * P:(first + n) * P, :].rearrange("(b p) d -> p b d", p=P),
                               u_whole[:, 0:n * D].rearrange("p (b d) -> p b d", b=n)).then_inc(filled, 16)
            with pool.Fori(0, GROUPS - 1) as g:
                group(g, False)
            group(GROUPS - 1, True)
            def split(raw, v):
                hi = w_hi[v]
                st.did(pool.tensor_tensor(hi, w_all[raw], one[:, 0:1].unsqueeze(2).to_broadcast([P, KD, P]), ALU.mult))
                st.settle()
                pool.tensor_tensor(w_lo[v], w_all[raw], hi.bitcast(F32), ALU.subtract).then_inc(split_ready, 1)

            def split_gates(landed_before, done):
                with pool.Fori(0, 7) as i:
                    st.enter(i, 1)
                    pool.wait_ge(w_landed[0], i * 16 + (landed_before + 32))
                    pool.wait_ge(done, i * 3 + 3)
                    split(0, 0)
                st.leave(7)

            def split_short(i, first):
                for v in range(6):
                    pool.wait_ge(w_landed[v % 3], i * 32 + ((256 if v % 3 == 0 else 192) + 16 * (v // 3 + 1)))
                    if first and v == 0:
                        pool.wait_ge(gb_done, 24)
                    elif first and v == 1:
                        pool.wait_ge(yb_done, 24)
                    else:
                        pool.wait_ge(short_done, i * 18 + (3 * v - 3))
                    split(v % 3, v % 2)

            pool.wait_ge(proj_done, 144)
            pool.wait_ge(w_landed[0], 144)
            split(0, 0)
            split_gates(128, gb_done)
            split_short(0, True)
            with pool.Fori(0, 3) as i:
                st.enter(i, 6)
                split_short(i + 1, False)
            st.leave(3)
            pool.wait_ge(w_landed[0], 384 + 16)
            pool.wait_ge(short_done, 69)
            split(0, 0)
            split_gates(384, ga_done)
            pool.wait_ge(filled, 16 * len(range(LEAST, BLOCKS, KD)))
            pool.wait_ge(merged_a, 24)
            st.did(pool.iota(iota_r, [[1, P]], base=0, channel_multiplier=0, allow_small_or_imprecise_dtypes=True))
            st.did(pool.iota(tok_id, [[P, NI]], base=0, channel_multiplier=1, allow_small_or_imprecise_dtypes=True))
            st.did(pool.memset(one32, 1.0))
            st.settle()
            pool.tensor_single_scalar(valid, tok_id, float(TOK), ALU.is_lt).then_inc(iotas_ready, 1)
            for i in range(TILES + 1):
                rows = P if i < TILES else NS
                pool.wait_ge(u2_ready, i + 1)
                pool.dma_start(tile_rows(u2_dram, i), u2[i % 2][0:rows, :]).then_inc(u2_stored[i % 2], 16)
            pool.wait_ge(u2_stored[0], 80)
            pool.wait_ge(u2_stored[1], 64)

            def gather(b, column):
                pool.indirect_dma_start(xg[b], None, u2_dram, bass.IndirectOffsetOnAxis(ap=column, axis=0)).then_inc(xg_landed[b], 16)

            def carry_wait(carries_before):
                if carries_before is not None:
                    pool.wait_ge(carried, carries_before)
                pool.tensor_tensor(spare, ones[:, 0:1], ones[:, 0:1], ALU.mult).then_inc(carried, 1)

            pool.wait_ge(routed, 1)
            pairs = pool.value_load(plan[:, NBX:NBX + 1], min_val=1, max_val=BLOCKS // 2)
            carry_wait(None)
            for b in range(2):
                gather(b, tok_of[:, b:b + 1])
            with pool.Fori(0, pairs) as i:
                for b in range(2):
                    pool.wait_ge(xg_turned, i * 2 + (b + 1))
                    pool.wait_ge(idx_ready, i * 2 + (b + 1))
                    carry_wait(i * 2 + (b + 1))
                    gather(b, idx2[:, b:b + 1])
            pool.wait_ge(xg_landed[0], pairs * 16 + 16)
            pool.wait_ge(xg_landed[1], pairs * 16 + 16)
            pool.wait_ge(rows_stored[0], pairs * 16)
            pool.wait_ge(rows_stored[1], pairs * 16)
            carry_wait(pairs * 2 + 1)
            for i in range(TILES + 1):
                rows = P if i < TILES else NS
                if i >= 3:
                    pool.wait_ge(y_stored[i % 3], 16 * (i // 3))
                for a, buf in enumerate((fa, fb)):
                    pool.indirect_dma_start(
                        buf[i % 3][0:rows, :], None, rows_dram,
                        bass.IndirectOffsetOnAxis(ap=dest_i[0:rows, a * NI + i:a * NI + i + 1], axis=0)).then_inc(fin_landed[i % 3], 16)

        @block.scalar
        def _(act):
            st = Steps(act, act_step)
            act.wait_ge(ct_turned, 1)
            act.activation(c_t.rearrange("p k m -> p (k m)"), bank6[:, 0:KD * MROWS], ACT.Silu).then_inc(ct_ready, 1)
            act.wait_ge(consts_ready, 1)

            def std(i):
                rows = P if i < TILES else NS
                act.wait_ge(var_ready, i + 1)
                act.activation(mv[0:rows, i % 4, 2:3], mv[0:rows, i % 4, 1:2], ACT.Sqrt,
                               bias=epsc[0:rows, :]).then_inc(std_ready, 1)

            def ut(i):
                act.wait_ge(cols_copied, 1)
                act.wait_ge(x_turned, i + 1)
                for k in range(KD):
                    src = banks[2 + 2 * (i % 2) + k // 4][:, (k % 4) * P:(k % 4 + 1) * P]
                    last = act.activation(uT[:, k, i * P:(i + 1) * P], src, ACT.Identity,
                                          bias=mod_t[:, k, NS:MROWS], scale=mod_t[:, KD + k, NS:MROWS])
                last.then_inc(ut_ready, 1)

            for i in range(4):
                std(i)
            for i in range(TILES):
                if i + 4 <= TILES:
                    std(i + 4)
                ut(i)
            act.wait_ge(dt_in, 1)
            st.did(act.activation(dte, dtr, ACT.Abs))
            st.settle()
            act.activation(dte, dte, ACT.Exp, scale=-1.0).then_inc(dt_exp, 1)
            act.wait_ge(small_landed, 13 * 16)
            act.activation(alog, alog, ACT.Exp).then_inc(dt_ln, 1)
            act.wait_ge(dt_sum, 1)
            act.activation(dtl, dtw, ACT.Ln).then_inc(dt_ln, 1)
            act.wait_ge(mod_stored, 16)
            for s in range(3):
                act.wait_ge(proj_done, s + 1)
                act.activation(raw[0][:, s * SUB:(s + 1) * SUB], banks[s][:, 0:SUB], ACT.Copy).then_inc(raw_ready, 1)
            act.wait_ge(dta_ready, 2)
            act.activation(das, das, ACT.Exp).then_inc(dt_exp, 1)
            act.wait_ge(dt_sum, 2)
            act.activation(wend, wend, ACT.Exp).then_inc(wend_ready, 1)
            act.activation(decay, cend, ACT.Exp).then_inc(wend_ready, 1)

            def turn(g, proj, ssd, steps=range(18)):
                gp = g - 1 if ssd else None
                n0 = g * 18

                def cum_side(c):
                    q = gp * 8
                    act.wait_ge(cum_landed[c % 2], gp * 64 + 16 * (c // 2 + 1))
                    if c:
                        act.wait_ge(y_ready, q + c)
                    act.activation(csc, cumb[c % 2], ACT.Exp).then_inc(ecum_ready, 1)

                def e_side(c):
                    act.wait_ge(seg_ready, gp * 8 + (c + 1))
                    act.activation(segm, segm, ACT.Exp).then_inc(e_ready, 1)
                    if c < 6 or proj:
                        act.wait_ge(ecum_ready, gp * 8 + (c + 1))
                        act.dma_start(cumb[c % 2], chunk_sums(gp * 8 + (c + 2))).then_inc(cum_landed[c % 2], 16)

                def rms_side(c):
                    w = P if c < 8 else NS
                    act.wait_ge(rms_ready, gp * 9 + (c + 1))
                    if c:
                        act.wait_ge(normed, gp * 9 + c)
                    act.activation(rs[:, 0:w], bank7[:, 0:w], ACT.Ln, bias=epsc).then_inc(act_ln, 1)
                    act.wait_ge(act_ln, gp * 9 + (c + 1))
                    act.activation(rs[:, 0:w], rs[:, 0:w], ACT.Exp, scale=-0.5).then_inc(rs_ready, 1)

                def square(c):
                    w = P if c < 8 else NS
                    act.wait_ge(y_gated, gp * 9 + (c + 1))
                    if c:
                        act.wait_ge(rms_ready, gp * 9 + c)
                    act.activation(sq[:, :, 0:w], ybuf[c % 2][:, :, 0:w], ACT.Square).then_inc(sq_ready, 1)

                def silu(u):
                    act.wait_ge(conv_done, gp * 4 + (u + 1))
                    act.activation(proc[u], proc[u], ACT.Silu).then_inc(silu_done, 1)

                if ssd:
                    for j in range(2):
                        act.wait_ge(raw_ready, gp * 18 + (15 + 3 * j))
                        act.activation(raw[4 + j], raw[4 + j], ACT.Silu).then_inc(zsilu_done, 1)
                for s in steps:
                    u = s // 3
                    if proj:
                        act.wait_ge(proj_done, n0 + (s + 1))
                        if ssd and u < 4:
                            act.wait_ge(conv_done, gp * 4 + (u + 1))
                            if s == 0:
                                act.wait_ge(tails_done, gp + 1)
                        if ssd and u >= 4:
                            act.wait_ge(y_gated, gp * 9 + 3 * (s % 3 + 1))
                        act.activation(raw[u][:, (s % 3) * SUB:(s % 3 + 1) * SUB], banks[s % 3][:, 0:SUB],
                                       ACT.Copy).then_inc(raw_ready, 1)
                    if not ssd:
                        continue
                    if s == 0:
                        act.wait_ge(tails_done, gp + 1)
                        act.activation(tail, bank6[0:11, :], ACT.Copy).then_inc(tail_copied, 1)
                    if s <= 2:
                        silu(s)
                    if s == 2:
                        silu(3)
                    if s == 3:
                        cum_side(0)
                        e_side(0)
                    if 6 <= s <= LAST_S2:
                        c = s - 6
                        if c < 7:
                            cum_side(c + 1)
                        if c:
                            rms_side(c - 1)
                        square(c)
                        if c < 7:
                            e_side(c + 1)
                    if s == 14:
                        rms_side(7)
                        square(8)
                    if s == 15:
                        rms_side(8)
                if ssd:
                    act.wait_ge(normed, gp * 9 + 9)
                    act.wait_ge(tail_stored, gp * 96 + 96)

            turn(0, True, False, range(3, 18))
            with act.Fori(0, GROUPS - 1) as i:
                turn(i + 1, True, True)
            turn(GROUPS, False, True)
            act.wait_ge(normed, 72)
            act.wait_ge(hs_stored, 256)
            act.wait_ge(tail_stored, 768)
            act.wait_ge(pstate_stored, 128)
            for k in range(0, KD, 2):
                act.activation(u_hi[:, k:k + 2, :], uT[:, k:k + 2, :], ACT.Copy).then_inc(u_hi_ready, 1)

            def gates(i, first, done, ready, used, swapped=False):
                for h in range(2):
                    for part in range(3):
                        n = 3 * h + part
                        act.wait_ge(done, i * 6 + (n + 1))
                        if not (first and h == 0):
                            act.wait_ge(used, i * 6 + (n - 2))
                        bank = banks[3 + part if swapped and h == 0 else part]
                        act.activation(gsb[:, part * SUB:(part + 1) * SUB], bank[:, 0:SUB],
                                       ACT.Sigmoid).then_inc(ready, 1)

            gates(0, True, gb_done, gsig_ready, merged_b, True)
            with act.Fori(0, 3) as i:
                gates(i + 1, False, gb_done, gsig_ready, merged_b)

            def short(i, first):
                for h in range(2):
                    v = 3 * h
                    for part in range(3):
                        act.wait_ge(short_done, i * 18 + (3 * v + part + 1))
                        if not first:
                            act.wait_ge(p_made, i * 6 + (3 * h + part - 5))
                        act.activation(scb[h][:, part * SUB:(part + 1) * SUB],
                                       banks[3 * (v % 2) + part][:, 0:SUB], ACT.Copy).then_inc(sc_copied, 1)
                    for part in range(3):
                        act.wait_ge(short_done, i * 18 + (3 * (v + 2) + part + 1))
                        if not first:
                            act.wait_ge(ya_ready, i * 2 + (h - 1))
                        act.activation(sbb[h][:, part * SUB:(part + 1) * SUB],
                                       banks[3 * (v % 2) + part][:, 0:SUB], ACT.Copy).then_inc(sb_copied, 1)
                    act.wait_ge(tail2_done, i * 2 + (h + 1))
                    act.activation(tail_sc[:, ds((i * 2 + h) * P, P)], bank6[0:10, h * P:(h + 1) * P],
                                   ACT.Copy).then_inc(tail2_copied, 1)

            short(0, True)
            with act.Fori(0, 3) as i:
                short(i + 1, False)
            gates(0, True, ga_done, gsig2_ready, merged_a)
            with act.Fori(0, 3) as i:
                gates(i + 1, False, ga_done, gsig2_ready, merged_a)

            for i in range(TILES + 1):
                rows = P if i < TILES else NS
                act.wait_ge(mvar_ready, i + 1)
                act.activation(mv2[0:rows, i % 2, 2:3], mv2[0:rows, i % 2, 1:2], ACT.Sqrt,
                               bias=epsc[0:rows, :]).then_inc(mstd_ready, 1)
                act.wait_ge(u2_turned, i + 1)
                for half in range(2):
                    src = banks[4 + half].rearrange("p (k t) -> p k t", k=4)[:, :, 0:rows]
                    dst = u2t[i % 2][:, 512 * half:512 * half + 512].rearrange("p (k t) -> p k t", k=4)[:, :, 0:rows]
                    last = act.activation(dst, src, ACT.Copy)
                    if half == 0:
                        st.did(last)
                last.then_inc(u2t_ready, 1)
            act.wait_ge(route_d, 1)
            act.activation(grp_t, grp_d, ACT.Exp).then_inc(route_e, 1)
            act.wait_ge(route_d, 2)
            act.activation(lt, ld, ACT.Exp).then_inc(route_e, 1)
            act.wait_ge(route_d, 3)
            act.activation(wb, wb, ACT.Exp).then_inc(route_e, 1)

            def turned(b, n):
                act.wait_ge(xg_turned, n)
                st.did(act.activation(xt[b][:, 0:512], banks[4][:, :], ACT.Copy))
                act.activation(xt[b][:, 512:1024], banks[5][:, :], ACT.Copy).then_inc(xt_ready, 1)

            act.wait_ge(routed, 1)
            pairs = act.value_load(plan[:, NBX:NBX + 1], min_val=1, max_val=BLOCKS // 2)
            turned(0, 1)
            with act.Fori(0, pairs) as i:
                for b in range(2):
                    act.wait_ge(gate_done, i * 2 + (b + 1))
                    act.activation(hm[b], banks[0][:, :], ACT.Silu).then_inc(sig_ready, 1)
                    turned(1 - b, i * 2 + (b + 2))
                    act.wait_ge(o_free, i * 2 + (b + 2))
                    act.dma_start(rows_dram[ds((i * 2 + b) * P, P), :], yo[b]).then_inc(rows_stored[b], 16)
            for i in range(TILES + 1):
                rows = P if i < TILES else NS
                act.wait_ge(fin_landed[i % 3], 32 * (i // 3 + 1))
                act.activation(fa[i % 3][0:rows, :], fa[i % 3][0:rows, :], ACT.Copy,
                               scale=wts[0:rows, i:i + 1]).then_inc(f_scaled, 1)
                act.wait_ge(fvar_ready, i + 1)
                act.activation(mv2[0:rows, i % 2, 2:3], mv2[0:rows, i % 2, 1:2], ACT.Sqrt,
                               bias=epsc[0:rows, :]).then_inc(fstd_ready, 1)

        @block.vector
        def _(dve):
            st = Steps(dve, dve_step)

            def norm(i):
                rows = P if i < TILES else NS
                x = xr[i % 4][0:rows, :]
                dve.wait_ge(x_landed[i % 4], 16 * (i // 4 + 1))
                for h in range(2):
                    st.did(dve.bn_stats(stats[0:rows, i % 4, 6 * h:6 * h + 6], x[:, 512 * h:512 * h + 512]))
                st.settle()
                dve.bn_aggr(mv[0:rows, i % 4, 0:2], stats[0:rows, i % 4, :]).then_inc(var_ready, 1)
                dve.wait_ge(std_ready, i + 1)
                st.did(dve.reciprocal(mv[0:rows, i % 4, 3:4], mv[0:rows, i % 4, 2:3]))
                if i == 0:
                    dve.wait_ge(small_landed, 13 * 16)
                st.did(dve.scalar_tensor_tensor(x, x, mv[0:rows, i % 4, 0:1], ln_g[0:rows, :], ALU.subtract,
                                                ALU.mult))
                st.settle()
                dve.scalar_tensor_tensor(x, x, mv[0:rows, i % 4, 3:4], ln_b[0:rows, :], ALU.mult,
                                         ALU.add).then_inc(x0_ready, 1)

            def add_mod(q):
                dve.wait_ge(mod_done, q + 1)
                dve.tensor_tensor(mod[:, q * 512:(q + 1) * 512], banks[q % 2][0:MROWS, :],
                                  bada[:, q * 512:(q + 1) * 512], ALU.add).then_inc(mod_added, 1)

            for q in range(4):
                norm(q)
                add_mod(q)
            dve.wait_ge(cols_turned, 1)
            st.did(dve.tensor_copy(mod_t[:, 0:KD, :], bank6[:, 0:72].rearrange("p (k m) -> p k m", k=KD)))
            dve.tensor_scalar(mod_t[:, KD:16, :], bank6[:, 72:144].rearrange("p (k m) -> p k m", k=KD), 1.0, None,
                              ALU.add).then_inc(cols_copied, 1)
            dve.wait_ge(cols_turned, 2)
            src = bank6[:, 0:KD * ROWS_C].rearrange("p (k r) -> p k r", k=KD)
            for a, b in ((0, 3), (19, 21)):
                st.did(dve.tensor_copy(colc[:, :, a:b], src[:, :, a:b]))
            for r in range(2):
                last = dve.tensor_copy(colc[:, :, 3 + r * NS:3 + (r + 1) * NS],
                                       src[:, :, 3:19].rearrange("p k (b r) -> p r k b", r=2)[:, r])
                if r == 0:
                    st.did(last)
            last.then_inc(cols_copied, 1)
            dve.wait_ge(cols_copied, 2)
            for r in range(2):
                st.did(dve.tensor_copy(normg[:, KD * r:KD * r + KD], colc[:, :, 19 + r]))
            for h in range(2):
                st.did(dve.tensor_copy(dskip[HD * h:HD * h + HD, :],
                                       dskb[HD * h:HD * h + HD, :].rearrange("p (j h) -> p h j", h=2)[:, h, :]))
            for half in range(2):
                dve.wait_ge(cols_turned, 3 + half)
                src = bank6[:, 0:16 * ROWS_S].rearrange("p (k r) -> p k r", k=16)
                st.did(dve.tensor_copy(convw_f.rearrange("p (k r) -> p k r", r=5)[:, 16 * half:16 * half + 16, :],
                                       src[:, :, 0:5]))
                for r in range(3):
                    last = dve.tensor_copy(
                        convst_f.rearrange("p (k r b) -> p k r b", r=3, b=NS)[:, 16 * half:16 * half + 16, r, :],
                        src[:, :, 5:29].rearrange("p k (b r) -> p r k b", r=3)[:, r])
                    if r < 2:
                        st.did(last)
                last.then_inc(cols_copied, 1)
            for i in range(TILES):
                if i + 4 <= TILES:
                    norm(i + 4)
                add_mod(4 + i)
            dve.wait_ge(x_turned, 9)
            for k in range(KD):
                src = banks[2 + k // 4][:, (k % 4) * P:(k % 4) * P + NS]
                st.did(dve.tensor_tensor(uT[:, k, SEQ:TOK], src, mod_t[:, KD + k, 0:NS], ALU.mult))
            st.settle()
            for k in range(KD):
                last = dve.tensor_tensor(uT[:, k, SEQ:TOK], uT[:, k, SEQ:TOK], mod_t[:, k, 0:NS], ALU.add)
            last.then_inc(ut_s_ready, 1)

            st.did(dve.memset(dtr, 0.0))
            st.settle()
            dve.wait_ge(dt_raw, 1)
            NP_ = TILES * HEADS
            st.did(dve.tensor_tensor(dtr[:, 0:NP_].rearrange("p (c h) -> p c h", c=TILES),
                                     bank7[:, 0:NP_].rearrange("p (c h) -> p c h", c=TILES),
                                     widen(dtb, 1, TILES), ALU.add))
            dve.tensor_tensor(dtr[0:NS, NP_:DTW], bank7[0:NS, NP_:DTW], dtb[0:NS, :], ALU.add).then_inc(dt_in, 1)
            dve.wait_ge(dt_exp, 1)
            st.did(dve.tensor_scalar(dtw, dte, 1.0, None, ALU.add))
            st.settle()
            dve.tensor_scalar(dtq, dtw, -1.0, None, ALU.add).then_inc(dt_sum, 1)
            dve.wait_ge(dt_sum, 1)
            st.did(dve.tensor_scalar(dtm, dtq, 0.0, None, ALU.is_equal))
            st.settle()
            st.did(dve.tensor_tensor(dtq, dtq, dtm, ALU.add))
            st.settle()
            st.did(dve.reciprocal(dtq, dtq))
            dve.wait_ge(dt_ln, 2)
            st.did(dve.tensor_tensor(dtl, dtl, dtm, ALU.add))
            st.settle()
            st.did(dve.tensor_tensor(dtl, dtl, dte, ALU.mult))
            st.did(dve.tensor_scalar(dtr, dtr, 0.0, None, ALU.max))
            st.settle()
            st.did(dve.tensor_tensor(dtl, dtl, dtq, ALU.mult))
            st.did(dve.tensor_scalar(alog, alog, -1.0, None, ALU.mult))
            st.settle()
            st.did(dve.tensor_tensor(dtr, dtr, dtl, ALU.add))
            st.settle()
            gcr = dict(g=GROUPS, c=CHUNKS, r=HPG)
            st.did(dve.tensor_copy(dt_g.rearrange("p (g c r) -> p c g r", **gcr),
                                   dtr[:, 0:NP_].rearrange("p (c g r) -> p c g r", **gcr)))
            st.settle()
            dve.tensor_tensor(dta_g.rearrange("p (g c r) -> p g c r", **gcr),
                              dt_g.rearrange("p (g c r) -> p g c r", **gcr),
                              widen(alog.rearrange("p (g r) -> p g r", g=GROUPS), 2, CHUNKS),
                              ALU.mult).then_inc(dta_ready, 1)
            dve.wait_ge(mod_stored, 16)
            dve.tensor_tensor(das, dtr[0:NS, NP_:DTW], alog[0:NS, :], ALU.mult).then_inc(dta_ready, 1)
            dve.wait_ge(cum_done, 1)
            dve.tensor_copy(cum_rows, bank6[:, 0:256]).then_inc(cols_copied, 1)
            st.did(dve.tensor_copy(cum_t, bank7[:, 0:256]))
            st.did(dve.tensor_copy(cend, bank7[:, 256:512]))
            st.settle()
            dve.tensor_tensor(wend, cend, cum_t, ALU.subtract).then_inc(dt_sum, 1)
            dve.wait_ge(dt_exp, 2)
            spr = spread.rearrange("p (x b h) -> p x b h", x=2, b=NS)
            st.did(dve.tensor_tensor(spr[:, 0], widen(dtr[0:NS, NP_:DTW], 1, NS),
                                     widen(ident[0:NS, 0:NS], 2, HEADS), ALU.mult))
            dve.tensor_tensor(spr[:, 1], widen(das, 1, NS),
                              widen(ident[0:NS, 0:NS], 2, HEADS), ALU.mult).then_inc(spread_ready, 1)
            dve.wait_ge(wend_ready, 1)
            st.did(dve.tensor_tensor(wend, wend, dt_g, ALU.mult))
            dve.wait_ge(spread_done, 1)
            dve.wait_ge(wend_ready, 2)
            for x, dst in ((0, dt_s), (1, dec_s)):
                for h in range(2):
                    src = bank7[HD * h:HD * h + HD, 256 * x:256 * x + 256].rearrange("p (b j h) -> p h j b", b=NS, h=2)
                    last = dve.tensor_copy(dst[HD * h:HD * h + HD, :].rearrange("p (j b) -> p j b", b=NS), src[:, h])
                    if (x, h) != (1, 1):
                        st.did(last)
            last.then_inc(dt_ready, 1)
            dve.wait_ge(dt_ready, 1)

            def scan(g):
                idx = [g * 2, g * 2 + 1, g + 16, g + 24]
                for u in range(4):
                    src, dst = raw[u], proc[u]

                    def w(k):
                        return convw_f[:, ds(idx[u] * 5 + k, 1)]

                    def old(r):
                        return convst_f[:, ds(idx[u] * 24 + r * 8, NS)]

                    dve.wait_ge(raw_ready, g * 18 + (3 * u + 3))
                    st.did(dve.tensor_scalar(dst, src, w(3), w(4), ALU.mult, ALU.add))
                    for back in (1, 2, 3):
                        st.settle()
                        st.did(dve.scalar_tensor_tensor(dst[:, SEQ:TOK], old(3 - back), w(3 - back), dst[:, SEQ:TOK],
                                                        ALU.mult, ALU.add))
                        last = dve.scalar_tensor_tensor(dst[:, back:SEQ], src[:, 0:SEQ - back], w(3 - back),
                                                        dst[:, back:SEQ], ALU.mult, ALU.add)
                        if back < 3:
                            st.did(last)
                    last.then_inc(conv_done, 1)

                def operands(c):
                    at = slice(c * P, (c + 1) * P)
                    q = g * 8 + (c + 1)
                    rp = dict(r=HPG)
                    dve.wait_ge(scores_ready, q)
                    st.did(dve.tensor_tensor(cb_m, banks[3][:, 384:512], tri, ALU.mult))
                    x_tok = banks[3][:, 0:256].rearrange("p (r d) -> p r d", **rp)
                    st.did(dve.tensor_tensor(xdt.rearrange("p (r d) -> p r d", **rp), x_tok,
                                             widen(dt_g[:, ds(g * 32 + c * 4, 4)], 2, HD), ALU.mult))
                    st.did(dve.tensor_tensor(xw.rearrange("p (r d) -> p r d", **rp), x_tok,
                                             widen(wend[:, ds(g * 32 + c * 4, 4)], 2, HD), ALU.mult))
                    st.did(dve.tensor_copy(b_tok, banks[3][:, 256:384]))
                    dve.wait_ge(cum_landed[c % 2], g * 64 + 16 * (c // 2 + 1))
                    for r in range(HPG):
                        last = dve.tensor_scalar(segm[:, r * P:(r + 1) * P], cumb[c % 2][:, r * P:(r + 1) * P],
                                                 cum_t[:, ds(g * 32 + (c * 4 + r), 1)], 0.0, ALU.subtract, ALU.min)
                        if r < 3:
                            st.did(last)
                    last.then_inc(seg_ready, 1)
                    dve.wait_ge(ecum_ready, q)
                    cs3 = csc.rearrange("p (r t) -> p r t", **rp)
                    st.did(dve.tensor_tensor(cs3, cs3, widen(proc[3][:, at], 1, HPG), ALU.mult))
                    dve.wait_ge(e_ready, q)
                    st.settle()
                    m3 = segm.rearrange("p (r t) -> p r t", **rp)
                    dve.tensor_tensor(m3, m3, widen(cb_m, 1, HPG), ALU.mult).then_inc(ops_ready, 1)

                def gate(c, y_in, w):
                    at = slice(c * P, c * P + w)
                    yb = ybuf[c % 2][:, :, 0:w]
                    for j in range(2):
                        st.did(dve.scalar_tensor_tensor(yb[:, j, :], xs2[:, j, at], dskip[:, ds(g * 2 + j, 1)],
                                                        y_in[:, j, 0:w], ALU.mult, ALU.add))
                    st.settle()
                    dve.tensor_tensor(yb, yb, z2[:, :, at], ALU.mult).then_inc(y_gated, 1)

                def apply(c):
                    w = P if c < 8 else NS
                    dve.wait_ge(rs_ready, g * 9 + (c + 1))
                    for j in range(2):
                        last = dve.scalar_tensor_tensor(ybT_f[:, ds((g * 2 + j) * TOK + c * P, w)],
                                                        ybuf[c % 2][:, j, 0:w], normg[:, ds(g * 2 + j, 1)],
                                                        rs[:, 0:w], ALU.mult, ALU.mult)
                        if j == 0:
                            st.did(last)
                    last.then_inc(normed, 1)

                operands(0)
                dve.wait_ge(silu_done, g * 4 + 4)
                st.did(dve.tensor_tensor(dtx, xs2[:, :, SEQ:TOK],
                                         dt_s[:, ds(g * 16, 16)].rearrange("p (j b) -> p j b", j=2), ALU.mult))
                dve.wait_ge(h0_landed, g * 32 + 32)
                st.did(dve.tensor_tensor(hs, hs, widen(dec_s[:, ds(g * 16, 16)].rearrange("p (j b) -> p b j", j=2),
                                                       3, N), ALU.mult))
                dve.wait_ge(sb_ready, g + 1)
                st.settle()
                spread_bc = pair[:, :].rearrange("p (b n) -> p b n", b=NS)
                st.did(dve.tensor_tensor(tmp, spread_bc, widen(dtx[:, 0, :], 2, N), ALU.mult))
                st.settle()
                st.did(dve.tensor_tensor(hs[:, :, 0, :], hs[:, :, 0, :], tmp, ALU.add))
                st.settle()
                dve.tensor_tensor(tmp, spread_bc, widen(dtx[:, 1, :], 2, N), ALU.mult).then_inc(sb_used, 1)
                dve.wait_ge(sb_used, g + 1)
                dve.tensor_tensor(hs[:, :, 1, :], hs[:, :, 1, :], tmp, ALU.add).then_inc(hs_ready, 1)
                dve.wait_ge(hs_ready, g + 1)
                dve.wait_ge(sc_ready, g + 1)
                st.did(dve.tensor_tensor(tmp, hs[:, :, 0, :], spread_bc, ALU.mult))
                st.settle()
                st.did(dve.tensor_reduce(ys[:, 0, :], tmp, AX.X, ALU.add))
                st.settle()
                dve.tensor_tensor(tmp, hs[:, :, 1, :], spread_bc, ALU.mult).then_inc(sc_used, 1)
                dve.wait_ge(sc_used, g + 1)
                st.did(dve.tensor_reduce(ys[:, 1, :], tmp, AX.X, ALU.add))
                dve.wait_ge(zsilu_done, g * 2 + 2)
                for c in range(CHUNKS):
                    dve.wait_ge(y_ready, g * 8 + (c + 1))
                    new = banks[5][:, 256:512]
                    if c == 0:
                        st.did(dve.tensor_copy(h_t, new))
                    else:
                        h3 = h_t.rearrange("p (r d) -> p r d", r=HPG)
                        st.did(dve.tensor_tensor(h3, h3, widen(decay[:, ds(g * 32 + c * 4, 4)], 2, HD), ALU.mult))
                        st.settle()
                        st.did(dve.tensor_tensor(h_t, h_t, new, ALU.add))
                    gate(c, banks[5][:, 0:256].rearrange("p (j t) -> p j t", j=2), P)
                    if c < 7:
                        operands(c + 1)
                    if c:
                        apply(c - 1)
                st.settle()
                dve.wait_ge(normed, g * 9 + 7)
                gate(8, ys, NS)
                apply(7)
                dve.wait_ge(ht_ready, g + 1)
                dve.tensor_copy(pstate, bank6[:, 0:256]).then_inc(pstate_copied, 1)
                apply(8)

            PER = 137
            with dve.Fori(0, GROUPS) as g:
                st.enter(g, PER)
                scan(g)
            st.leave(GROUPS)
            dve.wait_ge(hs_stored, 256)
            dve.wait_ge(tail_stored, 768)
            dve.wait_ge(pstate_stored, 128)

            for k in range(0, KD, 2):
                dve.wait_ge(u_hi_ready, k // 2 + 1)
                dve.tensor_tensor(u_lo[:, k:k + 2, :], uT[:, k:k + 2, :], u_hi[:, k:k + 2, :].bitcast(F32),
                                  ALU.subtract).then_inc(u_lo_ready, 1)
            dve.wait_ge(filled, 16 * len(range(LEAST, BLOCKS, KD)))
            dve.wait_ge(u_lo_ready, KD // 2)

            def merge_b(i, swapped=False):
                for h in range(2):
                    for part in range(3):
                        n = 3 * h + part
                        dve.wait_ge(gsig_ready, i * 6 + (n + 1))
                        dve.wait_ge(yb_done, i * 6 + (n + 1))
                        dve.tensor_tensor(merged_f[:, ds((i * 2 + h) * TOK + part * SUB, SUB)],
                                          gsb[:, part * SUB:(part + 1) * SUB],
                                          banks[part if swapped and h == 0 else 3 + part][:, 0:SUB],
                                          ALU.mult).then_inc(merged_b, 1)

            merge_b(0, True)
            with dve.Fori(0, 3) as i:
                merge_b(i + 1)

            def short(i):
                for h in range(2):
                    p, k = pt[h], i * 2 + h
                    for part in range(3):
                        at = slice(part * SUB, (part + 1) * SUB)
                        dve.wait_ge(sc_copied, i * 6 + (3 * h + part + 1))
                        dve.wait_ge(short_done, i * 18 + (9 * h + 3 + part + 1))
                        dve.tensor_tensor(p[:, at], scb[h][:, at], banks[3 * ((3 * h + 1) % 2) + part][:, 0:SUB],
                                          ALU.mult).then_inc(p_made, 1)
                    dve.wait_ge(p_made, i * 6 + (3 * h + 3))

                    def w(x):
                        return colc_f[:, ds(k * ROWS_C + x, 1)]

                    st.did(dve.tensor_scalar(acc, p, w(2), None, ALU.mult))
                    for back in (1, 2):
                        st.settle()
                        st.did(dve.scalar_tensor_tensor(acc[:, SEQ:TOK],
                                                        colc_f[:, ds(k * ROWS_C + (3 + (2 - back) * NS), NS)],
                                                        w(2 - back), acc[:, SEQ:TOK], ALU.mult, ALU.add))
                        st.did(dve.scalar_tensor_tensor(acc[:, back:SEQ], p[:, 0:SEQ - back], w(2 - back),
                                                        acc[:, back:SEQ], ALU.mult, ALU.add))
                    dve.wait_ge(sb_copied, i * 6 + (3 * h + 3))
                    st.settle()
                    dve.tensor_tensor(ya_f[:, ds(k * TOK, TOK)], acc, sbb[h], ALU.mult).then_inc(ya_ready, 1)

            SHORT_STEPS = 10
            with dve.Fori(0, 4) as i:
                st.enter(i, SHORT_STEPS)
                short(i)
            st.leave(4)

            def merge_a(i):
                for h in range(2):
                    for part in range(3):
                        n = 3 * h + part
                        g = gsb[:, part * SUB:(part + 1) * SUB]
                        m = merged_f[:, ds((i * 2 + h) * TOK + part * SUB, SUB)]
                        dve.wait_ge(gsig2_ready, i * 6 + (n + 1))
                        dve.wait_ge(ya_done, i * 6 + (n + 1))
                        st.did(dve.tensor_tensor(g, g, banks[3 + part][:, 0:SUB], ALU.mult))
                        st.settle()
                        dve.tensor_tensor(m, m, g, ALU.add).then_inc(merged_a, 1)

            with dve.Fori(0, 4) as i:
                st.enter(i, 6)
                merge_a(i)
            st.leave(4)

            dve.wait_ge(mixw_landed, 12 * 16)
            dve.wait_ge(merged_a, 24)
            for row in (g1_p, g1_s, sc2_p, sc2_s):
                st.did(dve.tensor_scalar(row, row, 1.0, None, ALU.add))
            for i in range(TILES + 1):
                rows = P if i < TILES else NS
                g1, sc2, sh2 = (g1_p, sc2_p, sh2_p) if i < TILES else (g1_s, sc2_s, sh2_s)
                x = x1[0:rows, i, :]
                x0 = x0b[i % 2][0:rows, :]
                st.settle()
                dve.wait_ge(wo_done, i + 1)
                for half in range(2):
                    at = slice(512 * half, 512 * half + 512)
                    st.did(dve.tensor_tensor(x[:, at], banks[2 * (i % 2) + half][0:rows, :], g1[:, at], ALU.mult))
                st.settle()
                dve.wait_ge(x0_landed[i % 2], 16 * (i // 2 + 1))
                dve.scalar_tensor_tensor(x, x0, ALPHA, x, ALU.mult, ALU.add).then_inc(x0_used, 1)
                dve.wait_ge(x0_used, i + 1)
                for half in range(2):
                    st.did(dve.bn_stats(stats2[0:rows, 6 * half:6 * half + 6], x[:, 512 * half:512 * half + 512]))
                st.settle()
                dve.bn_aggr(mv2[0:rows, i % 2, 0:2], stats2[0:rows, :]).then_inc(mvar_ready, 1)
                dve.wait_ge(mvar_ready, i + 1)
                st.did(dve.scalar_tensor_tensor(x, x, mv2[0:rows, i % 2, 0:1], mix_g[0:rows, :], ALU.subtract,
                                                ALU.mult))
                dve.wait_ge(mstd_ready, i + 1)
                st.did(dve.reciprocal(mv2[0:rows, i % 2, 3:4], mv2[0:rows, i % 2, 2:3]))
                st.settle()
                st.did(dve.scalar_tensor_tensor(x, x, mv2[0:rows, i % 2, 3:4], mix_b[0:rows, :], ALU.mult,
                                                ALU.add))
                st.settle()
                u = u2[i % 2][0:rows, :]
                if i >= 2:
                    dve.wait_ge(u2_turned, i - 1)
                    dve.wait_ge(u2_stored[i % 2], 16 * (i // 2))
                st.did(dve.tensor_tensor(u, x, sc2, ALU.mult))
                st.settle()
                dve.tensor_tensor(u, u, sh2, ALU.add).then_inc(u2_ready, 1)

            dve.wait_ge(iotas_ready, 1)
            st.did(dve.memset(logit, 0.0))
            st.settle()
            dve.wait_ge(logits_done, 1)
            ps = bank7[:, 0:NI * 36].rearrange("p (i e) -> p i e", i=NI)
            st.did(dve.tensor_tensor(logit[:, 0:TILES, :], ps[:, 0:TILES, :], widen(b_r, 1, TILES), ALU.add))
            st.did(dve.tensor_tensor(logit[0:NS, TILES, :], ps[0:NS, TILES, :], b_r[0:NS, :], ALU.add))
            st.settle()

            def step(ins):
                st.did(ins)
                st.settle()

            def first_of(eq, n, idx, onehot):
                step(dve.scalar_tensor_tensor(eq, eq, -64.0, widen(iota_r[:, 0:n], 1, NI), ALU.mult, ALU.add))
                step(dve.tensor_reduce(idx, eq, AX.X, ALU.min))
                step(dve.tensor_scalar(idx, idx, 64.0, None, ALU.add))
                step(dve.tensor_tensor(onehot, widen(iota_r[:, 0:n], 1, NI), widen(idx, 2, n), ALU.is_equal))

            l4, l32 = logit[:, :, 0:EGROUPS], logit[:, :, EGROUPS:36]
            step(dve.tensor_reduce(gmx, l4, AX.X, ALU.max))
            dve.tensor_tensor(grp_d, l4, widen(gmx, 2, EGROUPS), ALU.subtract).then_inc(route_d, 1)
            dve.wait_ge(route_d, 1)
            dve.wait_ge(route_e, 1)
            step(dve.tensor_reduce(gsum, grp_t, AX.X, ALU.add))
            step(dve.tensor_scalar(grp_d, grp_d, 0.0, None, ALU.is_equal))
            first_of(grp_d, EGROUPS, gix, grp)
            step(dve.tensor_scalar(grp_t, grp, -NEG, NEG, ALU.mult, ALU.add))

            def by_group(x):
                return x.rearrange("p i (g e) -> p i g e", g=EGROUPS)

            step(dve.tensor_tensor(by_group(lm), by_group(l32), widen(grp, 3, PER_GROUP), ALU.mult))
            step(dve.tensor_tensor(by_group(lm), by_group(lm), widen(grp_t, 3, PER_GROUP), ALU.add))
            step(dve.tensor_reduce(m1, lm, AX.X, ALU.max))
            dve.tensor_tensor(ld, lm, widen(m1, 2, EXPERTS), ALU.subtract).then_inc(route_d, 1)
            dve.wait_ge(route_d, 2)
            dve.wait_ge(route_e, 2)
            step(dve.tensor_reduce(esum, lt, AX.X, ALU.add))
            step(dve.tensor_scalar(ld, ld, 0.0, None, ALU.is_equal))
            first_of(ld, EXPERTS, ix, e1)
            step(dve.scalar_tensor_tensor(lm, e1, 2 * NEG, lm, ALU.mult, ALU.add))
            step(dve.tensor_reduce(m2, lm, AX.X, ALU.max))
            dve.tensor_tensor(wb, m2, m1, ALU.subtract).then_inc(route_d, 1)
            step(dve.tensor_tensor(ld, lm, widen(m2, 2, EXPERTS), ALU.is_equal))
            first_of(ld, EXPERTS, ix, e2)
            dve.wait_ge(route_e, 3)
            step(dve.reciprocal(wa, esum))
            step(dve.tensor_tensor(wb, wb, wa, ALU.mult))
            step(dve.tensor_tensor(esum, wa, wb, ALU.add))
            step(dve.tensor_tensor(esum, esum, gsum, ALU.mult))
            step(dve.reciprocal(esum, esum))
            step(dve.tensor_tensor(wts[:, 0:NI], wa, esum, ALU.mult))
            step(dve.tensor_tensor(wts[:, NI:2 * NI], wb, esum, ALU.mult))
            step(dve.tensor_tensor(mm, e1, e2, ALU.add))
            step(dve.tensor_tensor(mm, mm, widen(valid, 2, EXPERTS), ALU.mult))
            step(dve.memset(ss[:, 0, :], 0.0))
            for i in range(1, NI):
                step(dve.tensor_tensor(ss[:, i, :], ss[:, i - 1, :], mm[:, i - 1, :], ALU.add))
            dve.tensor_tensor(s_all, ss[:, TILES, :], mm[:, TILES, :], ALU.add).then_inc(member_ready, 1)
            dve.wait_ge(rank_done, 1)
            step(dve.tensor_scalar(nb, banks[5][:, 0:EXPERTS], float(P - 1), None, ALU.add))
            step(dve.tensor_copy(nb_i, nb))
            step(dve.tensor_single_scalar(nb_i, nb_i, 7, ALU.arith_shift_right))
            step(dve.tensor_copy(nb, nb_i))
            step(dve.tensor_tensor_scan(bend, one32, nb, 0.0, ALU.mult, ALU.add))
            step(dve.tensor_tensor(bst, bend, nb, ALU.subtract))
            step(dve.tensor_scalar(bst, bst, float(P), None, ALU.mult))
            step(dve.tensor_tensor(rr, bank6[:, 0:NI * EXPERTS].rearrange("p (i e) -> p i e", i=NI),
                                   widen(bst, 1, NI), ALU.add))
            for a, e in enumerate((e1, e2)):
                step(dve.tensor_tensor(e, e, rr, ALU.mult))
                step(dve.tensor_reduce(dest_f[:, a * NI:(a + 1) * NI], e, AX.X, ALU.add))
            step(dve.tensor_copy(dest_i, dest_f))
            step(dve.tensor_single_scalar(lo_i, dest_i, P - 1, ALU.bitwise_and))
            step(dve.tensor_single_scalar(hi_i, dest_i, 7, ALU.arith_shift_right))
            step(dve.tensor_copy(lo_f, lo_i))
            step(dve.tensor_copy(hi_f, hi_i))
            step(dve.tensor_tensor(oh_lo, widen(iota_r, 1, 2 * NI), widen(lo_f, 2, P), ALU.is_equal))
            step(dve.tensor_tensor(oh_hi, widen(iota_r[:, 0:NBX], 1, 2 * NI), widen(hi_f, 2, NBX), ALU.is_equal))
            step(dve.tensor_tensor(tok_id, tok_id, valid, ALU.mult))
            step(dve.tensor_tensor(oh_hi[:, 0:NI, :], oh_hi[:, 0:NI, :], widen(tok_id, 2, NBX), ALU.mult))
            dve.tensor_tensor(oh_hi[:, NI:2 * NI, :], oh_hi[:, NI:2 * NI, :], widen(tok_id, 2, NBX),
                              ALU.mult).then_inc(onehot_ready, 1)
            step(dve.tensor_tensor(cmp, widen(bend[0:1, :], 1, NBX), widen(iota_r[0:1, 0:NBX], 2, EXPERTS),
                                   ALU.is_le))
            step(dve.tensor_reduce(ef, cmp, AX.X, ALU.add))
            step(dve.tensor_scalar(ef, ef, float(EXPERTS - 1), None, ALU.min))
            step(dve.tensor_copy(plan[:, 0:NBX], ef))
            step(dve.tensor_scalar(ef[:, 0:1], bend[0:1, EXPERTS - 1:EXPERTS], 1.0, None, ALU.add))
            step(dve.tensor_copy(plan[:, NBX:NBX + 1], ef[:, 0:1]))
            step(dve.tensor_single_scalar(plan[:, NBX:NBX + 1], plan[:, NBX:NBX + 1], 1, ALU.arith_shift_right))
            dve.wait_ge(slots_done, 1)
            dve.tensor_copy(tok_of, banks[4][:, 0:NBX]).then_inc(routed, 1)
            dve.wait_ge(routed, 1)

            pairs = dve.value_load(plan[:, NBX:NBX + 1], min_val=1, max_val=BLOCKS // 2)
            dve.memset(yo[0][:, 0:1], 0.0).then_inc(o_free, 1)
            with dve.Fori(0, pairs) as i:
                st.enter(i, 2)
                for b in range(2):
                    n = i * 2 + (b + 1)
                    dve.tensor_copy(idx2[:, b:b + 1], tok_of[:, ds(i * 2 + (b + 2), 1)]).then_inc(idx_ready, 1)
                    dve.wait_ge(up_done, i * 2 + (b + 3))
                    dve.wait_ge(sig_ready, n)
                    dve.tensor_tensor(hm[b], hm[b], banks[1][:, :], ALU.mult).then_inc(h_ready, 1)
                    dve.wait_ge(ht_turned, n)
                    dve.tensor_copy(ht[b], bank6).then_inc(ht_copied, 1)
                    dve.wait_ge(o_done, i * 2 + (b + 3))
                    st.did(dve.tensor_copy(yo[b][:, 0:512], banks[2][:, :]))
                    dve.tensor_copy(yo[b][:, 512:1024], banks[3][:, :]).then_inc(o_free, 1)
                dve.wait_ge(rows_stored[0], i * 16 + 16)
                dve.wait_ge(rows_stored[1], i * 16 + 16)
            dve.wait_ge(finw_landed, 64)
            dve.wait_ge(routed, 1)
            fin = Steps(dve, fin_step)
            for row in (g2_p, g2_s):
                fin.did(dve.tensor_scalar(row, row, 1.0, None, ALU.add))
            for i in range(TILES + 1):
                rows = P if i < TILES else NS
                g2 = g2_p if i < TILES else g2_s
                x = fa[i % 3][0:rows, :]
                dve.wait_ge(fin_landed[i % 3], 32 * (i // 3 + 1))
                dve.wait_ge(f_scaled, i + 1)
                fin.did(dve.scalar_tensor_tensor(x, fb[i % 3][0:rows, :], wts[0:rows, NI + i:NI + i + 1], x,
                                                 ALU.mult, ALU.add))
                fin.settle()
                fin.did(dve.tensor_tensor(x, x, g2, ALU.mult))
                fin.settle()
                fin.did(dve.scalar_tensor_tensor(x, x1[0:rows, i, :], ALPHA, x, ALU.mult, ALU.add))
                fin.settle()
                for half in range(2):
                    fin.did(dve.bn_stats(stats2[0:rows, 6 * half:6 * half + 6], x[:, 512 * half:512 * half + 512]))
                fin.settle()
                dve.bn_aggr(mv2[0:rows, i % 2, 0:2], stats2[0:rows, :]).then_inc(fvar_ready, 1)
                dve.wait_ge(fvar_ready, i + 1)
                fin.did(dve.scalar_tensor_tensor(x, x, mv2[0:rows, i % 2, 0:1], ffn_g[0:rows, :], ALU.subtract,
                                                 ALU.mult))
                dve.wait_ge(fstd_ready, i + 1)
                fin.did(dve.reciprocal(mv2[0:rows, i % 2, 3:4], mv2[0:rows, i % 2, 2:3]))
                fin.settle()
                dve.scalar_tensor_tensor(x, x, mv2[0:rows, i % 2, 3:4], ffn_b[0:rows, :], ALU.mult,
                                         ALU.add).then_inc(y_out, 1)

        @block.tensor
        def _(pe):
            pe.wait_ge(consts_ready, 1)
            pe.wait_ge(c_landed, 32)
            for k in range(KD):
                last = pe.transpose(bank6[:, k * MROWS:(k + 1) * MROWS], crow[:, k * P:(k + 1) * P],
                                    ident[0:MROWS, 0:MROWS])
            last.then_inc(ct_turned, 1)
            pe.wait_ge(ct_ready, 1)

            def mod_group(q):
                pe.wait_ge(wada_landed[q % 3], 16 * (q // 3 + 1))
                if q >= 2:
                    pe.wait_ge(mod_added, q - 1)
                for k in range(KD):
                    last = pe.matmul(banks[q % 2][0:MROWS, :], c_t[:, k, :], wada[q % 3][:, k, :],
                                     start=(k == 0), stop=(k == KD - 1))
                last.then_inc(mod_done, 1)

            def turn_x(i):
                rows = P if i < TILES else NS
                pe.wait_ge(x0_ready, i + 1)
                if i >= 2:
                    pe.wait_ge(ut_ready, i - 1)
                for k in range(KD):
                    last = pe.transpose(banks[2 + 2 * (i % 2) + k // 4][:, (k % 4) * P:(k % 4) * P + rows],
                                        xr[i % 4][0:rows, k * P:(k + 1) * P], ident[0:rows, 0:rows])
                last.then_inc(x_turned, 1)

            for q in range(4):
                mod_group(q)
            pe.wait_ge(mod_added, 4)
            for k in range(16):
                last = pe.transpose(bank6[:, k * MROWS:(k + 1) * MROWS], mod[:, k * P:(k + 1) * P],
                                    ident[0:MROWS, 0:MROWS])
            last.then_inc(cols_turned, 1)
            pe.wait_ge(small_landed, 13 * 16)
            pe.wait_ge(cols_copied, 1)
            for k in range(KD):
                last = pe.transpose(bank6[:, k * ROWS_C:(k + 1) * ROWS_C], rows_c[:, k * P:(k + 1) * P],
                                    ident[0:ROWS_C, 0:ROWS_C])
            last.then_inc(cols_turned, 1)
            for half in range(2):
                pe.wait_ge(cols_copied, 2 + half)
                for k in range(16):
                    kk = 16 * half + k
                    last = pe.transpose(bank6[:, k * ROWS_S:(k + 1) * ROWS_S], rows_s[:, kk * P:(kk + 1) * P],
                                        ident[0:ROWS_S, 0:ROWS_S])
                last.then_inc(cols_turned, 1)
            for i in range(TILES):
                turn_x(i)
                mod_group(4 + i)
            turn_x(TILES)

            pe.wait_ge(ut_ready, TILES)
            pe.wait_ge(ut_s_ready, 1)
            for i in range(TILES + 1):
                rows = P if i < TILES else NS
                for k in range(KD):
                    last = pe.matmul(bank7[0:rows, i * HEADS:(i + 1) * HEADS], uT[:, k, i * P:i * P + rows],
                                     w_dt[:, k, :], start=(k == 0), stop=(k == KD - 1))
            last.then_inc(dt_raw, 1)
            def turn(g, proj, ssd, steps=range(18)):
                gp = g - 1 if ssd else None

                def sub(s):
                    u, part = s // 3, s % 3
                    if part == 0:
                        pe.wait_ge(w_landed[u], g * 16 + 16)
                    if ssd or s >= 3:
                        pe.wait_ge(raw_ready, g * 18 + (s - 2))
                    for k in range(KD):
                        last = pe.matmul(banks[part][:, 0:SUB], wslot[u][:, k, :],
                                         uT[:, k, part * SUB:(part + 1) * SUB], start=(k == 0), stop=(k == KD - 1))
                    last.then_inc(proj_done, 1)

                def tails():
                    pe.wait_ge(raw_ready, gp * 18 + 18)
                    for u in range(4):
                        last = pe.transpose(bank6[0:11, u * P:(u + 1) * P], raw[u][:, SEQ - 3:TOK], ident)
                    last.then_inc(tails_done, 1)

                def scores(c):
                    at = slice(c * P, (c + 1) * P)
                    if c == 0:
                        pe.wait_ge(silu_done, gp * 4 + 4)
                    pe.transpose(banks[3][:, 0:128], proc[0][:, at], ident)
                    pe.transpose(banks[3][:, 128:256], proc[1][:, at], ident)
                    pe.transpose(banks[3][:, 256:384], proc[2][:, at], ident)
                    pe.matmul(banks[3][:, 384:512], proc[2][:, at], proc[3][:, at], start=True,
                              stop=True).then_inc(scores_ready, 1)

                def outputs(c):
                    pe.wait_ge(ops_ready, gp * 8 + (c + 1))
                    pe.matmul(banks[5][:, 256:512], b_tok, xw, start=True, stop=True)
                    for r in range(HPG):
                        out = banks[5][HD * (r % 2):HD * (r % 2) + HD, (r // 2) * P:(r // 2 + 1) * P]
                        last = pe.matmul(out, xdt[:, r * HD:(r + 1) * HD], segm[:, r * P:(r + 1) * P], start=True,
                                         stop=(c == 0))
                        if c:
                            last = pe.matmul(out, h_t[:, r * HD:(r + 1) * HD], csc[:, r * P:(r + 1) * P],
                                             start=False, stop=True)
                    last.then_inc(y_ready, 1)

                def rms(c):
                    w = P if c < 8 else NS
                    if c == 0:
                        pe.wait_ge(sc_used, gp + 1)
                    pe.wait_ge(sq_ready, gp * 9 + (c + 1))
                    for j in range(2):
                        last = pe.matmul(bank7[:, 0:w], ones_avg, sq[:, j, 0:w], start=(j == 0), stop=(j == 1))
                    last.then_inc(rms_ready, 1)

                def spread_rows(diag_ready, done):
                    pe.wait_ge(diag_ready, gp + 1)
                    for h in range(2):
                        last = pe.matmul(pair[:, 512 * h:512 * h + 512], ones, diag_f[:, 512 * h:512 * h + 512],
                                         start=True, stop=True)
                    last.then_inc(done, 1)

                for s in steps:
                    if proj:
                        sub(s)
                    if not proj:
                        first_product(range(DONE_K * s // 18 * 3, DONE_K * (s + 1) // 18 * 3))
                    if not ssd:
                        continue
                    if s == 0:
                        tails()
                    if s == 3:
                        scores(0)
                    if s == 4:
                        pe.wait_ge(tail_copied, gp + 1)
                        spread_rows(diag_b_ready, sb_ready)
                    if s == 5:
                        pe.wait_ge(sb_used, gp + 1)
                        spread_rows(diag_c_ready, sc_ready)
                    if 6 <= s <= LAST_S2:
                        c = s - 6
                        outputs(c)
                        if c < 7:
                            scores(c + 1)
                        if c:
                            rms(c - 1)
                    if s == 14:
                        rms(7)
                        for j in range(2):
                            last = pe.transpose(bank6[:, j * P:(j + 1) * P], h_t[:, j * P:(j + 1) * P], ident)
                        last.then_inc(ht_ready, 1)
                    if s == 15:
                        rms(8)
                if ssd:
                    pe.wait_ge(pstate_copied, gp + 1)
                    pe.wait_ge(rs_ready, gp * 9 + 9)

            DONE_K = 2 * (GROUPS - 1)

            def first_product(steps):
                for x in steps:
                    part, k = x // DONE_K, x % DONE_K
                    if x == 0:
                        pe.wait_ge(raw_ready, 144)
                    if k in (0, KD):
                        pe.wait_ge(w_landed[1 + k // KD], 144)
                    pe.matmul(banks[part][:, 0:SUB], wslot[1 + k // KD][:, k % KD, :],
                              ybT[:, k, part * SUB:(part + 1) * SUB], start=(k == 0), stop=False)

            def step_sizes():
                turn(0, True, False, range(0, 3))
                pe.wait_ge(dta_ready, 1)
                for x in range(2):
                    pe.matmul(bank6[:, x * P:(x + 1) * P], dta_g[:, x * P:(x + 1) * P], tri, start=True, stop=True)
                pe.matmul(bank7[:, 0:256], tri, dta_g, start=True, stop=True)
                pe.matmul(bank7[:, 256:512], ones, dta_g, start=True, stop=True).then_inc(cum_done, 1)
                turn(0, True, False, range(3, 6))
                pe.wait_ge(spread_ready, 1)
                pe.matmul(bank7, ones[0:NS, :], spread, start=True, stop=True).then_inc(spread_done, 1)
                turn(0, True, False, range(6, 18))

            step_sizes()
            with pe.Fori(0, GROUPS - 1) as i:
                turn(i + 1, True, True)
            turn(GROUPS, False, True)
            pe.wait_ge(normed, 72)
            pe.wait_ge(raw_ready, 144)

            def projection(out, v, part):
                at = slice(part * SUB, (part + 1) * SUB)
                for k in range(KD):
                    pe.matmul(out, w_hi[v][:, k, :], u_hi[:, k, at], start=(k == 0), stop=False)
                    pe.matmul(out, w_hi[v][:, k, :], u_lo[:, k, at], start=False, stop=False)
                    last = pe.matmul(out, w_lo[v][:, k, :], u_hi[:, k, at], start=False, stop=(k == KD - 1))
                return last

            def first_tile():
                for part in range(3):
                    for k in range(DONE_K, 2 * KD):
                        last = pe.matmul(banks[part][:, 0:SUB], wslot[1 + k // KD][:, k % KD, :],
                                         ybT[:, k, part * SUB:(part + 1) * SUB], start=False, stop=(k == 2 * KD - 1))
                    last.then_inc(yb_done, 1)
                pe.wait_ge(u_lo_ready, KD // 2)
                pe.wait_ge(split_ready, 1)
                for part in range(3):
                    projection(banks[3 + part][:, 0:SUB], 0, part).then_inc(gb_done, 1)

            def merge(i, first, split_before, out_slots, src, gate_sem, gate_free, out_sem, out_free):
                swapped = first and src is ybT
                if swapped:
                    first_tile()
                    gate_free, out_free = out_free, gate_free
                for h in range(1 if swapped else 0, 2):
                    pe.wait_ge(split_ready, i * 2 + (split_before + h + 1))
                    for part in range(3):
                        n = 3 * h + part
                        if not (first and h == 0):
                            pe.wait_ge(gate_free, i * 6 + (n - 2))
                        projection(banks[part][:, 0:SUB], 0, part).then_inc(gate_sem, 1)
                    ks = KD * len(out_slots[h])
                    for slot, before in out_slots[h]:
                        pe.wait_ge(w_landed[slot], i * 16 + (before + 16))
                    for part in range(3):
                        n = 3 * h + part
                        if not (first and h == 0):
                            pe.wait_ge(out_free, i * 6 + (n - 2))
                        for k in range(ks):
                            last = pe.matmul(banks[3 + part][:, 0:SUB], wslot[out_slots[h][k // KD][0]][:, k % KD, :],
                                             src[:, k, part * SUB:(part + 1) * SUB], start=(k == 0),
                                             stop=(k == ks - 1))
                        last.then_inc(out_sem, 1)

            args_b = (0, (((1, 128), (2, 128)), ((5, 128), (6, 0))), ybT, gb_done, gsig_ready, yb_done, merged_b)
            merge(0, True, *args_b)
            with pe.Fori(0, 3) as i:
                merge(i + 1, False, *args_b)
            pe.wait_ge(merged_b, 24)

            def short(i, first):
                for h in range(2):
                    for x in range(3):
                        v = 3 * h + x
                        pe.wait_ge(split_ready, i * 6 + (8 + v + 1))
                        for part in range(3):
                            n = 3 * h + part + 1
                            if x == 2:
                                pe.wait_ge(sc_copied, i * 6 + n)
                            elif not (first and h == 0):
                                pe.wait_ge(p_made if x == 0 else sb_copied, i * 6 + (n - 3))
                            projection(banks[3 * (v % 2) + part][:, 0:SUB], v % 2, part).then_inc(short_done, 1)
                    pe.wait_ge(p_made, i * 6 + (3 * h + 3))
                    if not (first and h == 0):
                        pe.wait_ge(tail2_copied, i * 2 + h)
                    pe.transpose(bank6[0:10, h * P:(h + 1) * P], pt[h][:, SEQ - 2:TOK], ident).then_inc(tail2_done, 1)

            short(0, True)
            with pe.Fori(0, 3) as i:
                short(i + 1, False)
            pe.wait_ge(ya_ready, 8)
            args_a = (32, (((1, 320),), ((2, 320),)), yaT, ga_done, gsig2_ready, ya_done, merged_a)
            pe.wait_ge(sb_copied, 24)
            merge(0, True, *args_a)
            with pe.Fori(0, 3) as i:
                merge(i + 1, False, *args_a)

            pe.wait_ge(merged_a, 24)
            pe.wait_ge(wo_landed, 16)

            def turn_u2(i):
                rows = P if i < TILES else NS
                pe.wait_ge(u2_ready, i + 1)
                if i:
                    pe.wait_ge(u2t_ready, i)
                for k in range(KD):
                    last = pe.transpose(banks[4 + k // 4][:, (k % 4) * P:(k % 4) * P + rows],
                                        u2[i % 2][0:rows, k * P:(k + 1) * P], ident[0:rows, 0:rows])
                last.then_inc(u2_turned, 1)

            def logits(i):
                rows = P if i < TILES else NS
                pe.wait_ge(u2t_ready, i + 1)
                if i == 0:
                    pe.wait_ge(mixw_landed, 12 * 16)
                for k in range(KD):
                    last = pe.matmul(bank7[0:rows, i * 36:(i + 1) * 36], u2t[i % 2][:, k * P:k * P + rows],
                                     w_r[:, k, :], start=(k == 0), stop=(k == KD - 1))
                if i == TILES:
                    last.then_inc(logits_done, 1)

            for i in range(TILES + 1):
                rows = P if i < TILES else NS
                if i >= 2:
                    pe.wait_ge(x0_used, i - 1)
                for half in range(2):
                    for k in range(KD):
                        last = pe.matmul(banks[2 * (i % 2) + half][0:rows, :], merged[:, k, i * P:i * P + rows],
                                         w_o[:, k, 512 * half:512 * half + 512], start=(k == 0), stop=(k == KD - 1))
                last.then_inc(wo_done, 1)
                if i >= 2:
                    logits(i - 2)
                if i >= 1:
                    turn_u2(i - 1)
            logits(TILES - 1)
            turn_u2(TILES)
            logits(TILES)

            pe.wait_ge(member_ready, 1)
            flat = dict(i=NI)
            pe.matmul(bank6[:, 0:NI * EXPERTS], stri, mm.rearrange("p i e -> p (i e)", **flat), start=True, stop=False)
            pe.matmul(bank6[:, 0:NI * EXPERTS], ones, ss.rearrange("p i e -> p (i e)", **flat), start=False, stop=True)
            pe.matmul(banks[5][:, 0:EXPERTS], ones, s_all, start=True, stop=True).then_inc(rank_done, 1)
            pe.wait_ge(onehot_ready, 1)
            primes = {0: up_done, 1: up_done, 2: o_done, 3: o_done, 2 * NI - 1: slots_done}
            for a in range(2 * NI):
                last = pe.matmul(banks[4][:, 0:NBX], oh_lo[:, a, :], oh_hi[:, a, :], start=(a == 0),
                                 stop=(a == 2 * NI - 1))
                if a in primes:
                    last.then_inc(primes[a], 1)

            def turn_rows(b, landed):
                pe.wait_ge(xg_landed[b], landed)
                for k in range(KD):
                    last = pe.transpose(banks[4 + k // 4][:, (k % 4) * P:(k % 4 + 1) * P], xg[b][:, k * P:(k + 1) * P],
                                        ident)
                last.then_inc(xg_turned, 1)

            pe.wait_ge(routed, 1)
            pairs = pe.value_load(plan[:, NBX:NBX + 1], min_val=1, max_val=BLOCKS // 2)
            turn_rows(0, 16)
            with pe.Fori(0, pairs) as i:
                for b in range(2):
                    n = i * 2 + (b + 1)
                    pe.wait_ge(xt_ready, n)
                    pe.wait_ge(w13_landed[b], i * 16 + 16)
                    for half, done in ((0, gate_done), (1, up_done)):
                        for k in range(KD):
                            last = pe.matmul(banks[half][:, :], xt[b][:, k * P:(k + 1) * P],
                                             w13[b][:, k, D_EXP * half:D_EXP * half + D_EXP], start=(k == 0),
                                             stop=(k == KD - 1))
                        last.then_inc(done, 1)
                    turn_rows(1 - b, i * 16 + (16 if b == 0 else 32))
                    pe.wait_ge(h_ready, n)
                    for k in range(4):
                        last = pe.transpose(bank6[:, k * P:(k + 1) * P], hm[b][:, k * P:(k + 1) * P], ident)
                    last.then_inc(ht_turned, 1)
                    pe.wait_ge(ht_copied, n)
                    pe.wait_ge(w2_landed[b], i * 16 + 16)
                    pe.wait_ge(o_free, n)
                    for half in range(2):
                        for k in range(4):
                            last = pe.matmul(banks[2 + half][:, :], ht[b][:, k * P:(k + 1) * P],
                                             w2[b][:, k, 512 * half:512 * half + 512], start=(k == 0), stop=(k == 3))
                    last.then_inc(o_done, 1)


_INS = ["x_prompt", "x_sample", "state_ssm", "state_ssm_conv", "state_sc_conv", "c_prompt", "c_sample", "ln_in_g",
        "ln_in_b", "w_ada", "b_ada", "w_in", "conv_sc_w", "w_sc_out", "conv_ssm_w", "conv_ssm_b", "dt_bias", "a_log",
        "d_skip", "ssm_norm_g", "w_ssm_out", "w_o", "ln_mix_g", "ln_mix_b", "w_route_g", "b_route_g", "w_route_e",
        "b_route_e", "w_moe_13", "w_moe_2", "ln_ffn_g", "ln_ffn_b"]
_OUTS = [(1, SEQ, D), (NS, 1, D), (1, 1, HEADS, HD, N), (1, 1, 3, CONV_DIM), (1, 1, 2, D), (1, NS, HEADS, HD, N),
         (1, NS, 3, CONV_DIM), (1, NS, 2, D)]


def kernel(**inputs):
    import numpy as _np
    import concourse.bacc as _bacc
    from concourse.bass_utils import run_bass_kernel_spmd as _run

    nc = _bacc.Bacc("TRN2", target_bir_lowering=False, num_devices=1)
    arrays, args, outs = {}, {}, []
    for name in _INS:
        a = _np.ascontiguousarray(inputs[name])
        arrays[f"in_{name}_dram"] = a
        args[name] = nc.dram_tensor(f"in_{name}_dram", a.shape, mybir.dt.from_np(a.dtype), kind="ExternalInput").ap()
    for i, shape in enumerate(_OUTS):
        outs.append(nc.dram_tensor(f"out_{i}_dram", shape, F32, kind="ExternalOutput").ap())
    build(nc, args, outs)
    r = _run(nc, [arrays], core_ids=[0])
    return tuple(r.results[0][f"out_{i}_dram"] for i in range(len(_OUTS)))
```
